# Optimizing a Trainium2 kernel written in Bass

```python
import math
import jax, jax.numpy as jnp
from jax import lax
import numpy as np

D_MODEL = 1024
BATCH = 1
SEQ = 512
DEPTH = 2

A_HEADS = 4
A_HEAD_DIM = 64
A_WIDTH = A_HEADS * 2 * A_HEAD_DIM
Q_BLOCK = 128
B_WIDTH = 512
B_GROUPS = 4
B_GROUP_DIM = B_WIDTH // B_GROUPS
B_CHUNK = 128
C_HEADS = 8
C_HEAD_DIM = 64
C_WIDTH = C_HEADS * C_HEAD_DIM
C_PATTERNS = ((128, 1), (512, 4), (2048, 16))
C_BLOCK = 128
N_BRANCH = 3
BRANCH_WIDTH = 512
IN_COLS = 4 * A_WIDTH + 3 * B_WIDTH + 4 * C_WIDTH + N_BRANCH * D_MODEL
ROPE_THETA = 500000.0
ROPE_FRAC = 4
EPS = 1e-6


def rmsnorm(t, g):
    tf = t.astype(jnp.float32)
    y = tf * lax.rsqrt(jnp.mean(tf * tf, axis=-1, keepdims=True) + EPS)
    return (y * g.astype(jnp.float32)).astype(t.dtype)

def layernorm(t, g, b):
    tf = t.astype(jnp.float32)
    mu = jnp.mean(tf, axis=-1, keepdims=True)
    var = jnp.mean(jnp.square(tf - mu), axis=-1, keepdims=True)
    y = (tf - mu) * lax.rsqrt(var + EPS)
    return (y * g.astype(jnp.float32) + b.astype(jnp.float32)).astype(t.dtype)

def partial_rope(t, positions):
    dh = t.shape[-1]
    rot = dh // ROPE_FRAC
    half = rot // 2
    inv = jnp.power(jnp.float32(ROPE_THETA), -jnp.arange(half, dtype=jnp.float32) * 2.0 / rot)
    ang = positions.astype(jnp.float32)[:, :, None] * inv
    cos = jnp.cos(ang)[:, :, None, :]
    sin = jnp.sin(ang)[:, :, None, :]
    tf = t.astype(jnp.float32)
    x1 = tf[..., :half]
    x2 = tf[..., half:rot]
    out = jnp.concatenate([x1 * cos - x2 * sin, x2 * cos + x1 * sin, tf[..., rot:]], axis=-1)
    return out.astype(t.dtype)

def split_cols(proj):
    sizes = [A_WIDTH, A_WIDTH, A_WIDTH, A_WIDTH,
             2 * B_WIDTH, B_WIDTH,
             C_WIDTH, C_WIDTH, C_WIDTH, C_WIDTH,
             N_BRANCH * D_MODEL]
    idx = np.cumsum(sizes)[:-1].tolist()
    return jnp.split(proj, idx, axis=-1)

def diff_attention(q, k, v, lam):
    B, S, H, _, d = q.shape
    nb = S // Q_BLOCK
    scale = 1.0 / math.sqrt(d)
    qb = q.reshape(B, nb, Q_BLOCK, H, 2, d).transpose(1, 0, 2, 3, 4, 5)
    kpos = jnp.arange(S)

    def block(args):
        i, qblk = args
        s = jnp.einsum('bqhmd,bkhmd->bhmqk', qblk, k,
                       preferred_element_type=jnp.float32) * scale
        qpos = i * Q_BLOCK + jnp.arange(Q_BLOCK)
        mask = kpos[None, :] <= qpos[:, None]
        s = jnp.where(mask, s, -jnp.inf)
        p = jax.nn.softmax(s, axis=-1)
        pd = p[:, :, 0] - lam * p[:, :, 1]
        return jnp.einsum('bhqk,bkhe->bqhe', pd.astype(v.dtype), v)

    out = lax.map(block, (jnp.arange(nb), qb))
    return out.transpose(1, 0, 2, 3, 4).reshape(B, S, H, 2 * d)

def dilated_window_attention(q, k, v, window, dil):
    B, S, H, dh = q.shape
    L = S // dil
    n_back = window // dil
    nb = -(-L // C_BLOCK)
    Lp = nb * C_BLOCK
    BD = B * dil
    scale = 1.0 / math.sqrt(dh)

    def to_sub(t):
        t = t.reshape(B, L, dil, H, dh).transpose(0, 2, 1, 3, 4).reshape(BD, L, H, dh)
        return jnp.pad(t, ((0, 0), (0, Lp - L), (0, 0), (0, 0)))

    def windows(t):
        t = jnp.pad(t, ((0, 0), (C_BLOCK, 0), (0, 0), (0, 0))).reshape(BD, nb + 1, C_BLOCK, H, dh)
        return jnp.concatenate([t[:, :-1], t[:, 1:]], axis=2)

    qb = to_sub(q).reshape(BD, nb, C_BLOCK, H, dh)
    kw = windows(to_sub(k))
    vw = windows(to_sub(v))
    s = jnp.einsum('bnqhd,bnkhd->bnhqk', qb, kw,
                   preferred_element_type=jnp.float32) * scale
    qi = jnp.arange(nb)[:, None, None] * C_BLOCK + jnp.arange(C_BLOCK)[None, :, None]
    ki = jnp.arange(nb)[:, None, None] * C_BLOCK - C_BLOCK + jnp.arange(2 * C_BLOCK)[None, None, :]
    rel = qi - ki
    mask = (rel >= 0) & (rel <= n_back) & (ki >= 0)
    s = jnp.where(mask[None, :, None], s, -jnp.inf)
    m = jnp.max(s, axis=-1, keepdims=True)
    e = jnp.exp(s - m)
    den = jnp.sum(e, axis=-1)
    o = jnp.einsum('bnhqk,bnkhd->bnqhd', e, vw.astype(jnp.float32))
    den_q = den.transpose(0, 1, 3, 2)
    o = o / den_q[..., None]
    lse = m[..., 0].transpose(0, 1, 3, 2) + jnp.log(den_q)

    def from_sub(t):
        rest = t.shape[3:]
        t = t.reshape((B, dil, Lp) + rest)[:, :, :L]
        t = jnp.moveaxis(t, 1, 2)
        return t.reshape((B, S) + rest)

    return from_sub(o), from_sub(lse)

def hybrid_layer(x, positions, layer_idx, norm_g, w_in, lam_q1, lam_k1, lam_q2, lam_k2,
                 subln_g, sgu_ln_g, sgu_ln_b, sgu_w, sgu_b, w_branch, w_out):
    B, S, D = x.shape
    h = rmsnorm(x, norm_g)
    proj = jnp.einsum('bsd,dc->bsc', h, w_in)
    aq, ak, av, az, buv, bz, cq, ck, cv, cz, gl = split_cols(proj)

    lam_init = 0.8 - 0.6 * math.exp(-0.3 * layer_idx)
    lam = (jnp.exp(jnp.sum(lam_q1.astype(jnp.float32) * lam_k1.astype(jnp.float32)))
           - jnp.exp(jnp.sum(lam_q2.astype(jnp.float32) * lam_k2.astype(jnp.float32)))
           + lam_init)
    qa = partial_rope(aq.reshape(B, S, 2 * A_HEADS, A_HEAD_DIM), positions).reshape(B, S, A_HEADS, 2, A_HEAD_DIM)
    ka = partial_rope(ak.reshape(B, S, 2 * A_HEADS, A_HEAD_DIM), positions).reshape(B, S, A_HEADS, 2, A_HEAD_DIM)
    va = av.reshape(B, S, A_HEADS, 2 * A_HEAD_DIM)
    oa = diff_attention(qa, ka, va, lam)
    oa = rmsnorm(oa, subln_g) * (1.0 - lam_init)
    ya = oa.reshape(B, S, A_WIDTH) * jax.nn.silu(az)

    uv = jax.nn.gelu(buv)
    u, vb = uv[..., :B_WIDTH], uv[..., B_WIDTH:]
    vb = layernorm(vb, sgu_ln_g, sgu_ln_b).reshape(B, S // B_CHUNK, B_CHUNK, B_GROUPS, B_GROUP_DIM)
    w_causal = sgu_w * jnp.tril(jnp.ones((B_CHUNK, B_CHUNK), dtype=sgu_w.dtype))
    mixed = jnp.einsum('gts,bnsgc->bntgc', w_causal, vb) + sgu_b.T[None, None, :, :, None]
    yb = u * mixed.reshape(B, S, B_WIDTH) * jax.nn.silu(bz)

    qc = partial_rope(cq.reshape(B, S, C_HEADS, C_HEAD_DIM), positions)
    kc = partial_rope(ck.reshape(B, S, C_HEADS, C_HEAD_DIM), positions)
    vc = cv.reshape(B, S, C_HEADS, C_HEAD_DIM)
    outs = []
    lses = []
    for window, dil in C_PATTERNS:
        o_p, lse_p = dilated_window_attention(qc, kc, vc, window, dil)
        outs.append(o_p)
        lses.append(lse_p)
    wts = jax.nn.softmax(jnp.stack(lses, axis=0), axis=0)
    oc = jnp.sum(wts[..., None] * jnp.stack(outs, axis=0), axis=0).astype(x.dtype)
    yc = oc.reshape(B, S, C_WIDTH) * jax.nn.silu(cz)

    ys = jnp.stack([ya, yb, yc], axis=0)
    pb = jnp.einsum('nbsc,ncd->nbsd', ys, w_branch)
    gates = jax.nn.sigmoid(gl.reshape(B, S, N_BRANCH, D))
    merged = jnp.einsum('bsnd,nbsd->bsd', gates, pb)
    return x + jnp.einsum('bsd,de->bse', merged, w_out)

def first_inputs(seed: int = 0) -> dict:
    key = jax.random.key(seed)
    ks = jax.random.split(key, 16)
    f32 = jnp.float32
    x = jax.random.normal(ks[0], (BATCH, SEQ, D_MODEL), f32)
    positions = jnp.broadcast_to(jnp.arange(SEQ, dtype=jnp.int32)[None, :], (BATCH, SEQ))
    norm_g = 1.0 + 0.05 * jax.random.normal(ks[1], (DEPTH, D_MODEL), f32)
    w_in = jax.random.normal(ks[2], (DEPTH, D_MODEL, IN_COLS), f32) * D_MODEL ** -0.5
    lam_q1 = 0.1 * jax.random.normal(ks[3], (DEPTH, A_HEAD_DIM), f32)
    lam_k1 = 0.1 * jax.random.normal(ks[4], (DEPTH, A_HEAD_DIM), f32)
    lam_q2 = 0.1 * jax.random.normal(ks[5], (DEPTH, A_HEAD_DIM), f32)
    lam_k2 = 0.1 * jax.random.normal(ks[6], (DEPTH, A_HEAD_DIM), f32)
    subln_g = 1.0 + 0.05 * jax.random.normal(ks[7], (DEPTH, 2 * A_HEAD_DIM), f32)
    sgu_ln_g = 1.0 + 0.05 * jax.random.normal(ks[8], (DEPTH, B_WIDTH), f32)
    sgu_ln_b = 0.02 * jax.random.normal(ks[9], (DEPTH, B_WIDTH), f32)
    sgu_w = jax.random.normal(ks[10], (DEPTH, B_GROUPS, B_CHUNK, B_CHUNK), f32) * B_CHUNK ** -0.5
    sgu_b = 1.0 + 0.1 * jax.random.normal(ks[11], (DEPTH, B_GROUPS, B_CHUNK), f32)
    w_branch = jax.random.normal(ks[12], (DEPTH, N_BRANCH, BRANCH_WIDTH, D_MODEL), f32) * BRANCH_WIDTH ** -0.5
    w_out = jax.random.normal(ks[13], (DEPTH, D_MODEL, D_MODEL), f32) * (2.0 * D_MODEL) ** -0.5
    final_g = 1.0 + 0.05 * jax.random.normal(ks[14], (D_MODEL,), f32)
    return {'x': x, 'positions': positions, 'norm_g': norm_g, 'w_in': w_in,
            'lam_q1': lam_q1, 'lam_k1': lam_k1, 'lam_q2': lam_q2, 'lam_k2': lam_k2,
            'subln_g': subln_g, 'sgu_ln_g': sgu_ln_g, 'sgu_ln_b': sgu_ln_b,
            'sgu_w': sgu_w, 'sgu_b': sgu_b, 'w_branch': w_branch, 'w_out': w_out,
            'final_g': final_g}

def first_block(x, positions, norm_g, w_in, lam_q1, lam_k1, lam_q2, lam_k2, subln_g,
              sgu_ln_g, sgu_ln_b, sgu_w, sgu_b, w_branch, w_out, final_g):
    h = x
    for l in range(DEPTH):
        h = hybrid_layer(h, positions, l, norm_g[l], w_in[l], lam_q1[l], lam_k1[l],
                         lam_q2[l], lam_k2[l], subln_g[l], sgu_ln_g[l], sgu_ln_b[l],
                         sgu_w[l], sgu_b[l], w_branch[l], w_out[l])
    return rmsnorm(h, final_g)


HEAD_DIM = 64
GROUP_HEADS = 4
GROUP_WIDTH = GROUP_HEADS * HEAD_DIM
N_GROUPS = 4
MIX_WIDTH = N_GROUPS * GROUP_WIDTH
BLOCK = 128
NEG_INF = -1e30

FOX_H = GROUP_HEADS
FOX_BIAS_INIT = 3.0
MLA_H = GROUP_HEADS
MLA_Q_RANK = D_MODEL // 4
MLA_KV_RANK = D_MODEL // 8
MLA_NOPE = HEAD_DIM
MLA_ROPE = HEAD_DIM // 2
MLA_V = HEAD_DIM
ROPE_THETA_2 = 10000.0
SB_H = GROUP_HEADS
SWA_H = GROUP_HEADS
SWA_KV_H = 2
WINDOW = 128
D_FF = ((8 * D_MODEL + 767) // 768) * 256
ALPHA = (2.0 * DEPTH) ** 0.25
BETA = (8.0 * DEPTH) ** -0.25

SPLIT_SIZES = (
    FOX_H * HEAD_DIM, FOX_H * HEAD_DIM, FOX_H * HEAD_DIM, FOX_H,
    MLA_Q_RANK, MLA_KV_RANK, MLA_ROPE,
    SB_H * HEAD_DIM, SB_H * HEAD_DIM, SB_H * HEAD_DIM,
    SWA_H * HEAD_DIM, SWA_KV_H * HEAD_DIM, SWA_KV_H * HEAD_DIM,
)
IN_WIDTH = sum(SPLIT_SIZES)


def _layernorm(x, g, b, eps=1e-5):
    xf = x.astype(jnp.float32)
    mu = jnp.mean(xf, axis=-1, keepdims=True)
    var = jnp.mean(jnp.square(xf - mu), axis=-1, keepdims=True)
    return ((xf - mu) * lax.rsqrt(var + eps) * g + b).astype(x.dtype)

def _rmsnorm(x, g, eps=1e-6):
    xf = x.astype(jnp.float32)
    return (xf * lax.rsqrt(jnp.mean(jnp.square(xf), axis=-1, keepdims=True) + eps) * g).astype(x.dtype)

def _group_rmsnorm(mix, g, eps=1e-6):
    B, S, _ = mix.shape
    xf = mix.astype(jnp.float32).reshape(B, S, N_GROUPS, GROUP_WIDTH)
    xf = xf * lax.rsqrt(jnp.mean(jnp.square(xf), axis=-1, keepdims=True) + eps)
    return (xf.reshape(B, S, MIX_WIDTH) * g).astype(mix.dtype)

def _heads(t, n):
    B, S, _ = t.shape
    return t.reshape(B, S, n, -1)

def _rope_tables(S):
    pos = jnp.arange(S, dtype=jnp.float32)
    inv = ROPE_THETA_2 ** (-jnp.arange(0, MLA_ROPE, 2, dtype=jnp.float32) / MLA_ROPE)
    ang = pos[:, None] * inv[None, :]
    return jnp.cos(ang), jnp.sin(ang)

def _rope(x, cos, sin):
    x1, x2 = jnp.split(x.astype(jnp.float32), 2, axis=-1)
    c = cos[None, :, None, :]
    s = sin[None, :, None, :]
    return jnp.concatenate([x1 * c - x2 * s, x1 * s + x2 * c], axis=-1).astype(x.dtype)

def _alibi_slopes(n):
    return jnp.exp2(-8.0 * jnp.arange(1, n + 1, dtype=jnp.float32) / n)

def _causal_softmax_blocks(q, k, v, scale, cum_log_f=None):
    B, S, H, _ = q.shape
    nb = S // BLOCK
    qb = q.reshape(B, nb, BLOCK, H, -1).swapaxes(0, 1)
    kpos = jnp.arange(S)

    def one_block(args):
        i, qi = args
        s = jnp.einsum('bqhd,bkhd->bhqk', qi, k).astype(jnp.float32) * scale
        qpos = i * BLOCK + jnp.arange(BLOCK)
        if cum_log_f is not None:
            cq = lax.dynamic_slice_in_dim(cum_log_f, i * BLOCK, BLOCK, axis=2)
            s = s + cq[..., :, None] - cum_log_f[..., None, :]
        s = jnp.where(kpos[None, :] <= qpos[:, None], s, NEG_INF)
        p = jax.nn.softmax(s, axis=-1).astype(v.dtype)
        return jnp.einsum('bhqk,bkhd->bqhd', p, v)

    out = lax.map(one_block, (jnp.arange(nb), qb))
    return out.swapaxes(0, 1).reshape(B, S, H, -1)

def _stick_breaking_blocks(q, k, v):
    B, S, H, D = q.shape
    nb = S // BLOCK
    scale = D ** -0.5
    qb = q.reshape(B, nb, BLOCK, H, D).swapaxes(0, 1)
    kpos = jnp.arange(S)

    def one_block(args):
        i, qi = args
        z = jnp.einsum('bqhd,bkhd->bhqk', qi, k).astype(jnp.float32) * scale
        qpos = i * BLOCK + jnp.arange(BLOCK)
        strict = kpos[None, :] < qpos[:, None]
        log_1mb = jnp.where(strict, jax.nn.log_sigmoid(-z), 0.0)
        between = lax.cumsum(log_1mb, axis=3, reverse=True) - log_1mb
        a = jnp.where(strict, jnp.exp(jax.nn.log_sigmoid(z) + between), 0.0)
        return jnp.einsum('bhqk,bkhd->bqhd', a.astype(v.dtype), v)

    out = lax.map(one_block, (jnp.arange(nb), qb))
    return out.swapaxes(0, 1).reshape(B, S, H, D)

def _mla(cq, ckv, kr, g_q, g_kv, w_uq, w_ukv, cos, sin):
    B, S, _ = cq.shape
    q = (_rmsnorm(cq, g_q) @ w_uq).reshape(B, S, MLA_H, MLA_NOPE + MLA_ROPE)
    kv = (_rmsnorm(ckv, g_kv) @ w_ukv).reshape(B, S, MLA_H, MLA_NOPE + MLA_V)
    k_nope, v = kv[..., :MLA_NOPE], kv[..., MLA_NOPE:]
    q = jnp.concatenate([q[..., :MLA_NOPE], _rope(q[..., MLA_NOPE:], cos, sin)], axis=-1)
    k_rope = jnp.broadcast_to(_rope(kr[:, :, None, :], cos, sin), (B, S, MLA_H, MLA_ROPE))
    k = jnp.concatenate([k_nope, k_rope.astype(k_nope.dtype)], axis=-1)
    return _causal_softmax_blocks(q.astype(k.dtype), k, v, (MLA_NOPE + MLA_ROPE) ** -0.5)

def _swa_sink_alibi(q, k, v, sinks, slopes):
    B, S, Hq, D = q.shape
    Hkv = k.shape[2]
    G = Hq // Hkv
    nb = S // BLOCK
    qb = q.reshape(B, nb, BLOCK, Hkv, G, D)
    pad = jnp.zeros((B, BLOCK, Hkv, D), k.dtype)
    kp = jnp.concatenate([pad, k], axis=1).reshape(B, nb + 1, BLOCK, Hkv, D)
    vp = jnp.concatenate([pad.astype(v.dtype), v], axis=1).reshape(B, nb + 1, BLOCK, Hkv, D)
    kb = jnp.concatenate([kp[:, :-1], kp[:, 1:]], axis=2)
    vb = jnp.concatenate([vp[:, :-1], vp[:, 1:]], axis=2)
    s = jnp.einsum('bnqhgd,bnkhd->bnhgqk', qb, kb).astype(jnp.float32) * (D ** -0.5)
    dist = jnp.arange(BLOCK)[:, None] + BLOCK - jnp.arange(2 * BLOCK)[None, :]
    band = (dist >= 0) & (dist < WINDOW)
    kpos = (jnp.arange(nb)[:, None] - 1) * BLOCK + jnp.arange(2 * BLOCK)[None, :]
    valid = band[None, :, :] & (kpos >= 0)[:, None, :]
    s = s - slopes.reshape(Hkv, G)[:, :, None, None] * dist.astype(jnp.float32)
    s = jnp.where(valid[None, :, None, None], s, NEG_INF)
    sink = jnp.broadcast_to(sinks.astype(jnp.float32).reshape(Hkv, G)[None, None, :, :, None, None],
                            s.shape[:-1] + (1,))
    p = jax.nn.softmax(jnp.concatenate([s, sink], axis=-1), axis=-1)[..., :-1]
    out = jnp.einsum('bnhgqk,bnkhd->bnqhgd', p.astype(v.dtype), vb)
    return out.reshape(B, S, Hq, D)

def second_inputs(seed: int = 0) -> dict:
    key = jax.random.key(seed)
    ks = jax.random.split(key, 17)
    L = DEPTH

    def nrm(k, shape, scale):
        return jax.random.normal(k, shape, jnp.float32) * scale

    def gain(k, shape):
        return 1.0 + 0.02 * jax.random.normal(k, shape, jnp.float32)

    return {
        'x': nrm(ks[0], (BATCH, SEQ, D_MODEL), 1.0),
        'w_in': nrm(ks[1], (L, D_MODEL, IN_WIDTH), D_MODEL ** -0.5),
        'fox_b_f': FOX_BIAS_INIT + nrm(ks[2], (L, FOX_H), 0.1),
        'mla_g_q': gain(ks[3], (L, MLA_Q_RANK)),
        'mla_g_kv': gain(ks[4], (L, MLA_KV_RANK)),
        'mla_w_uq': nrm(ks[5], (L, MLA_Q_RANK, MLA_H * (MLA_NOPE + MLA_ROPE)), MLA_Q_RANK ** -0.5),
        'mla_w_ukv': nrm(ks[6], (L, MLA_KV_RANK, MLA_H * (MLA_NOPE + MLA_V)), MLA_KV_RANK ** -0.5),
        'swa_sinks': nrm(ks[7], (L, SWA_H), 0.5),
        'mix_g': gain(ks[8], (L, MIX_WIDTH)),
        'w_o': nrm(ks[9], (L, MIX_WIDTH, D_MODEL), BETA * MIX_WIDTH ** -0.5),
        'ln1_g': gain(ks[10], (L, D_MODEL)),
        'ln1_b': nrm(ks[11], (L, D_MODEL), 0.02),
        'w_gate': nrm(ks[12], (L, D_MODEL, D_FF), D_MODEL ** -0.5),
        'w_up': nrm(ks[13], (L, D_MODEL, D_FF), D_MODEL ** -0.5),
        'w_down': nrm(ks[14], (L, D_FF, D_MODEL), BETA * D_FF ** -0.5),
        'ln2_g': gain(ks[15], (L, D_MODEL)),
        'ln2_b': nrm(ks[16], (L, D_MODEL), 0.02),
    }

def second_block(x, w_in, fox_b_f, mla_g_q, mla_g_kv, mla_w_uq, mla_w_ukv, swa_sinks, mix_g, w_o,
              ln1_g, ln1_b, w_gate, w_up, w_down, ln2_g, ln2_b):
    B, S, _ = x.shape
    cos, sin = _rope_tables(S)
    slopes = _alibi_slopes(SWA_H)
    points = [int(p) for p in np.cumsum(SPLIT_SIZES)[:-1]]
    for l in range(DEPTH):
        h = x @ w_in[l]
        (fq, fk, fv, fgate, cq, ckv, kr, sq, sk, sv, wq, wk, wv) = jnp.split(h, points, axis=-1)
        log_f = jax.nn.log_sigmoid(fgate.astype(jnp.float32) + fox_b_f[l].astype(jnp.float32))
        cum = jnp.cumsum(log_f, axis=1).transpose(0, 2, 1)
        out_a = _causal_softmax_blocks(_heads(fq, FOX_H), _heads(fk, FOX_H), _heads(fv, FOX_H),
                                       HEAD_DIM ** -0.5, cum)
        out_b = _mla(cq, ckv, kr, mla_g_q[l], mla_g_kv[l], mla_w_uq[l], mla_w_ukv[l], cos, sin)
        out_c = _stick_breaking_blocks(_heads(sq, SB_H), _heads(sk, SB_H), _heads(sv, SB_H))
        out_d = _swa_sink_alibi(_heads(wq, SWA_H), _heads(wk, SWA_KV_H), _heads(wv, SWA_KV_H),
                                swa_sinks[l], slopes)
        mix = jnp.concatenate([out_a.reshape(B, S, GROUP_WIDTH), out_b.reshape(B, S, GROUP_WIDTH),
                               out_c.reshape(B, S, GROUP_WIDTH), out_d.reshape(B, S, GROUP_WIDTH)],
                              axis=-1).astype(x.dtype)
        y = _group_rmsnorm(mix, mix_g[l]) @ w_o[l]
        x = _layernorm(ALPHA * x + y, ln1_g[l], ln1_b[l])
        f = (jax.nn.silu(x @ w_gate[l]) * (x @ w_up[l])) @ w_down[l]
        x = _layernorm(ALPHA * x + f, ln2_g[l], ln2_b[l])
    return x


def setup_inputs(seed=0):
    out = dict(first_inputs(seed))
    for name, value in second_inputs(seed + 1).items():
        if name != "x":
            out[name + "_2"] = value
    return out


def reference(
    x, positions, norm_g, w_in, lam_q1, lam_k1, lam_q2, lam_k2, subln_g, sgu_ln_g, sgu_ln_b,
    sgu_w, sgu_b, w_branch, w_out, final_g, w_in_2, fox_b_f_2, mla_g_q_2, mla_g_kv_2,
    mla_w_uq_2, mla_w_ukv_2, swa_sinks_2, mix_g_2, w_o_2, ln1_g_2, ln1_b_2, w_gate_2, w_up_2,
    w_down_2, ln2_g_2, ln2_b_2,
):
    x = first_block(
        x, positions, norm_g, w_in, lam_q1, lam_k1, lam_q2, lam_k2, subln_g, sgu_ln_g, sgu_ln_b,
        sgu_w, sgu_b, w_branch, w_out, final_g,
    )
    return second_block(
        x, w_in_2, fox_b_f_2, mla_g_q_2, mla_g_kv_2, mla_w_uq_2, mla_w_ukv_2, swa_sinks_2,
        mix_g_2, w_o_2, ln1_g_2, ln1_b_2, w_gate_2, w_up_2, w_down_2, ln2_g_2, ln2_b_2,
    )


_drawn_inputs = setup_inputs


def setup_inputs(seed=0):
    import zlib

    import numpy as np

    out = dict(_drawn_inputs(seed))
    spreads = {}
    factors = {'lam_k1': 2.705,
     'lam_q2': 2.928,
     'subln_g': 3.949,
     'sgu_ln_g': 7.19,
     'sgu_ln_b': 8.0,
     'fox_b_f_2': 64.0,
     'mla_g_q_2': 8.0,
     'mla_g_kv_2': 7.242,
     'swa_sinks_2': 7.216,
     'mix_g_2': 5.257}
    for name, (base, spread) in spreads.items():
        noise = np.random.default_rng([zlib.crc32(name.encode()), seed]).standard_normal(out[name].shape)
        drawn = base * np.exp(spread * noise) if base else spread * noise
        out[name] = __import__('jax').numpy.asarray(drawn.astype(out[name].dtype))
    for name, factor in factors.items():
        out[name] = (out[name] * factor).astype(out[name].dtype)
    return out
```

```python
import math
from contextlib import ExitStack

import concourse.bass as bass
from concourse import mybir

F32 = mybir.dt.float32
F32R = mybir.dt.float32r
I32 = mybir.dt.int32
ALU = mybir.AluOpType
ACT = mybir.ActivationFunctionType
AX = mybir.AxisListType

DEPTH = 2
SEQ = 512
D = 1024
P = 128
NB = SEQ // P
KD = D // P
UNIT = 1024
RAW = 4
EPS = 1e-6
LN_EPS = 1e-5
ALPHA = (2.0 * DEPTH) ** 0.25
NEG = -(2.0 ** 100)
HD = 64

B1_V = 0
B1_UZ = 4
B1_HEADS = 12
B1_GATE = 44
B1_OUT = 92
B1_UNITS = 100
N_ATT = 8
N_A = 4

B2_PROJ = 0
B2_WO = 28
FF_TILES = 22
FF_HALF = FF_TILES // 2
DOWN_UNITS = (FF_HALF + 1) // 2
B2_FFN = 36
B2_FFN_HALF = 2 * FF_HALF + 2 * DOWN_UNITS
B2_UNITS = B2_FFN + 2 * B2_FFN_HALF

C_IDENT, C_ONES, C_NTRI, C_NONES, C_ROPE1, C_ROPE2, C_UPPER = (P * i for i in range(7))
C_SEL = 7 * P
C_INV = C_SEL + 4 * P
C_KEEP = C_INV + 1
M_CAUSAL, M_STRICT = 0, P
M_MULT = 2 * P
M_SWA = M_MULT + SEQ
M_WIDTH = M_SWA + 8 * P

P1_NORM, P1_SUBLN, P1_LAM, P1_INIT, P1_KEEP = 0, 8, 9, 9 + 4 * HD, 10 + 4 * HD
P1_COLS = 11 + 4 * HD
P2_GQ, P2_GKV, P2_MIX, P2_BF, P2_SINK = 0, 2, 3, 11, 12
P2_COLS = 16
ROWP = 2048


class Steps:

    def __init__(self, eng, sem):
        self.eng, self.sem, self.n = eng, sem, 0

    def __call__(self, ins):
        ins.then_inc(self.sem, 1)
        self.n += 1
        return self.n

    def wait(self, value=None):
        self.eng.wait_ge(self.sem, self.n if value is None else value)


def program(nc, x_in, pos_in, const_in, mask_in, rope2_in, w1_in, col1_in, row1_in, final_in,
            w2_in, col2_in, row2_in, out):
    ctx = ExitStack()
    with ctx:
        base = nc.sbuf_base
        top = [(base + 31) // 32 * 32]
        addr = {}

        def sb(name, shape, dt=F32, at=None):
            size = 4
            for s in shape[1:]:
                size *= s
            offset = top[0] if at is None else at
            addr[name] = offset
            if at is None:
                top[0] += (size + 31) // 32 * 32
            return nc.alloc_sbuf_tensor_at(name, shape, dt, offset=offset)

        def sem(name):
            return ctx.enter_context(nc.semaphore(name))

        x = sb("x", [P, NB, D])
        h_hi = sb("h_hi", [P, KD, SEQ], F32R)
        h_lo = sb("h_lo", [P, KD, SEQ], F32R)
        raw_w = [sb(f"raw_w{s}", [P, UNIT]) for s in range(RAW)]
        w_hi = [sb(f"w_hi{s}", [P, UNIT], F32R) for s in range(2)]
        w_lo = [sb(f"w_lo{s}", [P, UNIT], F32R) for s in range(2)]
        act_hi = sb("act_hi", [P, 12, SEQ], F32R)
        act_lo = sb("act_lo", [P, 12, SEQ], F32R)
        const = sb("const", [P, C_KEEP])
        ident_r = sb("ident_r", [P, P], F32R)
        causal_r = sb("causal_r", [P, P], F32R)
        sbmask_r = sb("sbmask_r", [P, P], F32R)
        m2_hi = sb("m2_hi", [P, SEQ], F32R)
        m2_lo = sb("m2_lo", [P, SEQ], F32R)
        swa_r = sb("swa_r", [P, 4, 2 * P], F32R)
        cos = sb("cos", [P, SEQ])
        sin = sb("sin", [P, SEQ])
        rowp = sb("rowp", [P, ROWP])
        colp = sb("colp", [P, max(P1_COLS, P2_COLS)])
        small = sb("small", [P, 64])
        ext = [sb(f"ext{i}", [P, SEQ]) for i in range(4)]
        shared = top[0]
        qs = [sb(f"qs{i}", [P, SEQ]) for i in range(2)]
        ks = [sb(f"ks{i}", [P, SEQ]) for i in range(2)]
        vs = [sb(f"vs{i}", [P, NB, P]) for i in range(2)]
        raw_t = [sb(f"raw_t{i}", [P, SEQ]) for i in range(2)]
        prob = [sb(f"prob{i}", [P, SEQ]) for i in range(2)]
        pn = [sb(f"pn{i}", [P, SEQ]) for i in range(2)]
        pT = [sb(f"pT{i}", [P, SEQ]) for i in range(2)]
        sz = [sb(f"sz{i}", [P, SEQ]) for i in range(2)]
        z_t = sb("z_t", [P, SEQ])
        nrm = sb("nrm", [P, SEQ])
        rope_a = sb("rope_a", [P, SEQ])
        rope_b = sb("rope_b", [P, SEQ])
        ytmp = sb("ytmp", [P, SEQ])
        masks = sb("masks", [P, M_WIDTH], at=shared)
        hn = sb("hn", [P, NB, D], at=shared)
        mrg_hi = sb("mrg_hi", [P, KD, SEQ], F32R, at=shared)
        mrg_lo = sb("mrg_lo", [P, KD, SEQ], F32R, at=shared + KD * SEQ * 4)
        rowp_at, m2_at = addr["rowp"], addr["m2_hi"]
        wq_t = [sb(f"wq_t{i}", [P, SEQ], at=rowp_at + 4 * SEQ * i) for i in range(2)]
        wk_t = sb("wk_t", [P, SEQ], at=rowp_at + 8 * SEQ)
        ckv_t = sb("ckv_t", [P, SEQ], at=rowp_at + 12 * SEQ)
        cq_t = [sb(f"cq_t{i}", [P, SEQ], at=m2_at + 4 * SEQ * i) for i in range(2)]
        qr_t = sb("qr_t", [P, SEQ], at=addr["act_hi"] + 11 * 4 * SEQ)

        ps = [ctx.enter_context(nc.psum_tensor(f"bank{i}", [P, SEQ], F32)) for i in range(8)]
        PT, S, T, R, O = ps[0:2], ps[2:4], ps[4:6], ps[6], ps[7]
        TOK = ps[2:6]

        ident = const[:, C_IDENT:C_IDENT + P]
        ones = const[:, C_ONES:C_ONES + P]
        neg_tri = const[:, C_NTRI:C_NTRI + P]
        neg_ones = const[:, C_NONES:C_NONES + P]
        rope1 = const[:, C_ROPE1:C_ROPE1 + P]
        rope2 = const[:, C_ROPE2:C_ROPE2 + P]

        raw_loaded = [sem(f"raw_loaded{s}") for s in range(RAW)]
        params_loaded = sem("params_loaded")
        rows_loaded = sem("rows_loaded")
        hi_split = sem("hi_split")
        split_done = sem("split_done")
        unit_done = sem("unit_done")
        tile_out = [sem(f"tile_out{b}") for b in range(2)]
        tok_out = sem("tok_out")
        norm_in = sem("norm_in")
        xt_ready = sem("xt_ready")
        xt_hi = sem("xt_hi")
        xt_lo = sem("xt_lo")
        r_ready = sem("r_ready")
        r_out = sem("r_out")
        qk_ready = sem("qk_ready")
        scores_ready = sem("scores_ready")
        max_ready = sem("max_ready")
        probs_ready = sem("probs_ready")
        probs_normed = sem("probs_normed")
        t_ready = sem("t_ready")
        t_out = sem("t_out")
        pv_done = sem("pv_done")
        o_out = sem("o_out")
        sq_ready = sem("sq_ready")
        rs_ready = sem("rs_ready")
        z_ready = sem("z_ready")
        v_ready = sem("v_ready")
        vb_ready = sem("vb_ready")
        y_ready = sem("y_ready")
        merged = sem("merged")
        stat_ready = sem("stat_ready")
        lam_exp = sem("lam_exp")
        gate_ready = sem("gate_ready")
        latent_ready = sem("latent_ready")
        sb_scores = sem("sb_scores")
        sb_ln = sem("sb_ln")
        sb_sp = sem("sb_sp")
        sb_cum = sem("sb_cum")
        sb_sum = sem("sb_sum")
        sb_prob = sem("sb_prob")
        ln_done = sem("ln_done")
        ln_centre = sem("ln_centre")
        gate_ln = sem("gate_ln")
        gu_ready = sem("gu_ready")
        dve_step = sem("dve_step")
        act_step = sem("act_step")
        stored = sem("stored")
        sems = range(raw_loaded[0].num, stored.num + 1)
        engines = [e.engine for e in (nc.sync, nc.gpsimd, nc.scalar, nc.vector, nc.tensor)]

        def end_of_stage():
            nc.multi_engine_barrier(engines, sems_to_clear=sems)

        def load_units(sp, w_layer, units):
            def one(n, s, i):
                if not (isinstance(i, int) and i == 0):
                    sp.wait_ge(split_done, n - (RAW - 1))
                sp.dma_start(raw_w[s][:, :], w_layer[bass.ds(n, 1), :, :].rearrange("a p c -> p (a c)")) \
                  .then_inc(raw_loaded[s], 16)
            for s in range(RAW):
                one(s, s, 0)
            with sp.Fori(1, units // RAW) as i:
                for s in range(RAW):
                    one(i * RAW + s, s, i)

        def split_units(pool, units):
            def one(n, s, i):
                pool.wait_ge(raw_loaded[s], (i + 1) * 16)
                if not (isinstance(n, int) and n < 2):
                    pool.wait_ge(unit_done, n - 1)
                nc.gpsimd.tensor_tensor(w_hi[s % 2][:, :], raw_w[s][:, :], ones[:, 0:1].to_broadcast([P, UNIT]), ALU.mult) \
                  .then_inc(hi_split, 1)
                pool.wait_ge(hi_split, n + 1)
                nc.gpsimd.tensor_tensor(w_lo[s % 2][:, :], raw_w[s][:, :], w_hi[s % 2][:, :].bitcast(F32),
                                        ALU.subtract).then_inc(split_done, 1)
            for s in range(RAW):
                one(s, s, 0)
            with pool.Fori(1, units // RAW) as i:
                for s in range(RAW):
                    one(i * RAW + s, s, i)

        def mm3(dst, lh, ll, rh, rl, start, stop):
            nc.tensor.matmul(dst, lh, rh, start=start, stop=False)
            nc.tensor.matmul(dst, ll, rh, start=False, stop=False)
            return nc.tensor.matmul(dst, lh, rl, start=False, stop=stop)

        def tile_part(pe, n, before, half, slot, kt=KD, mov=None):
            m_hi, m_lo = mov if mov else (h_hi, h_lo)
            if half == 0:
                pe.wait_ge(split_done, n + 1)
                if not (isinstance(before, int) and before == 0):
                    pe.wait_ge(tile_out[slot], before)
            wh = w_hi[slot][:, :].rearrange("p (k c) -> p k c", c=P)
            wl = w_lo[slot][:, :].rearrange("p (k c) -> p k c", c=P)
            cut = (kt + 1) // 2
            for k in (range(cut) if half == 0 else range(cut, kt)):
                last = mm3(PT[slot][:, :], wh[:, k, :], wl[:, k, :], m_hi[:, k, :], m_lo[:, k, :],
                           k == 0, k == kt - 1)
            if half == 1 or kt == 1:
                last.then_inc(unit_done, 1)

        def tok_group(pe, n0, units, kts, st_hi, st_lo, before):
            for j in range(units):
                pe.wait_ge(split_done, n0 + j + 1)
                s = (n0 + j) % 2
                wh = w_hi[s][:, :].rearrange("p (k c) -> p k c", c=SEQ)
                wl = w_lo[s][:, :].rearrange("p (k c) -> p k c", c=SEQ)
                for tb in range(NB):
                    if j == 0 and before:
                        pe.wait_ge(tok_out, before - NB + tb + 1)
                    cols = slice(tb * P, (tb + 1) * P)
                    for k in range(2 * j, min(2 * j + 2, kts)):
                        last = mm3(TOK[tb][:, :], st_hi[:, k, cols], st_lo[:, k, cols],
                                   wh[:, k - 2 * j, :], wl[:, k - 2 * j, :], k == 0, k == kts - 1)
                last.then_inc(unit_done, 1)

        def transpose_in(pe, src, k0):
            for k in range(KD):
                if k >= 2:
                    pe.wait_ge(xt_lo, k0 + k - 1)
                for tb in range(NB):
                    last = nc.tensor.transpose(S[k % 2][:, tb * P:(tb + 1) * P],
                                               src[:, tb, k * P:(k + 1) * P], ident)
                last.then_inc(xt_ready, 1)

        def xt_hi_copy(act, k0, gain=None):
            for k in range(KD):
                act.wait_ge(xt_ready, k0 + k + 1)
                nc.scalar.activation(h_hi[:, k, :], S[k % 2][:, :], ACT.Copy,
                                     scale=1.0 if gain is None else gain[:, k:k + 1]).then_inc(xt_hi, 1)

        def xt_lo_sub(dve, k0, gain=None):
            for k in range(KD):
                dve.wait_ge(xt_hi, k0 + k + 1)
                hi = h_hi[:, k, :].bitcast(F32)
                if gain is None:
                    nc.vector.tensor_tensor(h_lo[:, k, :], S[k % 2][:, :], hi, ALU.subtract).then_inc(xt_lo, 1)
                else:
                    nc.vector.scalar_tensor_tensor(out=h_lo[:, k, :], in0=S[k % 2][:, :],
                                                   scalar=gain[:, k:k + 1], in1=hi,
                                                   op0=ALU.mult, op1=ALU.subtract).then_inc(xt_lo, 1)

        def rms_stats(act, st, src, dst):
            for tb in range(NB):
                last = st(nc.scalar.activation(hn[:, tb, :], src[:, tb, :], ACT.Square,
                                               accum_out=small[:, 60 + tb - 4:61 + tb - 4]))
            st.wait(last)
            st.wait(st(nc.scalar.activation(small[:, 60:64], small[:, 56:60], ACT.Ln, scale=1.0 / D, bias=EPS)))
            nc.scalar.activation(dst, small[:, 60:64], ACT.Exp, scale=-0.5).then_inc(stat_ready, 1)

        with nc.Block() as block:
            @block.sync
            def _(sp):
                sp.dma_start(const[:, :], const_in).then_inc(params_loaded, 16)
                sp.dma_start(masks[:, :], mask_in).then_inc(raw_loaded[1], 16)
                sp.dma_start(z_t[:, :].bitcast(I32), pos_in.partition_broadcast(P)).then_inc(rows_loaded, 16)
                sp.dma_start(x[:, :, :], x_in.rearrange("(b p) d -> p b d", p=P)).then_inc(raw_loaded[0], 16)
                sp.wait_ge(raw_loaded[0], 16)

            @block.vector
            def _(dve):
                st = Steps(dve, dve_step)
                dve.wait_ge(params_loaded, 16)
                st(nc.vector.tensor_copy(ident_r[:, :], ident))
                dve.wait_ge(raw_loaded[1], 16)
                st(nc.vector.tensor_copy(causal_r[:, :], masks[:, M_CAUSAL:M_CAUSAL + P]))
                st(nc.vector.tensor_copy(sbmask_r[:, :], masks[:, M_STRICT:M_STRICT + P]))
                st(nc.vector.tensor_copy(swa_r[:, :, :],
                                         masks[:, M_SWA:M_SWA + 8 * P].rearrange("p (h c) -> p h c", h=4)))
                m2 = masks[:, M_MULT:M_MULT + SEQ]
                st.wait(st(nc.vector.tensor_copy(m2_hi[:, :], m2)))
                st(nc.vector.tensor_tensor(m2_lo[:, :], m2, m2_hi[:, :].bitcast(F32), ALU.subtract))
                dve.wait_ge(rows_loaded, 16)
                st.wait(st(nc.vector.tensor_copy(nrm[:, :], z_t[:, :].bitcast(I32))))
                st.wait(st(nc.vector.tensor_scalar(rope_a[:, :], nrm[:, :], const[:, C_INV:C_INV + 1], None, ALU.mult)))
                big = 1.5 * 2.0 ** 23
                st.wait(st(nc.vector.tensor_scalar(nrm[:, :], rope_a[:, :], 1.0 / (2 * math.pi), big,
                                                   ALU.mult, ALU.add)))
                st.wait(st(nc.vector.tensor_scalar(nrm[:, :], nrm[:, :], big, None, ALU.subtract)))
                two_pi = 2 * math.pi
                p1 = 6.28125
                p2 = math.floor((two_pi - p1) * 2.0 ** 21) / 2.0 ** 21
                p3 = two_pi - p1 - p2
                for part in (p1, p2, p3):
                    st.wait(st(nc.vector.scalar_tensor_tensor(out=rope_a[:, :], in0=nrm[:, :], scalar=-part,
                                                              in1=rope_a[:, :], op0=ALU.mult, op1=ALU.add)))
                st.wait(st(nc.vector.tensor_scalar(rope_a[:, :], rope_a[:, :], math.pi, -math.pi, ALU.min, ALU.max)))
                st.wait(st(nc.vector.tensor_scalar(rope_b[:, :], rope_a[:, :], -1.0, None, ALU.mult)))
                st.wait(st(nc.vector.tensor_tensor(rope_b[:, :], rope_a[:, :], rope_b[:, :], ALU.max)))
                nc.vector.tensor_scalar(rope_b[:, :], rope_b[:, :], -1.0, math.pi / 2, ALU.mult, ALU.add) \
                  .then_inc(qk_ready, 1)

            @block.scalar
            def _(act):
                st = Steps(act, act_step)
                act.wait_ge(qk_ready, 1)
                st(nc.scalar.activation(sin[:, :], rope_a[:, :], ACT.Sin))
                st(nc.scalar.activation(cos[:, :], rope_b[:, :], ACT.Sin))
        end_of_stage()

        def t_index(a, qb, m, paired_from):
            return 4 * a + qb if a < paired_from else 4 * paired_from + 8 * (a - paired_from) + 2 * qb + m

        def before1(n):
            return (n - 4) // 2

        def head_unit(f, j):
            return B1_HEADS + 4 * f + j

        def r_first1(a):
            return 4 + 3 + sum(3 + (1 <= b <= N_A) for b in range(a))

        def r_rope1(f):
            return 4 if f == 0 else r_first1(f - 1) + (1 <= f - 1 <= N_A)

        def ti1(a, qb, m):
            return t_index(a, qb, m, N_A)

        with nc.Fori(0, DEPTH) as layer:
            with nc.Block() as block:
                w_layer = w1_in[bass.ds(layer, 1), :, :, :].rearrange("l n p c -> (l n) p c")

                @block.sync
                def _(sp):
                    sp.dma_start(colp[:, 0:P1_COLS], col1_in[bass.ds(layer, 1), :, :].rearrange("l p c -> p (l c)")) \
                      .then_inc(params_loaded, 16)
                    sp.dma_start(rowp[:, :], row1_in[bass.ds(layer, 1), :, :].rearrange("l p c -> p (l c)")) \
                      .then_inc(rows_loaded, 16)
                    load_units(sp, w_layer, B1_UNITS)

                @block.gpsimd
                def _(pool):
                    split_units(pool, B1_UNITS)

                @block.tensor
                def _(pe):
                    pe.wait_ge(norm_in, NB)
                    transpose_in(pe, hn, 0)
                    pe.wait_ge(xt_lo, KD)
                    for j in range(4):
                        pe.wait_ge(split_done, B1_V + j + 1)
                        s = j % 2
                        wh = w_hi[s][:, :].rearrange("p (k c) -> p k c", c=SEQ)
                        wl = w_lo[s][:, :].rearrange("p (k c) -> p k c", c=SEQ)
                        for tb in range(NB):
                            for k in (2 * j, 2 * j + 1):
                                last = mm3(TOK[tb][:, :], h_hi[:, k, tb * P:(tb + 1) * P], h_lo[:, k, tb * P:(tb + 1) * P],
                                           wh[:, k - 2 * j, :], wl[:, k - 2 * j, :], k == 0, k == KD - 1)
                        last.then_inc(unit_done, 1)

                    def mix(g):
                        pe.wait_ge(vb_ready, 2 * NB)
                        if g:
                            pe.wait_ge(r_out, g)
                        for c in range(NB):
                            last = nc.tensor.matmul(R[:, c * P:(c + 1) * P], ext[c][:, g * P:(g + 1) * P],
                                                    rowp[:, 3 * SEQ + g * P:3 * SEQ + (g + 1) * P], start=True, stop=True)
                        last.then_inc(r_ready, 1)

                    for g in range(4):
                        for j in range(2):
                            n = B1_UZ + 2 * g + j
                            for half in range(2):
                                tile_part(pe, n, before1(n), half, n % 2)
                        if g:
                            mix(g - 1)
                    mix(3)

                    def rope(f, which):
                        idx = r_rope1(f) + which
                        pe.wait_ge(tile_out[which], before1(head_unit(f, which)) + 1)
                        pe.wait_ge(r_out, idx)
                        nc.tensor.matmul(R[:, :], rope1, raw_t[which][:, :], start=True, stop=True).then_inc(r_ready, 1)

                    def v_transpose(f):
                        idx = r_rope1(f) + 2
                        pe.wait_ge(tile_out[0], before1(head_unit(f, 2)) + 1)
                        pe.wait_ge(r_out, idx)
                        for b in range(NB):
                            last = nc.tensor.transpose(R[:, b * P:(b + 1) * P], raw_t[0][:, b * P:(b + 1) * P], ident)
                        last.then_inc(r_ready, 1)

                    def scores(a, qb, m):
                        u, s, rows, nk = 8 * a + 2 * qb + m, a % 2, slice(HD * m, HD * m + HD), (qb + 1) * P
                        if qb == 0 and m == 0:
                            pe.wait_ge(qk_ready, 2 * a + 2)
                        if u >= 2:
                            pe.wait_ge(probs_ready, u - 1)
                        nc.tensor.matmul(S[m][:, 0:nk], qs[s][rows, qb * P:(qb + 1) * P], ks[s][rows, 0:nk],
                                         start=True, stop=False)
                        if a < N_A:
                            last = nc.tensor.matmul(S[m][:, nk - P:nk], ident_r[:, :], causal_r[:, :], start=False, stop=True)
                        else:
                            nc.tensor.matmul(S[m][:, 0:nk], ident_r[:, :], m2_hi[:, SEQ - nk:SEQ], start=False, stop=False)
                            last = nc.tensor.matmul(S[m][:, 0:nk], ident_r[:, :], m2_lo[:, SEQ - nk:SEQ],
                                                    start=False, stop=True)
                        last.then_inc(scores_ready, 1)

                    def probs_transpose(a, qb, m):
                        i = ti1(a, qb, m)
                        pe.wait_ge(probs_normed, 4 * a + qb + 1)
                        if i >= 2:
                            pe.wait_ge(t_out, i - 1)
                        for b in range(qb + 1):
                            last = nc.tensor.transpose(T[i % 2][:, b * P:(b + 1) * P], pn[m][:, b * P:(b + 1) * P], ident)
                        last.then_inc(t_ready, 1)

                    def pv(a, qb):
                        pe.wait_ge(t_out, ti1(a, qb, 0 if a < N_A else 1) + 1)
                        if qb == 0:
                            pe.wait_ge(r_out, r_rope1(a) + 3)
                            if a:
                                pe.wait_ge(o_out, a)
                        cols = slice(qb * P, (qb + 1) * P)
                        for m in range(1 if a < N_A else 2):
                            rows = slice(0, P) if a < N_A else slice(HD * m, HD * m + HD)
                            for b in range(qb + 1):
                                last = nc.tensor.matmul(O[rows, cols], vs[a % 2][:, b, rows],
                                                        pT[ti1(a, qb, m) % 2][:, b * P:(b + 1) * P],
                                                        start=(b == 0), stop=(b == qb))
                        last.then_inc(pv_done, 1)

                    def fill(a, part):
                        if a + 1 < N_ATT:
                            n = head_unit(a + 1, part // 2)
                            tile_part(pe, n, before1(n), part % 2, n % 2)

                    for j in range(4):
                        n = head_unit(0, j)
                        for half in range(2):
                            tile_part(pe, n, before1(n), half, n % 2)
                        if j == 1:
                            rope(0, 0)
                        elif j == 2:
                            rope(0, 1)
                    v_transpose(0)
                    for a in range(N_ATT):
                        for qb in range(NB):
                            scores(a, qb, 0)
                            scores(a, qb, 1)
                            fill(a, 2 * qb)
                            if qb == 0 and 1 <= a <= N_A:
                                pe.wait_ge(sq_ready, a)
                                pe.wait_ge(r_out, r_first1(a))
                                nc.tensor.matmul(R[:, :], ones, nrm[:, :], start=True, stop=True).then_inc(r_ready, 1)
                            if qb:
                                probs_transpose(a, qb - 1, 0)
                            fill(a, 2 * qb + 1)
                            if qb:
                                if a >= N_A:
                                    probs_transpose(a, qb - 1, 1)
                                pv(a, qb - 1)
                            if a + 1 < N_ATT:
                                if qb == 1:
                                    rope(a + 1, 0)
                                elif qb == 2:
                                    rope(a + 1, 1)
                                elif qb == 3:
                                    v_transpose(a + 1)
                        probs_transpose(a, 3, 0)
                        if a >= N_A:
                            probs_transpose(a, 3, 1)
                        pv(a, 3)
                    pe.wait_ge(y_ready, 12)
                    with pe.Fori(0, KD) as m:
                        for i in range(3):
                            n = m * 6 + (B1_GATE + 2 * i)
                            before = m * 3 + (before1(B1_GATE) + i)
                            for half in range(2):
                                tile_part(pe, n, before, half, 0)
                            for half in range(2):
                                tile_part(pe, n + 1, before, half, 1, kt=4,
                                          mov=(act_hi[:, 4 * i:4 * i + 4, :], act_lo[:, 4 * i:4 * i + 4, :]))
                    pe.wait_ge(merged, KD)
                    for c in range(2):
                        tok_group(pe, B1_OUT + 4 * c, 4, KD, mrg_hi, mrg_lo, NB * c)

                @block.scalar
                def _(act):
                    st = Steps(act, act_step)
                    rms_stats(act, st, x, small[:, 0:4])
                    act.wait_ge(params_loaded, 16)
                    xt_hi_copy(act, 0, colp[:, P1_NORM:P1_NORM + KD])
                    act.wait_ge(lam_exp, 1)
                    nc.scalar.activation(small[:, 6:8], small[:, 4:6], ACT.Exp).then_inc(lam_exp, 1)
                    act.wait_ge(unit_done, 4)
                    for tb in range(NB):
                        nc.scalar.activation(ext[tb][:, :], TOK[tb][:, :], ACT.Gelu_apprx_tanh,
                                             accum_out=small[:, 12 + tb:13 + tb]).then_inc(v_ready, 1)
                    for tb in range(NB):
                        act.wait_ge(vb_ready, tb + 1)
                        last = st(nc.scalar.activation((*qs, *ks)[tb][:, :], ext[tb][:, :], ACT.Square,
                                                       accum_out=small[:, 16 + tb:17 + tb]))
                    st.wait(last)
                    st.wait(st(nc.scalar.activation(small[:, 20:24], small[:, 16:20], ACT.Ln, scale=1.0 / SEQ, bias=EPS)))
                    nc.scalar.activation(small[:, 20:24], small[:, 20:24], ACT.Exp, scale=-0.5).then_inc(stat_ready, 1)
                    for g in range(4):
                        n = B1_UZ + 2 * g
                        act.wait_ge(unit_done, n + 1)
                        if g:
                            act.wait_ge(y_ready, g)
                        nc.scalar.activation(sz[0][:, :], PT[0][:, :], ACT.Gelu_apprx_tanh).then_inc(tile_out[0], 1)
                        act.wait_ge(unit_done, n + 2)
                        nc.scalar.activation(z_t[:, :], PT[1][:, :], ACT.Tanh, scale=0.5).then_inc(z_ready, 1)

                    def raw_copy(f, j):
                        n = head_unit(f, j)
                        act.wait_ge(unit_done, n + 1)
                        if j == 0 and f:
                            act.wait_ge(r_ready, r_rope1(f - 1) + 3)
                        elif j == 1 and f:
                            act.wait_ge(qk_ready, 2 * f)
                        elif j == 2:
                            act.wait_ge(qk_ready, 2 * f + 1)
                        nc.scalar.activation(raw_t[j % 2][:, :], PT[n % 2][:, :], ACT.Copy,
                                             scale=HD ** -0.5 if j == 0 else 1.0).then_inc(tile_out[n % 2], 1)

                    def v_copy(f):
                        act.wait_ge(r_ready, r_rope1(f) + 3)
                        if f >= 2:
                            act.wait_ge(pv_done, 4 * (f - 1))
                        nc.scalar.activation(vs[f % 2][:, :, :], R[:, :].rearrange("p (b c) -> p b c", c=P), ACT.Copy) \
                          .then_inc(r_out, 1)

                    def z_tanh(f):
                        act.wait_ge(unit_done, head_unit(f, 3) + 1)
                        act.wait_ge(tile_out[1], before1(head_unit(f, 3)))
                        nc.scalar.activation(z_t[:, :], PT[1][:, :], ACT.Tanh, scale=0.5).then_inc(z_ready, 1)

                    def softmax_exp(a, qb, m):
                        u, nk = 8 * a + 2 * qb + m, (qb + 1) * P
                        act.wait_ge(max_ready, u + 1)
                        if u >= 2:
                            act.wait_ge(probs_normed, 4 * a + qb)
                        nc.scalar.activation(prob[m][:, 0:nk], S[m][:, 0:nk], ACT.Exp, bias=small[:, 24 + 2 * qb + m:25 + 2 * qb + m],
                                             accum_out=small[:, 32 + 2 * qb + m:33 + 2 * qb + m]).then_inc(probs_ready, 1)

                    def pT_copy(a, qb):
                        for m in range(1 if a < N_A else 2):
                            i = ti1(a, qb, m)
                            act.wait_ge(t_ready, i + 1)
                            w = 4 * a + qb - (1 if a < N_A else 0)
                            if a == N_A and qb == 0:
                                w = 4 * a
                            if w > 0:
                                act.wait_ge(pv_done, w)
                            nc.scalar.activation(pT[i % 2][:, 0:(qb + 1) * P], T[i % 2][:, 0:(qb + 1) * P], ACT.Copy) \
                              .then_inc(t_out, 1)

                    for j in range(3):
                        raw_copy(0, j)
                    v_copy(0)
                    for a in range(N_ATT):
                        for qb in range(NB):
                            if qb == 0:
                                if 1 <= a <= N_A:
                                    act.wait_ge(pv_done, 4 * a)
                                    if a >= 2:
                                        act.wait_ge(o_out, a - 1)
                                    nc.scalar.activation(nrm[:, :], O[:, :], ACT.Square).then_inc(sq_ready, 1)
                                z_tanh(a)
                            elif a + 1 < N_ATT:
                                raw_copy(a + 1, qb - 1)
                            softmax_exp(a, qb, 0)
                            softmax_exp(a, qb, 1)
                            if qb == 0 and 1 <= a <= N_A:
                                act.wait_ge(r_ready, r_first1(a) + 1)
                                ln = nc.scalar.activation(nrm[:, :], R[:, :], ACT.Ln, scale=1.0 / P, bias=EPS)
                                ln.then_inc(r_out, 1)
                                act.wait_ge(r_out, r_first1(a) + 1)
                                nc.scalar.activation(nrm[:, :], nrm[:, :], ACT.Exp, scale=-0.5).then_inc(rs_ready, 1)
                            if qb:
                                pT_copy(a, qb - 1)
                        if a + 1 < N_ATT:
                            v_copy(a + 1)
                        pT_copy(a, 3)
                    with act.Fori(0, KD) as m:
                        for i in range(3):
                            act.wait_ge(unit_done, m * 6 + (B1_GATE + 2 * i + 1))
                            act.wait_ge(tile_out[1], m * 3 + (before1(B1_GATE) + i))
                            nc.scalar.activation(ext[i][:, :], PT[0][:, :], ACT.Sigmoid).then_inc(tile_out[0], 1)

                @block.vector
                def _(dve):
                    st = Steps(dve, dve_step)
                    dve.wait_ge(stat_ready, 1)
                    for tb in range(NB):
                        nc.vector.tensor_scalar(hn[:, tb, :], x[:, tb, :], small[:, tb:tb + 1], None, ALU.mult) \
                          .then_inc(norm_in, 1)
                    dve.wait_ge(params_loaded, 16)
                    xt_lo_sub(dve, 0, colp[:, P1_NORM:P1_NORM + KD])
                    lam = colp[:, P1_LAM:P1_LAM + 4 * HD].rearrange("p (a b d) -> p a b d", a=2, b=2)
                    st.wait(st(nc.vector.tensor_tensor(rope_a[:, 0:2 * HD].rearrange("p (a d) -> p a d", a=2),
                                                       lam[:, :, 0, :], lam[:, :, 1, :], ALU.mult)))
                    nc.vector.tensor_reduce(small[:, 4:6], rope_a[:, 0:2 * HD].rearrange("p (a d) -> p a d", a=2),
                                            AX.X, ALU.add).then_inc(lam_exp, 1)
                    dve.wait_ge(lam_exp, 2)
                    st.wait(st(nc.vector.tensor_tensor(small[:, 8:9], small[:, 6:7], small[:, 7:8], ALU.subtract)))
                    st(nc.vector.tensor_tensor(small[:, 8:9], small[:, 8:9], colp[:, P1_INIT:P1_INIT + 1], ALU.add))
                    st(nc.vector.scalar_tensor_tensor(out=small[:, 9:10], in0=colp[:, P1_SUBLN:P1_SUBLN + 1], scalar=0.5,
                                                      in1=colp[:, P1_KEEP:P1_KEEP + 1], op0=ALU.mult, op1=ALU.mult))
                    dve.wait_ge(rows_loaded, 16)
                    sgw = rowp[:, 3 * SEQ:4 * SEQ].rearrange("p (g t) -> p g t", g=4)
                    upper = const[:, C_UPPER:C_UPPER + P].unsqueeze(1).to_broadcast([P, 4, P])
                    st(nc.vector.tensor_tensor(sgw, sgw, upper, ALU.mult))
                    for tb in range(NB):
                        dve.wait_ge(v_ready, tb + 1)
                        st.wait(st(nc.vector.tensor_scalar(small[:, 12 + tb:13 + tb], small[:, 12 + tb:13 + tb],
                                                           -1.0 / SEQ, None, ALU.mult)))
                        nc.vector.tensor_scalar(ext[tb][:, :], ext[tb][:, :], small[:, 12 + tb:13 + tb], None, ALU.add) \
                          .then_inc(vb_ready, 1)
                    dve.wait_ge(stat_ready, 2)
                    for tb in range(NB):
                        st.wait(st(nc.vector.scalar_tensor_tensor(out=ext[tb][:, :], in0=ext[tb][:, :],
                                                                  scalar=small[:, 20 + tb:21 + tb], in1=rowp[:, 0:SEQ],
                                                                  op0=ALU.mult, op1=ALU.mult)))
                        nc.vector.tensor_tensor(ext[tb][:, :], ext[tb][:, :], rowp[:, SEQ:2 * SEQ], ALU.add) \
                          .then_inc(vb_ready, 1)

                    def split_y(i):
                        st.wait(st(nc.vector.tensor_copy(act_hi[:, i, :], ytmp[:, :])))
                        nc.vector.tensor_tensor(act_lo[:, i, :], ytmp[:, :], act_hi[:, i, :].bitcast(F32), ALU.subtract) \
                          .then_inc(y_ready, 1)

                    for g in range(4):
                        dve.wait_ge(z_ready, g + 1)
                        nc.vector.scalar_tensor_tensor(out=sz[1][:, :], in0=z_t[:, :], scalar=1.0, in1=PT[1][:, :],
                                                       op0=ALU.add, op1=ALU.mult).then_inc(tile_out[1], 1)
                        dve.wait_ge(r_ready, g + 1)
                        bias = rowp[:, 2 * SEQ + g * P:2 * SEQ + (g + 1) * P].unsqueeze(1).to_broadcast([P, NB, P])
                        nc.vector.tensor_tensor(rope_a[:, :].rearrange("p (c t) -> p c t", c=NB),
                                                R[:, :].rearrange("p (c t) -> p c t", c=NB), bias, ALU.add).then_inc(r_out, 1)
                        dve.wait_ge(r_out, g + 1)
                        dve.wait_ge(tile_out[0], g + 1)
                        st.wait(st(nc.vector.scalar_tensor_tensor(out=rope_a[:, :], in0=rope_a[:, :], scalar=0.5, in1=sz[0][:, :],
                                                                  op0=ALU.mult, op1=ALU.mult)))
                        dve.wait_ge(tile_out[1], g + 1)
                        st.wait(st(nc.vector.tensor_tensor(ytmp[:, :], rope_a[:, :], sz[1][:, :], ALU.mult)))
                        split_y(4 + g)

                    def rotate(f, which):
                        idx = r_rope1(f) + which
                        dst = (qs, ks)[which][f % 2]
                        dve.wait_ge(r_ready, idx + 1)
                        if which or f:
                            dve.wait_ge(qk_ready, 2 * f + which)
                        st(nc.vector.tensor_tensor(rope_a[:, :], raw_t[which][:, :], cos[:, :], ALU.mult))
                        nc.vector.tensor_tensor(rope_b[:, :], R[:, :], sin[:, :], ALU.mult).then_inc(r_out, 1)
                        st.wait()
                        dve.wait_ge(r_out, idx + 1)
                        nc.vector.tensor_tensor(dst[:, :], rope_a[:, :], rope_b[:, :], ALU.add).then_inc(qk_ready, 1)

                    def row_max(a, qb, m):
                        u = 8 * a + 2 * qb + m
                        dve.wait_ge(scores_ready, u + 1)
                        nc.vector.tensor_reduce(small[:, 24 + 2 * qb + m:25 + 2 * qb + m], S[m][:, 0:(qb + 1) * P], AX.X,
                                                ALU.max, negate=True).then_inc(max_ready, 1)

                    def silu_z(f):
                        dve.wait_ge(z_ready, 4 + f + 1)
                        nc.vector.scalar_tensor_tensor(out=sz[f % 2][:, :], in0=z_t[:, :], scalar=1.0, in1=PT[1][:, :],
                                                       op0=ALU.add, op1=ALU.mult).then_inc(tile_out[1], 1)

                    def normalise(a, qb):
                        nk = (qb + 1) * P
                        l, r = small[:, 32 + 2 * qb:34 + 2 * qb], small[:, 40:42]
                        dve.wait_ge(probs_ready, 8 * a + 2 * qb + 2)
                        st.wait(st(nc.vector.reciprocal(r, l)))
                        if a or qb:
                            dve.wait_ge(t_ready, ti1(a, qb - 1, 1) + 1 if qb else ti1(a - 1, 3, 1) + 1)
                        if a < N_A:
                            st.wait(st(nc.vector.tensor_scalar(small[:, 41:42], small[:, 41:42], small[:, 8:9], None, ALU.mult)))
                            st.wait(st(nc.vector.tensor_scalar(prob[1][:, 0:nk], prob[1][:, 0:nk], small[:, 41:42], None, ALU.mult)))
                            nc.vector.scalar_tensor_tensor(out=pn[0][:, 0:nk], in0=prob[0][:, 0:nk], scalar=small[:, 40:41],
                                                           in1=prob[1][:, 0:nk], op0=ALU.mult, op1=ALU.subtract) \
                              .then_inc(probs_normed, 1)
                        else:
                            st.wait(st(nc.vector.tensor_scalar(pn[0][:, 0:nk], prob[0][:, 0:nk], small[:, 40:41], None, ALU.mult)))
                            nc.vector.tensor_scalar(pn[1][:, 0:nk], prob[1][:, 0:nk], small[:, 41:42], None, ALU.mult) \
                              .then_inc(probs_normed, 1)

                    def epilogue(a):
                        dve.wait_ge(pv_done, 4 * a + 4)
                        dve.wait_ge(tile_out[1], before1(head_unit(a, 3)) + 1)
                        if a < N_A:
                            dve.wait_ge(rs_ready, a + 1)
                            nc.vector.tensor_tensor(rope_a[:, :], O[:, :], nrm[:, :], ALU.mult).then_inc(o_out, 1)
                            dve.wait_ge(o_out, a + 1)
                            st.wait(st(nc.vector.scalar_tensor_tensor(out=ytmp[:, :], in0=rope_a[:, :], scalar=small[:, 9:10],
                                                                      in1=sz[a % 2][:, :], op0=ALU.mult, op1=ALU.mult)))
                        else:
                            nc.vector.scalar_tensor_tensor(out=ytmp[:, :], in0=O[:, :], scalar=0.5, in1=sz[a % 2][:, :],
                                                           op0=ALU.mult, op1=ALU.mult).then_inc(o_out, 1)
                            dve.wait_ge(o_out, a + 1)
                        split_y(a if a < N_A else 8 + a - N_A)

                    rotate(0, 0)
                    rotate(0, 1)
                    for a in range(N_ATT):
                        for qb in range(NB):
                            row_max(a, qb, 0)
                            row_max(a, qb, 1)
                            if qb == 0:
                                silu_z(a)
                            elif qb >= 2 and a + 1 < N_ATT:
                                rotate(a + 1, qb - 2)
                            normalise(a, qb)
                            if qb == 0 and a:
                                epilogue(a - 1)
                    epilogue(N_ATT - 1)
                    base_step = st.n
                    gate_acc = (ytmp[:, :], rope_a[:, :])
                    per_turn = 3
                    with dve.Fori(0, KD) as m:
                        k = 0

                        def chain(ins):
                            nonlocal k
                            k += 1
                            ins.then_inc(dve_step, 1)
                            dve.wait_ge(dve_step, m * per_turn + (base_step + k))

                        for i in range(3):
                            dve.wait_ge(tile_out[0], m * 3 + (before1(B1_GATE) + i + 1))
                            dve.wait_ge(unit_done, m * 6 + (B1_GATE + 2 * i + 2))
                            nc.vector.tensor_tensor(gate_acc[0 if i == 0 else 1], ext[i][:, :], PT[1][:, :], ALU.mult) \
                              .then_inc(tile_out[1], 1)
                            dve.wait_ge(tile_out[1], m * 3 + (before1(B1_GATE) + i + 1))
                            if i:
                                chain(nc.vector.tensor_tensor(gate_acc[0], gate_acc[0], gate_acc[1], ALU.add))
                        hi = mrg_hi[:, bass.ds(m, 1), :]
                        chain(nc.vector.tensor_copy(hi.rearrange("p a t -> p (a t)"), gate_acc[0]))
                        nc.vector.tensor_tensor(mrg_lo[:, bass.ds(m, 1), :].rearrange("p a t -> p (a t)"), gate_acc[0],
                                                hi.rearrange("p a t -> p (a t)").bitcast(F32), ALU.subtract).then_inc(merged, 1)
                        dve.wait_ge(merged, m + 1)
                    for c in range(2):
                        dve.wait_ge(unit_done, B1_OUT + 4 * c + 4)
                        for tb in range(NB):
                            cols = slice(c * SEQ, (c + 1) * SEQ)
                            nc.vector.tensor_tensor(x[:, tb, cols], x[:, tb, cols], TOK[tb][:, :], ALU.add).then_inc(tok_out, 1)
            end_of_stage()

        with nc.Block() as block:
            @block.sync
            def _(sp):
                sp.dma_start(rowp[:, 0:D], final_in.to_broadcast([P, D])).then_inc(rows_loaded, 16)
                sp.dma_start(cos[:, :], rope2_in[0, :, :]).then_inc(params_loaded, 16)
                sp.dma_start(sin[:, :], rope2_in[1, :, :]).then_inc(params_loaded, 16)
                sp.wait_ge(params_loaded, 32)

            @block.scalar
            def _(act):
                rms_stats(act, Steps(act, act_step), x, small[:, 0:4])

            @block.vector
            def _(dve):
                dve.wait_ge(stat_ready, 1)
                dve.wait_ge(rows_loaded, 16)
                for tb in range(NB):
                    nc.vector.scalar_tensor_tensor(out=x[:, tb, :], in0=x[:, tb, :], scalar=small[:, tb:tb + 1],
                                                   in1=rowp[:, 0:D], op0=ALU.mult, op1=ALU.mult)
        end_of_stage()

        FOX, SB, SWA, MLA = range(4)
        KIND = (FOX, FOX, SB, SB, SWA, SWA, MLA, MLA)
        SOFTMAX = {0: 0, 1: 1, 4: 2, 5: 3, 6: 4, 7: 5}
        R2 = {name: i for i, name in enumerate(
            ("v0", "v1", "v2", "vw", "e1", "v3", "e3", "ckv", "cq", "kr", "qr", "v6", "v7", "e5", "e7"))}
        V_UNITS = {2: ("v0", 0, vs[0]), 6: ("v1", 0, vs[1]), 10: ("v2", 0, vs[0]), 14: ("v3", 0, vs[1]),
                   11: ("vw", 1, None), 26: ("v6", 0, vs[0]), 27: ("v7", 1, vs[1])}
        vw_t = ext[3][:, :].rearrange("p (b c) -> p b c", c=P)
        U_GATE, U_CKV, U_WQ0, U_WK, U_WQ1, U_CQ, U_KR, U_UQ, U_UQR, U_UKV = 3, 7, 15, 16, 17, 18, 20, 21, 23, 24
        q_unit = {0: 0, 1: 4, 2: 8, 3: 12, 4: U_WQ0, 5: U_WQ1, 6: U_UQ, 7: U_UQ + 1}
        k_unit = {0: 1, 1: 5, 2: 9, 3: 13, 4: U_WK, 5: U_WK, 6: U_UKV, 7: U_UKV + 1}

        def q_of(a):
            return wq_t[a - 4] if KIND[a] == SWA else qs[a % 2]

        def k_of(a):
            return wk_t if KIND[a] == SWA else ks[a % 2]

        def v_of(a):
            return vw_t if KIND[a] == SWA else vs[a % 2]

        def head_of(a, m):
            i = a % 2
            return i + 2 * m if KIND[a] == SWA else 2 * i + m

        def first_key(a, qb):
            return max(0, qb - 1) * P if KIND[a] == SWA else 0

        def u_of(a, qb, m):
            return 8 * SOFTMAX[a] + 2 * qb + m

        mla_scale = (HD + HD // 2) ** -0.5
        kt_of = {U_UQ: 2, U_UQ + 1: 2, U_UQR: 2, **{U_UKV + j: 1 for j in range(4)}}

        with nc.Fori(0, DEPTH) as layer:
            with nc.Block() as block:
                w_layer2 = w2_in[bass.ds(layer, 1), :, :, :].rearrange("l n p c -> (l n) p c")
                rows2 = row2_in[bass.ds(layer, 1), :, :, :].rearrange("l r p c -> (l r) p c")

                @block.sync
                def _(sp):
                    sp.dma_start(colp[:, 0:P2_COLS], col2_in[bass.ds(layer, 1), :, :].rearrange("l p c -> p (l c)")) \
                      .then_inc(params_loaded, 16)
                    load_units(sp, w_layer2, B2_UNITS)

                @block.gpsimd
                def _(pool):
                    split_units(pool, B2_UNITS)

                @block.tensor
                def _(pe):
                    transpose_in(pe, x, 0)
                    pe.wait_ge(xt_lo, KD)

                    def part(n, half):
                        mov = None
                        if n in kt_of:
                            pe.wait_ge(latent_ready, 1 if kt_of[n] == 1 else 3)
                            t = 10 if kt_of[n] == 1 else 8
                            mov = (act_hi[:, t:t + 2, :], act_lo[:, t:t + 2, :])
                        if half == 0 or kt_of.get(n) != 1:
                            tile_part(pe, n, n // 2, half, n % 2, kt=kt_of.get(n, KD), mov=mov)

                    def r_free(name):
                        if R2[name]:
                            pe.wait_ge(r_out, R2[name])

                    def v_transpose(n):
                        name, buf, _ = V_UNITS[n]
                        pe.wait_ge(tile_out[n % 2], n // 2 + 1)
                        r_free(name)
                        for b in range(NB):
                            last = nc.tensor.transpose(R[:, b * P:(b + 1) * P], raw_t[buf][:, b * P:(b + 1) * P], ident)
                        last.then_inc(r_ready, 1)

                    def rope(name, n, buf):
                        pe.wait_ge(tile_out[n % 2], n // 2 + 1)
                        r_free(name)
                        nc.tensor.matmul(R[:, :], rope2, raw_t[buf][:, :], start=True, stop=True).then_inc(r_ready, 1)

                    def sum_squares(name, tiles, squares):
                        pe.wait_ge(sq_ready, squares)
                        r_free(name)
                        for i, t in enumerate(tiles):
                            last = nc.tensor.matmul(R[:, :], ones, t[:, :], start=(i == 0), stop=(i == len(tiles) - 1))
                        last.then_inc(r_ready, 1)

                    def scores(a, qb, m):
                        kind, u, k0, k1 = KIND[a], u_of(a, qb, m), first_key(a, qb), (qb + 1) * P
                        rows, h, nk = slice(HD * m, HD * m + HD), head_of(a, m), k1 - k0
                        if qb == 0 and m == 0:
                            pe.wait_ge(tile_out[q_unit[a] % 2], q_unit[a] // 2 + 1)
                            pe.wait_ge(tile_out[k_unit[a] % 2], k_unit[a] // 2 + 1)
                            if kind == FOX:
                                pe.wait_ge(gate_ready, 1)
                            elif kind == MLA:
                                pe.wait_ge(qk_ready, 2)
                        if u >= 2:
                            pe.wait_ge(probs_ready, u - 1)
                        block_q = slice(qb * P, (qb + 1) * P)
                        nc.tensor.matmul(S[m][:, 0:nk], q_of(a)[rows, block_q], k_of(a)[rows, k0:k1], start=True, stop=False)
                        if kind == FOX:
                            nc.tensor.matmul(S[m][:, 0:nk], const[0:4, C_SEL + h * P:C_SEL + (h + 1) * P], ext[2][0:4, 0:nk],
                                             start=False, stop=False)
                        elif kind == MLA:
                            r = slice(32 * h, 32 * h + 32)
                            nc.tensor.matmul(S[m][:, 0:nk], qr_t[r, block_q], z_t[r, 0:nk], start=False, stop=False,
                                             tile_position=(32 * h, 0))
                        if kind == SWA:
                            last = nc.tensor.matmul(S[m][:, 0:nk], ident_r[:, :], swa_r[:, h, 2 * P - nk:2 * P],
                                                    start=False, stop=True)
                        else:
                            last = nc.tensor.matmul(S[m][:, nk - P:nk], ident_r[:, :], causal_r[:, :], start=False, stop=True)
                        last.then_inc(scores_ready, 1)

                    def probs_transpose(a, qb, m):
                        u, nk = u_of(a, qb, m), (qb + 1) * P - first_key(a, qb)
                        pe.wait_ge(probs_normed, u // 2 + 1)
                        if u >= 2:
                            pe.wait_ge(t_out, u - 1)
                        for b in range(nk // P):
                            last = nc.tensor.transpose(T[m][:, b * P:(b + 1) * P], pn[m][:, b * P:(b + 1) * P], ident)
                        last.then_inc(t_ready, 1)

                    def v_wait(a):
                        n = {0: 2, 1: 6, 2: 10, 3: 14, 4: 11, 5: 11, 6: 26, 7: 27}[a]
                        pe.wait_ge(r_out, R2[V_UNITS[n][0]] + 1)
                        if a:
                            pe.wait_ge(o_out, a)

                    def pv(a, qb):
                        pe.wait_ge(t_out, u_of(a, qb, 1) + 1)
                        if qb == 0:
                            v_wait(a)
                        b0 = first_key(a, qb) // P
                        for m in range(2):
                            rows = slice(HD * m, HD * m + HD)
                            for b in range(b0, qb + 1):
                                last = nc.tensor.matmul(O[rows, qb * P:(qb + 1) * P], v_of(a)[:, b, rows],
                                                        pT[m][:, (b - b0) * P:(b - b0 + 1) * P], start=(b == b0), stop=(b == qb))
                        last.then_inc(pv_done, 1)

                    def fill(a, i):
                        if a + 1 < 7:
                            part(4 * (a + 1) + i // 2, i % 2)

                    def norm_work(a, qb):
                        if qb == 0 and a in (2, 4, 6):
                            sum_squares(f"e{a - 1}", (nrm, rope_b), {2: 1, 4: 2, 6: 4}[a])
                        if qb == 0 and a == 4:
                            sum_squares("ckv", (z_t,), 3)
                            sum_squares("cq", raw_t, 3)

                    def late_work(a, qb):
                        if a in (0, 1, 2, 5) and qb == 3:
                            v_transpose(4 * (a + 1) + 2)
                        if a == 4 and qb == 1:
                            rope("kr", U_KR, 0)

                    def end_work(a):
                        if a == 1:
                            v_transpose(11)
                        elif a == 5:
                            v_transpose(27)
                        elif a == 4:
                            rope("qr", U_UQR, 1)

                    for n in range(4):
                        for half in range(2):
                            part(n, half)
                    v_transpose(2)
                    for a in range(N_ATT):
                        if KIND[a] != SB:
                            for qb in range(NB):
                                scores(a, qb, 0)
                                scores(a, qb, 1)
                                fill(a, 2 * qb)
                                norm_work(a, qb)
                                if qb:
                                    probs_transpose(a, qb - 1, 0)
                                fill(a, 2 * qb + 1)
                                if qb:
                                    probs_transpose(a, qb - 1, 1)
                                    pv(a, qb - 1)
                                late_work(a, qb)
                            probs_transpose(a, 3, 0)
                            probs_transpose(a, 3, 1)
                            pv(a, 3)
                        else:
                            for j in range(NB):
                                kb = NB - 1 - j
                                lo = kb * P
                                w = 8 * (a - 2) + 2 * j
                                for m in range(2):
                                    rows = slice(HD * m, HD * m + HD)
                                    if j == 0 and m == 0:
                                        pe.wait_ge(tile_out[q_unit[a] % 2], q_unit[a] // 2 + 1)
                                        pe.wait_ge(tile_out[k_unit[a] % 2], k_unit[a] // 2 + 1)
                                    if w + m >= 2:
                                        pe.wait_ge(sb_prob, w + m - 1)
                                    nc.tensor.matmul(S[m][:, lo:SEQ], ks[a % 2][rows, lo:lo + P], qs[a % 2][rows, lo:SEQ],
                                                     start=True, stop=False)
                                    nc.tensor.matmul(S[m][:, lo:lo + P], ident_r[:, :], sbmask_r[:, :], start=False, stop=True) \
                                      .then_inc(sb_scores, 1)
                                fill(a, 2 * j)
                                norm_work(a, j)
                                for m in range(2):
                                    pe.wait_ge(sb_sp, w + m + 1)
                                    last = nc.tensor.matmul(S[m][:, lo:SEQ], neg_tri, pn[m][:, lo:SEQ], start=False, stop=True,
                                                            skip_group_check=True)
                                    if j:
                                        pe.wait_ge(sb_sum, w + m - 1)
                                        last = nc.tensor.matmul(S[m][:, lo + P:SEQ], neg_ones, sz[m][:, lo + P:SEQ],
                                                                start=False, stop=True, skip_group_check=True)
                                    last.then_inc(sb_cum, 1)
                                fill(a, 2 * j + 1)
                                if j == 0:
                                    v_wait(a)
                                pe.wait_ge(sb_prob, w + 2)
                                for m in range(2):
                                    rows = slice(HD * m, HD * m + HD)
                                    last = nc.tensor.matmul(O[rows, lo:SEQ], vs[a % 2][:, kb, rows], pT[m][:, lo:SEQ],
                                                            start=(j == 0), stop=(j == NB - 1), skip_group_check=True)
                                last.then_inc(pv_done, 1)
                                late_work(a, j)
                        end_work(a)
                    sum_squares("e7", (nrm, rope_b), 5)
                    pe.wait_ge(y_ready, 8)
                    for c in range(2):
                        tok_group(pe, B2_WO + 4 * c, 4, KD, act_hi, act_lo, NB * c)
                    pe.wait_ge(ln_done, NB)
                    transpose_in(pe, x, KD)
                    pe.wait_ge(xt_lo, 2 * KD)
                    for hf in range(2):
                        n0 = B2_FFN + hf * B2_FFN_HALF
                        done = (n0 - 8 - 12 * hf) // 2
                        with pe.Fori(0, FF_HALF) as j:
                            for t in range(2):
                                for half in range(2):
                                    tile_part(pe, j * 2 + (n0 + t), j + done, half, t)
                        pe.wait_ge(gu_ready, FF_HALF * (hf + 1))
                        for c in range(2):
                            tok_group(pe, n0 + 2 * FF_HALF + DOWN_UNITS * c, DOWN_UNITS, FF_HALF, act_hi, act_lo,
                                      NB * (2 + 2 * hf + c))

                @block.scalar
                def _(act):
                    st = Steps(act, act_step)
                    nc.scalar.preload_act_table_set("natural_log_exp_and_others")
                    xt_hi_copy(act, 0)

                    def tile_copy(n):
                        act.wait_ge(unit_done, n + 1)
                        scale = 1.0
                        if n in V_UNITS:
                            name, buf, _ = V_UNITS[n]
                            dst = raw_t[buf]
                            if name in ("v1", "v2", "v3"):
                                act.wait_ge(r_ready, R2[f"v{int(name[1]) - 1}"] + 1)
                            elif name == "v6":
                                act.wait_ge(qk_ready, 1)
                            elif name == "v7":
                                act.wait_ge(qk_ready, 2)
                        elif n in (0, 4, 8, 12):
                            dst, scale = qs[n // 4 % 2], HD ** -0.5
                        elif n in (1, 5, 9, 13):
                            dst = ks[n // 4 % 2]
                        elif n == U_CKV:
                            dst = ckv_t
                        elif n in (U_WQ0, U_WQ1):
                            dst, scale = wq_t[n == U_WQ1], HD ** -0.5
                        elif n == U_WK:
                            dst = wk_t
                        elif n in (U_CQ, U_CQ + 1):
                            dst = cq_t[n - U_CQ]
                        elif n == U_KR:
                            act.wait_ge(latent_ready, 3)
                            dst = raw_t[0]
                        elif n in (U_UQ, U_UQ + 1):
                            dst, scale = qs[n - U_UQ], mla_scale
                        elif n == U_UQR:
                            dst, scale = raw_t[1], mla_scale
                        else:
                            dst = ks[n - U_UKV]
                        nc.scalar.activation(dst[:, :], PT[n % 2][:, :], ACT.Copy, scale=scale).then_inc(tile_out[n % 2], 1)

                    def v_copy(n):
                        name, _, dst = V_UNITS[n]
                        act.wait_ge(r_ready, R2[name] + 1)
                        last_use = {"v2": 4, "v3": 8, "v6": 12, "v7": 16}.get(name)
                        if last_use:
                            act.wait_ge(pv_done, last_use)
                        dst = vw_t if dst is None else dst[:, :, :]
                        nc.scalar.activation(dst, R[:, :].rearrange("p (b c) -> p b c", c=P), ACT.Copy).then_inc(r_out, 1)

                    def rstd(name, dst, width):
                        act.wait_ge(r_ready, R2[name] + 1)
                        nc.scalar.activation(dst[:, :], R[:, :], ACT.Ln, scale=1.0 / width, bias=EPS).then_inc(r_out, 1)
                        act.wait_ge(r_out, R2[name] + 1)
                        nc.scalar.activation(dst[:, :], dst[:, :], ACT.Exp, scale=-0.5).then_inc(rs_ready, 1)

                    def output_copy(a):
                        act.wait_ge(pv_done, 4 * a + 4)
                        if a >= 2:
                            act.wait_ge(y_ready, 2 * (a // 2))
                        nc.scalar.activation(ext[a % 2][:, :], O[:, :], ACT.Copy).then_inc(o_out, 1)
                        if a % 2:
                            act.wait_ge(o_out, a + 1)
                            st(nc.scalar.activation(nrm[:, :], ext[0][:, :], ACT.Square))
                            st.wait()
                            nc.scalar.activation(rope_b[:, :], ext[1][:, :], ACT.Square).then_inc(sq_ready, 1)

                    def softmax_exp(a, qb, m):
                        u, nk, c = u_of(a, qb, m), (qb + 1) * P - first_key(a, qb), 2 * qb + m
                        act.wait_ge(max_ready, u + 1)
                        if u >= 2:
                            act.wait_ge(probs_normed, u // 2)
                        if KIND[a] == SWA:
                            sink = colp[:, P2_SINK + head_of(a, m):P2_SINK + head_of(a, m) + 1]
                            st(nc.scalar.activation(small[:, 44 + m:45 + m], sink, ACT.Exp, bias=small[:, 24 + c:25 + c]))
                        nc.scalar.activation(prob[m][:, 0:nk], S[m][:, 0:nk], ACT.Exp, bias=small[:, 24 + c:25 + c],
                                             accum_out=small[:, 32 + c:33 + c]).then_inc(probs_ready, 1)

                    def pT_copy(a, qb):
                        nk = (qb + 1) * P - first_key(a, qb)
                        for m in range(2):
                            act.wait_ge(t_ready, u_of(a, qb, m) + 1)
                            if 4 * a + qb:
                                act.wait_ge(pv_done, 4 * a + qb)
                            nc.scalar.activation(pT[m][:, 0:nk], T[m][:, 0:nk], ACT.Copy).then_inc(t_out, 1)

                    act.wait_ge(params_loaded, 16)
                    for n in range(3):
                        tile_copy(n)
                    v_copy(2)
                    act.wait_ge(tile_out[1], 2)
                    st.wait(st(nc.scalar.activation(rope_a[0:4, :], nrm[0:4, :], ACT.Abs)))
                    st.wait(st(nc.scalar.activation(rope_a[0:4, :], rope_a[0:4, :], ACT.Exp, scale=-1.0)))
                    nc.scalar.activation(rope_a[0:4, :], rope_a[0:4, :], ACT.Ln, bias=1.0).then_inc(gate_ln, 1)
                    for a in range(N_ATT):
                        for qb in range(NB):
                            if qb == 0:
                                if 0 < a < 7 and 4 * a + 3 < B2_WO:
                                    tile_copy(4 * a + 3)
                                if a == 2:
                                    v_copy(11)
                                elif a == 6:
                                    v_copy(27)
                                if a:
                                    output_copy(a - 1)
                                if a == 4:
                                    st(nc.scalar.activation(z_t[:, :], ckv_t[:, :], ACT.Square))
                                    act.wait_ge(tile_out[1], (U_CQ + 1) // 2 + 1)
                                    st(nc.scalar.activation(raw_t[0][:, :], cq_t[0][:, :], ACT.Square))
                                    st.wait()
                                    nc.scalar.activation(raw_t[1][:, :], cq_t[1][:, :], ACT.Square).then_inc(sq_ready, 1)
                            elif a + 1 < 7:
                                tile_copy(4 * (a + 1) + qb - 1)
                            if KIND[a] == SB:
                                lo, w = (NB - 1 - qb) * P, 8 * (a - 2) + 2 * qb
                                for m in range(2):
                                    e = prob[m][:, lo:SEQ]
                                    act.wait_ge(sb_scores, w + m + 1)
                                    if w + m >= 2:
                                        act.wait_ge(sb_sp, w + m - 1)
                                    st.wait(st(nc.scalar.activation(e, S[m][:, lo:SEQ], ACT.Abs)))
                                    st.wait(st(nc.scalar.activation(e, e, ACT.Exp, scale=-1.0)))
                                    nc.scalar.activation(e, e, ACT.Ln, bias=1.0).then_inc(sb_ln, 1)
                            else:
                                softmax_exp(a, qb, 0)
                                softmax_exp(a, qb, 1)
                            if qb == 0 and a in (2, 4, 6):
                                rstd(f"e{a - 1}", nrm, 4 * HD)
                            if qb == 0 and a == 4:
                                rstd("ckv", z_t, P)
                                rstd("cq", raw_t[0], 2 * P)
                            if KIND[a] == SB:
                                for m in range(2):
                                    act.wait_ge(sb_cum, w + m + 1)
                                    if 4 * a + qb:
                                        act.wait_ge(pv_done, 4 * a + qb)
                                    nc.scalar.activation(pT[m][:, lo:SEQ], S[m][:, lo:SEQ], ACT.Exp).then_inc(sb_prob, 1)
                            elif qb:
                                pT_copy(a, qb - 1)
                        if a in (0, 1, 2, 5):
                            v_copy(4 * (a + 1) + 2)
                        if KIND[a] != SB:
                            pT_copy(a, 3)
                    output_copy(7)
                    act.dma_start(rowp[:, :], rows2[0, :, :]).then_inc(rows_loaded, 16)
                    rstd("e7", nrm, 4 * HD)

                    def ln_stats(count):
                        for tb in range(NB):
                            act.wait_ge(ln_centre, count + tb + 1)
                            last = st(nc.scalar.activation(hn[:, tb, :], x[:, tb, :], ACT.Square,
                                                           accum_out=small[:, 16 + tb:17 + tb]))
                        st.wait(last)
                        st.wait(st(nc.scalar.activation(small[:, 20:24], small[:, 16:20], ACT.Ln, scale=1.0 / D, bias=LN_EPS)))
                        nc.scalar.activation(small[:, 20:24], small[:, 20:24], ACT.Exp, scale=-0.5).then_inc(stat_ready, 1)

                    ln_stats(0)
                    xt_hi_copy(act, KD)
                    act.wait_ge(ln_done, NB)
                    act.dma_start(rowp[:, :], rows2[1, :, :]).then_inc(rows_loaded, 16)
                    for hf in range(2):
                        n0 = B2_FFN + hf * B2_FFN_HALF
                        done = (n0 - 8 - 12 * hf) // 2
                        with act.Fori(0, FF_HALF) as j:
                            act.wait_ge(unit_done, j * 2 + (n0 + 1))
                            act.wait_ge(tile_out[1], j + done)
                            nc.scalar.activation(nrm[:, :], PT[0][:, :], ACT.Silu).then_inc(tile_out[0], 1)
                    ln_stats(NB)

                @block.vector
                def _(dve):
                    st = Steps(dve, dve_step)
                    xt_lo_sub(dve, 0)
                    dve.wait_ge(params_loaded, 16)
                    dve.wait_ge(unit_done, U_GATE + 1)
                    nc.vector.tensor_scalar(nrm[0:4, :], PT[1][0:4, :], colp[0:4, P2_BF:P2_BF + 1], -1.0, ALU.add, ALU.mult) \
                      .then_inc(tile_out[1], 1)
                    dve.wait_ge(gate_ln, 1)
                    st.wait(st(nc.vector.scalar_tensor_tensor(out=nrm[0:4, :], in0=nrm[0:4, :], scalar=0.0, in1=rope_a[0:4, :],
                                                              op0=ALU.max, op1=ALU.add)))
                    nc.vector.tensor_tensor_scan(ext[2][0:4, :], nrm[0:4, :], nrm[0:4, :], 0.0, ALU.add, ALU.bypass) \
                      .then_inc(gate_ready, 1)
                    for h in range(4):
                        st(nc.vector.tensor_scalar(small[:, 48 + h:49 + h], colp[:, P2_SINK + h:P2_SINK + h + 1], -1.0, None, ALU.mult))
                    st.wait()

                    def row_max(a, qb, m):
                        u, c = u_of(a, qb, m), 2 * qb + m
                        nm = small[:, 24 + c:25 + c]
                        dve.wait_ge(scores_ready, u + 1)
                        top_ = nc.vector.tensor_reduce(nm, S[m][:, 0:(qb + 1) * P - first_key(a, qb)], AX.X, ALU.max, negate=True)
                        if KIND[a] != SWA:
                            top_.then_inc(max_ready, 1)
                            return
                        st.wait(st(top_))
                        h = head_of(a, m)
                        nc.vector.tensor_tensor(nm, nm, small[:, 48 + h:49 + h], ALU.min).then_inc(max_ready, 1)

                    def normalise(a, qb):
                        u, nk = u_of(a, qb, 0), (qb + 1) * P - first_key(a, qb)
                        l, r = small[:, 32 + 2 * qb:34 + 2 * qb], small[:, 40:42]
                        dve.wait_ge(probs_ready, u + 2)
                        if KIND[a] == SWA:
                            st.wait(st(nc.vector.tensor_tensor(l, l, small[:, 44:46], ALU.add)))
                        st.wait(st(nc.vector.reciprocal(r, l)))
                        if u:
                            dve.wait_ge(t_ready, u)
                        st.wait(st(nc.vector.tensor_scalar(pn[0][:, 0:nk], prob[0][:, 0:nk], small[:, 40:41], None, ALU.mult)))
                        nc.vector.tensor_scalar(pn[1][:, 0:nk], prob[1][:, 0:nk], small[:, 41:42], None, ALU.mult) \
                          .then_inc(probs_normed, 1)

                    def rotate(name, buf, dst, count):
                        dve.wait_ge(r_ready, R2[name] + 1)
                        st(nc.vector.tensor_tensor(rope_a[:, :], raw_t[buf][:, :], cos[:, :], ALU.mult))
                        nc.vector.tensor_tensor(rope_b[:, :], R[:, :], sin[:, :], ALU.mult).then_inc(r_out, 1)
                        st.wait()
                        dve.wait_ge(r_out, R2[name] + 1)
                        nc.vector.tensor_tensor(dst[:, :], rope_a[:, :], rope_b[:, :], ALU.add).then_inc(qk_ready, 1)

                    def scaled_split(src, gain, rs, i, ready, count):
                        st.wait(st(nc.vector.scalar_tensor_tensor(out=ytmp[:, :], in0=src[:, :], scalar=gain, in1=rs[:, :],
                                                                  op0=ALU.mult, op1=ALU.mult)))
                        st.wait(st(nc.vector.tensor_copy(act_hi[:, i, :], ytmp[:, :])))
                        nc.vector.tensor_tensor(act_lo[:, i, :], ytmp[:, :], act_hi[:, i, :].bitcast(F32), ALU.subtract) \
                          .then_inc(ready, 1)
                        dve.wait_ge(ready, count)

                    def group_norm(a, count):
                        dve.wait_ge(rs_ready, count)
                        for i in range(2):
                            t = a - 1 + i
                            scaled_split(ext[i], colp[:, P2_MIX + t:P2_MIX + t + 1], nrm, t, y_ready, t + 1)

                    for a in range(N_ATT):
                        for qb in range(NB):
                            if KIND[a] == SB:
                                lo, w = (NB - 1 - qb) * P, 8 * (a - 2) + 2 * qb
                                if qb == 0:
                                    if w:
                                        dve.wait_ge(sb_sum, w)
                                    for m in range(2):
                                        st(nc.vector.memset(sz[m][:, :], 0.0))
                                    st.wait()
                                for m in range(2):
                                    dve.wait_ge(sb_ln, w + m + 1)
                                    if w + m >= 2:
                                        dve.wait_ge(sb_sum, w + m - 1)
                                    nc.vector.scalar_tensor_tensor(out=pn[m][:, lo:SEQ], in0=S[m][:, lo:SEQ], scalar=0.0,
                                                                   in1=prob[m][:, lo:SEQ], op0=ALU.max, op1=ALU.add) \
                                      .then_inc(sb_sp, 1)
                                for m in range(2):
                                    dve.wait_ge(sb_cum, w + m + 1)
                                    nc.vector.tensor_tensor(sz[m][:, lo:SEQ], sz[m][:, lo:SEQ], pn[m][:, lo:SEQ], ALU.add) \
                                      .then_inc(sb_sum, 1)
                            else:
                                row_max(a, qb, 0)
                                row_max(a, qb, 1)
                                normalise(a, qb)
                            if qb == 0 and a in (2, 4, 6):
                                group_norm(a - 1, {2: 1, 4: 2, 6: 5}[a])
                            if a == 4 and qb == 0:
                                dve.wait_ge(rs_ready, 3)
                                scaled_split(ckv_t, colp[:, P2_GKV:P2_GKV + 1], z_t, 10, latent_ready, 1)
                                dve.wait_ge(rs_ready, 4)
                                for i in range(2):
                                    scaled_split(cq_t[i], colp[:, P2_GQ + i:P2_GQ + i + 1], raw_t[0], 8 + i, latent_ready, 2 + i)
                            if a == 4 and qb == 2:
                                rotate("kr", 0, z_t, 1)
                        if a == 4:
                            rotate("qr", 1, qr_t, 2)
                    group_norm(7, 6)

                    def to_residual(g, n_end, scale, sums):
                        c = g % 2
                        cols = slice(c * SEQ, (c + 1) * SEQ)
                        dve.wait_ge(unit_done, n_end)
                        for tb in range(NB):
                            acc = dict(accum_out=small[:, 2 * tb + c:2 * tb + c + 1]) if sums else {}
                            nc.vector.scalar_tensor_tensor(out=x[:, tb, cols], in0=x[:, tb, cols], scalar=scale,
                                                           in1=TOK[tb][:, :], op0=ALU.mult, op1=ALU.add, **acc) \
                              .then_inc(tok_out, 1)
                        dve.wait_ge(tok_out, NB * (g + 1))

                    def layernorm(count):
                        sums = small[:, 0:2 * NB].rearrange("p (b c) -> p b c", c=2)
                        st.wait(st(nc.vector.tensor_reduce(small[:, 52:56], sums, AX.X, ALU.add)))
                        st.wait(st(nc.vector.tensor_scalar(small[:, 52:56], small[:, 52:56], -1.0 / D, None, ALU.mult)))
                        for tb in range(NB):
                            nc.vector.tensor_scalar(x[:, tb, :], x[:, tb, :], small[:, 52 + tb:53 + tb], None, ALU.add) \
                              .then_inc(ln_centre, 1)
                        dve.wait_ge(stat_ready, count)
                        dve.wait_ge(rows_loaded, 16 * count)
                        for tb in range(NB):
                            st.wait(st(nc.vector.scalar_tensor_tensor(out=x[:, tb, :], in0=x[:, tb, :],
                                                                      scalar=small[:, 20 + tb:21 + tb], in1=rowp[:, 0:D],
                                                                      op0=ALU.mult, op1=ALU.mult)))
                            nc.vector.tensor_tensor(x[:, tb, :], x[:, tb, :], rowp[:, D:2 * D], ALU.add).then_inc(ln_done, 1)

                    for c in range(2):
                        to_residual(c, B2_WO + 4 * c + 4, ALPHA, True)
                    layernorm(1)
                    dve.wait_ge(ln_done, NB)
                    xt_lo_sub(dve, KD)
                    for hf in range(2):
                        n0 = B2_FFN + hf * B2_FFN_HALF
                        done = (n0 - 8 - 12 * hf) // 2
                        dve.wait_ge(unit_done, n0)
                        first = st.n + 1
                        with dve.Fori(0, FF_HALF) as j:
                            dve.wait_ge(tile_out[0], j + (done + 1))
                            dve.wait_ge(unit_done, j * 2 + (n0 + 2))
                            nc.vector.tensor_tensor(ytmp[:, :], nrm[:, :], PT[1][:, :], ALU.mult).then_inc(tile_out[1], 1)
                            dve.wait_ge(tile_out[1], j + (done + 1))
                            hi = act_hi[:, bass.ds(j, 1), :].rearrange("p a t -> p (a t)")
                            lo = act_lo[:, bass.ds(j, 1), :].rearrange("p a t -> p (a t)")
                            nc.vector.tensor_copy(hi, ytmp[:, :]).then_inc(dve_step, 1)
                            dve.wait_ge(dve_step, j + first)
                            nc.vector.tensor_tensor(lo, ytmp[:, :], hi.bitcast(F32), ALU.subtract).then_inc(gu_ready, 1)
                            dve.wait_ge(gu_ready, j + (FF_HALF * hf + 1))
                        st.n += FF_HALF
                        for c in range(2):
                            to_residual(2 + 2 * hf + c, n0 + 2 * FF_HALF + DOWN_UNITS * (c + 1), 1.0 if hf else ALPHA, hf == 1)
                    layernorm(2)
            end_of_stage()

        with nc.Block() as block:
            @block.sync
            def _(sp):
                sp.dma_start(out.rearrange("(b p) d -> p b d", p=P), x[:, :, :]).then_inc(stored, 16)
                sp.wait_ge(stored, 16)


def _t_unit(np, w):
    k = w.shape[0] // P
    u = np.zeros((P, UNIT), w.dtype)
    u[:, :k * P] = w.reshape(k, P, P).transpose(1, 0, 2).reshape(P, k * P)
    return u


def _tok_units(np, w):
    k = w.shape[0] // P
    out = []
    for j in range(0, k, 2):
        u = np.zeros((P, UNIT), w.dtype)
        for i in range(j, min(j + 2, k)):
            u[:, (i - j) * SEQ:(i - j + 1) * SEQ] = w[i * P:(i + 1) * P]
        out.append(u)
    return out


def _block1_units(np, w_in, w_branch, w_out):
    cols = lambda c, n=P: w_in[:, c:c + n]
    units = _tok_units(np, cols(2560, SEQ))
    for g in range(4):
        units += [_t_unit(np, cols(2048 + P * g)), _t_unit(np, cols(3072 + P * g))]
    for base in (0, 3584):
        for h in range(4):
            units += [_t_unit(np, cols(base + SEQ * j + P * h)) for j in range(4)]
    for m in range(KD):
        for i in range(3):
            units += [_t_unit(np, cols(5632 + D * i + P * m)), _t_unit(np, w_branch[i][:, P * m:P * m + P])]
    for c in range(2):
        units += _tok_units(np, w_out[:, SEQ * c:SEQ * (c + 1)])
    return np.stack(units)


def _block2_units(np, w_in, w_uq, w_ukv, w_o, w_gate, w_up, w_down):
    cols = lambda c, n=P: w_in[:, c:c + n]
    cat = lambda *a: np.concatenate(a, axis=1)
    gates = cat(cols(768, 4), np.zeros((D, P - 4), w_in.dtype))
    kr = cat(*[cols(1156, 32)] * 4)
    wq = [cat(cols(1956 + HD * i, HD), cols(1956 + HD * (i + 2), HD)) for i in range(2)]
    order = [cols(0), cols(256), cols(512), gates,
             cols(128), cols(384), cols(640), cols(1028),
             cols(1188), cols(1444), cols(1700), cols(2340),
             cols(1316), cols(1572), cols(1828), wq[0],
             cols(2212), wq[1], cols(772), cols(900), kr]
    q3 = w_uq.reshape(2 * P, 4, HD + 32)
    order += [q3[:, 0:2, :HD].reshape(2 * P, P), q3[:, 2:4, :HD].reshape(2 * P, P), q3[:, :, HD:].reshape(2 * P, P)]
    kv = w_ukv.reshape(P, 4, 2 * HD)
    order += [kv[:, 0:2, :HD].reshape(P, P), kv[:, 2:4, :HD].reshape(P, P),
              kv[:, 0:2, HD:].reshape(P, P), kv[:, 2:4, HD:].reshape(P, P)]
    units = [_t_unit(np, w) for w in order]
    w_o = _mix_order(np, w_o)
    for c in range(2):
        units += _tok_units(np, w_o[:, SEQ * c:SEQ * (c + 1)])
    for hf in range(2):
        for j in range(FF_HALF * hf, FF_HALF * (hf + 1)):
            units += [_t_unit(np, w_gate[:, P * j:P * j + P]), _t_unit(np, w_up[:, P * j:P * j + P])]
        rows = w_down[hf * FF_HALF * P:(hf + 1) * FF_HALF * P]
        for c in range(2):
            units += _tok_units(np, rows[:, SEQ * c:SEQ * (c + 1)])
    return np.stack(units)


def _mix_order(np, a):
    heads = a.reshape(16, HD, *a.shape[1:])
    return heads[[0, 1, 2, 3, 8, 9, 10, 11, 12, 14, 13, 15, 4, 5, 6, 7]].reshape(a.shape)


def _constants(np):
    f = np.float32
    c = np.zeros((P, C_KEEP), f)
    r = np.arange(P)
    c[:, C_IDENT:C_IDENT + P] = np.eye(P)
    c[:, C_ONES:C_ONES + P] = 1
    c[:, C_NTRI:C_NTRI + P] = -(r[:, None] >= r[None, :]).astype(f)
    c[:, C_NONES:C_NONES + P] = -1
    for at, width, half in ((C_ROPE1, HD, HD // 8), (C_ROPE2, 32, 16)):
        for p in range(P):
            d = p % width
            if d < half:
                c[p + half, at + p] = -1
            elif d < 2 * half:
                c[p - half, at + p] = 1
    c[:, C_UPPER:C_UPPER + P] = r[:, None] <= r[None, :]
    for h in range(4):
        c[h, C_SEL + P * h:C_SEL + P * (h + 1)] = 1
    inv = np.power(f(500000.0), -np.arange(8, dtype=f) * f(2.0) / f(16)).astype(f)
    for p in range(P):
        if p % HD < 16:
            c[p, C_INV] = inv[p % 8]
    m = np.zeros((P, M_WIDTH), f)
    m[:, M_CAUSAL:M_CAUSAL + P] = np.where(r[None, :] <= r[:, None], 0, NEG)
    m[:, M_STRICT:M_STRICT + P] = np.where(r[:, None] < r[None, :], 0, NEG)
    rel = r[:, None] - (np.arange(SEQ)[None, :] - (SEQ - P))
    count = (rel <= 128).astype(int) + (rel % 4 == 0) + (rel % 16 == 0)
    m[:, M_MULT:M_MULT + SEQ] = np.where((rel >= 0) & (count > 0), np.log(np.maximum(count, 1)), NEG)
    dist = r[:, None] + P - np.arange(2 * P)[None, :]
    for h in range(4):
        slope = 2.0 ** (-8.0 * (h + 1) / 4)
        m[:, M_SWA + 2 * P * h:M_SWA + 2 * P * (h + 1)] = np.where((dist >= 0) & (dist < 128), -slope * dist, NEG)
    inv2 = f(10000.0) ** (-np.arange(0, 32, 2, dtype=f) / f(32))
    ang = np.arange(SEQ, dtype=f)[None, :] * inv2[r % 16][:, None]
    rope2 = np.stack([np.cos(ang), np.sin(ang)]).astype(f)
    return c, m, rope2


def kernel(**inputs):
    import numpy as np
    import concourse.bacc as bacc
    from concourse.bass_utils import run_bass_kernel_spmd

    a = {k: np.asarray(v) for k, v in inputs.items()}
    f = a["x"].dtype
    c, m, rope2 = _constants(np)
    w1 = np.stack([_block1_units(np, a["w_in"][l], a["w_branch"][l], a["w_out"][l]) for l in range(DEPTH)])
    w2 = np.stack([_block2_units(np, a["w_in_2"][l], a["mla_w_uq_2"][l], a["mla_w_ukv_2"][l], a["w_o_2"][l],
                                 a["w_gate_2"][l], a["w_up_2"][l], a["w_down_2"][l]) for l in range(DEPTH)])
    rows = lambda v: np.broadcast_to(v.reshape(1, -1), (P, v.size))
    col1, row1, col2, row2 = [], [], [], []
    for l in range(DEPTH):
        lam_init = 0.8 - 0.6 * math.exp(-0.3 * l)
        col1.append(np.concatenate([
            a["norm_g"][l].reshape(KD, P).T, a["subln_g"][l].reshape(P, 1),
            rows(a["lam_q1"][l]), rows(a["lam_k1"][l]), rows(a["lam_q2"][l]), rows(a["lam_k2"][l]),
            np.full((P, 1), lam_init, f), np.full((P, 1), 1.0 - lam_init, f)], axis=1))
        row1.append(np.concatenate([
            rows(a["sgu_ln_g"][l]), rows(a["sgu_ln_b"][l]), rows(a["sgu_b"][l]),
            a["sgu_w"][l].transpose(2, 0, 1).reshape(P, SEQ)], axis=1))
        fox_b = np.zeros((P, 1), f)
        fox_b[:4, 0] = a["fox_b_f_2"][l]
        mix_g = _mix_order(np, a["mix_g_2"][l])
        col2.append(np.concatenate([
            a["mla_g_q_2"][l].reshape(2, P).T, a["mla_g_kv_2"][l].reshape(P, 1), mix_g.reshape(KD, P).T,
            fox_b, rows(a["swa_sinks_2"][l])], axis=1))
        row2.append(np.stack([np.concatenate([rows(a[g][l]), rows(a[b][l])], axis=1)
                              for g, b in (("ln1_g_2", "ln1_b_2"), ("ln2_g_2", "ln2_b_2"))]))
    arrays = {
        "x_dram": a["x"].reshape(SEQ, D), "pos_dram": a["positions"].reshape(1, SEQ), "const_dram": c, "mask_dram": m,
        "rope2_dram": rope2, "w1_dram": w1, "col1_dram": np.stack(col1), "row1_dram": np.stack(row1),
        "final_dram": a["final_g"].reshape(1, D), "w2_dram": w2, "col2_dram": np.stack(col2), "row2_dram": np.stack(row2),
    }
    arrays = {k: np.ascontiguousarray(v) for k, v in arrays.items()}
    nc = bacc.Bacc("TRN2", target_bir_lowering=False, num_devices=1)
    aps = [nc.dram_tensor(k, v.shape, mybir.dt.from_np(v.dtype), kind="ExternalInput").ap() for k, v in arrays.items()]
    out = nc.dram_tensor("out_dram", (SEQ, D), F32, kind="ExternalOutput").ap()
    program(nc, *aps, out)
    r = run_bass_kernel_spmd(nc, [arrays], core_ids=[0])
    return r.results[0]["out_dram"].reshape(1, SEQ, D)
```

```python
import math
from contextlib import ExitStack

import concourse.bass as bass
from concourse import mybir

F32 = mybir.dt.float32
F32R = mybir.dt.float32r
I32 = mybir.dt.int32
ALU = mybir.AluOpType
ACT = mybir.ActivationFunctionType
AX = mybir.AxisListType

DEPTH = 2
SEQ = 512
D = 1024
P = 128
NB = SEQ // P
KD = D // P
UNIT = 1024
RAW = 4
EPS = 1e-6
LN_EPS = 1e-5
ALPHA = (2.0 * DEPTH) ** 0.25
NEG = -(2.0 ** 100)
HD = 64

B1_V = 0
B1_UZ = 4
B1_HEADS = 12
B1_GATE = 44
GATE_TURN = 4
B1_OUT = 80
B1_UNITS = 88
N_ATT = 8
N_A = 4

B2_PACKED = (("wq0",), ("wk",), ("wv",), ("ckv",), ("cq0",), ("cq1",), ("wq1",), ("kr",), ("gates",), ("uq0", "uqr"),
             ("uk0", "uv0"), ("sq1",), ("sk1",), ("uq1", "uk1", "uv1"), ("sq0",), ("sk0",), ("sv0",), ("fq0",), ("fk0",),
             ("sv1",), ("fq1",), ("fk1",), ("fv0",), ("fv1",))
B2_TILES = tuple(name for unit in B2_PACKED for name in unit)
B2_KT = {"uq0": 2, "uq1": 2, "uqr": 2, "uk0": 1, "uk1": 1, "uv0": 1, "uv1": 1}
B2_WO = len(B2_PACKED)
FF_TILES = 22
FF_HALF = FF_TILES // 2
DOWN_UNITS = (FF_HALF + 1) // 2
B2_FFN = B2_WO + 8
B2_FFN_HALF = 2 * FF_HALF + 2 * DOWN_UNITS
B2_UNITS = B2_FFN + 2 * B2_FFN_HALF

C_IDENT, C_ONES, C_NTRI, C_NONES, C_ROPE1, C_ROPE2, C_UPPER = (P * i for i in range(7))
C_SEL = 7 * P
C_INV = C_SEL + 4 * P
C_KEEP = C_INV + 1
M_CAUSAL, M_STRICT = 0, P
M_MULT = 2 * P
M_SWA = M_MULT + SEQ
M_WIDTH = M_SWA + 8 * P

P1_NORM, P1_SUBLN, P1_LAM, P1_INIT, P1_KEEP = 0, 8, 9, 9 + 4 * HD, 10 + 4 * HD
P1_COLS = 11 + 4 * HD
P2_GQ, P2_GKV, P2_MIX, P2_BF, P2_SINK = 0, 2, 3, 11, 12
P2_COLS = 16
ROWP = 2048


class Steps:

    def __init__(self, eng, sem):
        self.eng, self.sem, self.n = eng, sem, 0

    def __call__(self, ins):
        ins.then_inc(self.sem, 1)
        self.n += 1
        return self.n

    def wait(self, value=None):
        self.eng.wait_ge(self.sem, self.n if value is None else value)


def program(nc, x_in, pos_in, const_in, mask_in, rope2_in, w1_in, col1_in, row1_in, final_in,
            w2_in, col2_in, row2_in, out):
    ctx = ExitStack()
    with ctx:
        base = nc.sbuf_base
        top = [(base + 31) // 32 * 32]
        addr = {}

        def sb(name, shape, dt=F32, at=None):
            size = 4
            for s in shape[1:]:
                size *= s
            offset = top[0] if at is None else at
            addr[name] = offset
            if at is None:
                top[0] += (size + 31) // 32 * 32
            return nc.alloc_sbuf_tensor_at(name, shape, dt, offset=offset)

        def sem(name):
            return ctx.enter_context(nc.semaphore(name))

        x = sb("x", [P, NB, D])
        h_hi = sb("h_hi", [P, KD, SEQ], F32R)
        h_lo = sb("h_lo", [P, KD, SEQ], F32R)
        raw_w = [sb(f"raw_w{s}", [P, UNIT]) for s in range(RAW)]
        w_hi = [sb(f"w_hi{s}", [P, UNIT], F32R) for s in range(2)]
        w_lo = [sb(f"w_lo{s}", [P, UNIT], F32R) for s in range(2)]
        act_hi = sb("act_hi", [P, 12, SEQ], F32R)
        act_lo = sb("act_lo", [P, 12, SEQ], F32R)
        const = sb("const", [P, C_KEEP])
        ident_r = sb("ident_r", [P, P], F32R)
        causal_r = sb("causal_r", [P, P], F32R)
        sbmask_r = sb("sbmask_r", [P, P], F32R)
        m2_hi = sb("m2_hi", [P, SEQ], F32R)
        m2_lo = sb("m2_lo", [P, SEQ], F32R)
        swa_r = sb("swa_r", [P, 4, 2 * P], F32R)
        cos = sb("cos", [P, SEQ])
        sin = sb("sin", [P, SEQ])
        rowp = sb("rowp", [P, ROWP])
        colp = sb("colp", [P, max(P1_COLS, P2_COLS)])
        small = sb("small", [P, 64])
        ext = [sb(f"ext{i}", [P, SEQ]) for i in range(4)]
        shared = top[0]
        qs = [sb(f"qs{i}", [P, SEQ]) for i in range(2)]
        ks = [sb(f"ks{i}", [P, SEQ]) for i in range(2)]
        vs = [sb(f"vs{i}", [P, NB, P]) for i in range(2)]
        raw_t = [sb(f"raw_t{i}", [P, SEQ]) for i in range(2)]
        prob = [sb(f"prob{i}", [P, SEQ]) for i in range(2)]
        pn = [sb(f"pn{i}", [P, SEQ]) for i in range(2)]
        pT = [sb(f"pT{i}", [P, SEQ]) for i in range(2)]
        sz = [sb(f"sz{i}", [P, SEQ]) for i in range(2)]
        z_t = sb("z_t", [P, SEQ])
        nrm = sb("nrm", [P, SEQ])
        rope_a = sb("rope_a", [P, SEQ])
        rope_b = sb("rope_b", [P, SEQ])
        ytmp = sb("ytmp", [P, SEQ])
        masks = sb("masks", [P, M_WIDTH], at=shared)
        hn = sb("hn", [P, NB, D], at=shared)
        mrg_hi = sb("mrg_hi", [P, KD, SEQ], F32R, at=shared)
        mrg_lo = sb("mrg_lo", [P, KD, SEQ], F32R, at=shared + KD * SEQ * 4)
        rowp_at, m2_at = addr["rowp"], addr["m2_hi"]
        wq_t = [sb(f"wq_t{i}", [P, SEQ], at=rowp_at + 4 * SEQ * i) for i in range(2)]
        wk_t = sb("wk_t", [P, SEQ], at=rowp_at + 8 * SEQ)
        ckv_t = sb("ckv_t", [P, SEQ], at=rowp_at + 12 * SEQ)
        cq_t = [sb(f"cq_t{i}", [P, SEQ], at=m2_at + 4 * SEQ * i) for i in range(2)]
        qr_t = sb("qr_t", [P, SEQ], at=addr["act_hi"] + 11 * 4 * SEQ)

        ps = [ctx.enter_context(nc.psum_tensor(f"bank{i}", [P, SEQ], F32)) for i in range(8)]
        PT, S, T, R, O = ps[0:2], ps[2:4], ps[4:6], ps[6], ps[7]
        TOK = ps[2:6]

        ident = const[:, C_IDENT:C_IDENT + P]
        ones = const[:, C_ONES:C_ONES + P]
        neg_tri = const[:, C_NTRI:C_NTRI + P]
        neg_ones = const[:, C_NONES:C_NONES + P]
        rope1 = const[:, C_ROPE1:C_ROPE1 + P]
        rope2 = const[:, C_ROPE2:C_ROPE2 + P]

        raw_loaded = [sem(f"raw_loaded{s}") for s in range(RAW)]
        params_loaded = sem("params_loaded")
        rows_loaded = sem("rows_loaded")
        hi_split = sem("hi_split")
        split_done = sem("split_done")
        small_done = sem("small_done")
        unit_done = sem("unit_done")
        tile_out = [sem(f"tile_out{b}") for b in range(2)]
        tok_out = sem("tok_out")
        norm_in = sem("norm_in")
        xt_ready = sem("xt_ready")
        xt_hi = sem("xt_hi")
        xt_lo = sem("xt_lo")
        r_ready = sem("r_ready")
        r_out = sem("r_out")
        qk_ready = sem("qk_ready")
        scores_ready = sem("scores_ready")
        max_ready = sem("max_ready")
        probs_ready = sem("probs_ready")
        probs_normed = sem("probs_normed")
        t_ready = sem("t_ready")
        t_out = sem("t_out")
        pv_done = sem("pv_done")
        o_out = sem("o_out")
        sq_ready = sem("sq_ready")
        rs_ready = sem("rs_ready")
        z_ready = sem("z_ready")
        v_ready = sem("v_ready")
        vb_ready = sem("vb_ready")
        y_ready = sem("y_ready")
        merged = sem("merged")
        stat_ready = sem("stat_ready")
        lam_exp = sem("lam_exp")
        gate_ready = sem("gate_ready")
        latent_ready = sem("latent_ready")
        sb_scores = sem("sb_scores")
        sb_ln = sem("sb_ln")
        sb_sp = sem("sb_sp")
        sb_cum = sem("sb_cum")
        sb_sum = sem("sb_sum")
        sb_prob = sem("sb_prob")
        ln_done = sem("ln_done")
        ln_centre = sem("ln_centre")
        gate_ln = sem("gate_ln")
        gu_ready = sem("gu_ready")
        dve_step = sem("dve_step")
        act_step = sem("act_step")
        stored = sem("stored")
        sems = range(raw_loaded[0].num, stored.num + 1)
        engines = [e.engine for e in (nc.sync, nc.gpsimd, nc.scalar, nc.vector, nc.tensor)]

        def end_of_stage():
            nc.multi_engine_barrier(engines, sems_to_clear=sems)

        def load_units(sp, w_layer, units):
            def one(n, s, i):
                if not (isinstance(i, int) and i == 0):
                    sp.wait_ge(split_done, n - (RAW - 1))
                sp.dma_start(raw_w[s][:, :], w_layer[bass.ds(n, 1), :, :].rearrange("a p c -> p (a c)")) \
                  .then_inc(raw_loaded[s], 16)
            for s in range(RAW):
                one(s, s, 0)
            with sp.Fori(1, units // RAW) as i:
                for s in range(RAW):
                    one(i * RAW + s, s, i)

        def split_units(pool, units):
            def one(n, s, i):
                pool.wait_ge(raw_loaded[s], (i + 1) * 16)
                if not (isinstance(n, int) and n < 2):
                    pool.wait_ge(unit_done, n - 1)
                nc.gpsimd.tensor_tensor(w_hi[s % 2][:, :], raw_w[s][:, :], ones[:, 0:1].to_broadcast([P, UNIT]), ALU.mult) \
                  .then_inc(hi_split, 1)
                pool.wait_ge(hi_split, n + 1)
                nc.gpsimd.tensor_tensor(w_lo[s % 2][:, :], raw_w[s][:, :], w_hi[s % 2][:, :].bitcast(F32),
                                        ALU.subtract).then_inc(split_done, 1)
            for s in range(RAW):
                one(s, s, 0)
            with pool.Fori(1, units // RAW) as i:
                for s in range(RAW):
                    one(i * RAW + s, s, i)

        def mm3(dst, lh, ll, rh, rl, start, stop):
            nc.tensor.matmul(dst, lh, rh, start=start, stop=False)
            nc.tensor.matmul(dst, ll, rh, start=False, stop=False)
            return nc.tensor.matmul(dst, lh, rl, start=False, stop=stop)

        def tile_part(pe, n, before, half, slot, kt=KD, mov=None, bank=None, at=0, done=unit_done):
            m_hi, m_lo = mov if mov else (h_hi, h_lo)
            b = slot if bank is None else bank
            if half == 0:
                pe.wait_ge(split_done, n + 1)
                if not (isinstance(before, int) and before == 0):
                    pe.wait_ge(tile_out[b], before)
            wh = w_hi[slot][:, :].rearrange("p (k c) -> p k c", c=P)
            wl = w_lo[slot][:, :].rearrange("p (k c) -> p k c", c=P)
            cut = (kt + 1) // 2
            for k in (range(cut) if half == 0 else range(cut, kt)):
                last = mm3(PT[b][:, :], wh[:, at + k, :], wl[:, at + k, :], m_hi[:, k, :], m_lo[:, k, :],
                           k == 0, k == kt - 1)
            if half == 1 or kt == 1:
                last.then_inc(done, 1)

        def tok_unit(pe, n0, j, kts, st_hi, st_lo, before):
            pe.wait_ge(split_done, n0 + j + 1)
            s = (n0 + j) % 2
            wh = w_hi[s][:, :].rearrange("p (k c) -> p k c", c=SEQ)
            wl = w_lo[s][:, :].rearrange("p (k c) -> p k c", c=SEQ)
            for tb in range(NB):
                if j == 0 and before:
                    pe.wait_ge(tok_out, before - NB + tb + 1)
                cols = slice(tb * P, (tb + 1) * P)
                for k in range(2 * j, min(2 * j + 2, kts)):
                    last = mm3(TOK[tb][:, :], st_hi[:, k, cols], st_lo[:, k, cols],
                               wh[:, k - 2 * j, :], wl[:, k - 2 * j, :], k == 0, k == kts - 1)
            last.then_inc(unit_done, 1)

        def tok_group(pe, n0, units, kts, st_hi, st_lo, before):
            for j in range(units):
                tok_unit(pe, n0, j, kts, st_hi, st_lo, before)

        def transpose_in(pe, src, k0):
            for k in range(KD):
                if k >= 2:
                    pe.wait_ge(xt_lo, k0 + k - 1)
                for tb in range(NB):
                    last = nc.tensor.transpose(S[k % 2][:, tb * P:(tb + 1) * P],
                                               src[:, tb, k * P:(k + 1) * P], ident)
                last.then_inc(xt_ready, 1)

        def xt_hi_copy(act, k0, gain=None):
            for k in range(KD):
                act.wait_ge(xt_ready, k0 + k + 1)
                nc.scalar.activation(h_hi[:, k, :], S[k % 2][:, :], ACT.Copy,
                                     scale=1.0 if gain is None else gain[:, k:k + 1]).then_inc(xt_hi, 1)

        def xt_lo_sub(dve, k0, gain=None):
            for k in range(KD):
                dve.wait_ge(xt_hi, k0 + k + 1)
                hi = h_hi[:, k, :].bitcast(F32)
                if gain is None:
                    nc.vector.tensor_tensor(h_lo[:, k, :], S[k % 2][:, :], hi, ALU.subtract).then_inc(xt_lo, 1)
                else:
                    nc.vector.scalar_tensor_tensor(out=h_lo[:, k, :], in0=S[k % 2][:, :],
                                                   scalar=gain[:, k:k + 1], in1=hi,
                                                   op0=ALU.mult, op1=ALU.subtract).then_inc(xt_lo, 1)

        def rms_stats(act, st, src, dst):
            for tb in range(NB):
                last = st(nc.scalar.activation(hn[:, tb, :], src[:, tb, :], ACT.Square,
                                               accum_out=small[:, 60 + tb - 4:61 + tb - 4]))
            st.wait(last)
            st.wait(st(nc.scalar.activation(small[:, 60:64], small[:, 56:60], ACT.Ln, scale=1.0 / D, bias=EPS)))
            nc.scalar.activation(dst, small[:, 60:64], ACT.Exp, scale=-0.5).then_inc(stat_ready, 1)

        with nc.Block() as block:
            @block.sync
            def _(sp):
                sp.dma_start(const[:, :], const_in).then_inc(params_loaded, 16)
                sp.dma_start(masks[:, :], mask_in).then_inc(raw_loaded[1], 16)
                sp.dma_start(z_t[:, :].bitcast(I32), pos_in.partition_broadcast(P)).then_inc(rows_loaded, 16)
                sp.dma_start(x[:, :, :], x_in.rearrange("(b p) d -> p b d", p=P)).then_inc(raw_loaded[0], 16)
                sp.wait_ge(raw_loaded[0], 16)

            @block.vector
            def _(dve):
                st = Steps(dve, dve_step)
                dve.wait_ge(params_loaded, 16)
                st(nc.vector.tensor_copy(ident_r[:, :], ident))
                dve.wait_ge(raw_loaded[1], 16)
                st(nc.vector.tensor_copy(causal_r[:, :], masks[:, M_CAUSAL:M_CAUSAL + P]))
                st(nc.vector.tensor_copy(sbmask_r[:, :], masks[:, M_STRICT:M_STRICT + P]))
                st(nc.vector.tensor_copy(swa_r[:, :, :],
                                         masks[:, M_SWA:M_SWA + 8 * P].rearrange("p (h c) -> p h c", h=4)))
                m2 = masks[:, M_MULT:M_MULT + SEQ]
                st.wait(st(nc.vector.tensor_copy(m2_hi[:, :], m2)))
                st(nc.vector.tensor_tensor(m2_lo[:, :], m2, m2_hi[:, :].bitcast(F32), ALU.subtract))
                dve.wait_ge(rows_loaded, 16)
                st.wait(st(nc.vector.tensor_copy(nrm[:, :], z_t[:, :].bitcast(I32))))
                st.wait(st(nc.vector.tensor_scalar(rope_a[:, :], nrm[:, :], const[:, C_INV:C_INV + 1], None, ALU.mult)))
                big = 1.5 * 2.0 ** 23
                st.wait(st(nc.vector.tensor_scalar(nrm[:, :], rope_a[:, :], 1.0 / (2 * math.pi), big,
                                                   ALU.mult, ALU.add)))
                st.wait(st(nc.vector.tensor_scalar(nrm[:, :], nrm[:, :], big, None, ALU.subtract)))
                two_pi = 2 * math.pi
                p1 = 6.28125
                p2 = math.floor((two_pi - p1) * 2.0 ** 21) / 2.0 ** 21
                p3 = two_pi - p1 - p2
                for part in (p1, p2, p3):
                    st.wait(st(nc.vector.scalar_tensor_tensor(out=rope_a[:, :], in0=nrm[:, :], scalar=-part,
                                                              in1=rope_a[:, :], op0=ALU.mult, op1=ALU.add)))
                st.wait(st(nc.vector.tensor_scalar(rope_a[:, :], rope_a[:, :], math.pi, -math.pi, ALU.min, ALU.max)))
                st.wait(st(nc.vector.tensor_scalar(rope_b[:, :], rope_a[:, :], -1.0, None, ALU.mult)))
                st.wait(st(nc.vector.tensor_tensor(rope_b[:, :], rope_a[:, :], rope_b[:, :], ALU.max)))
                nc.vector.tensor_scalar(rope_b[:, :], rope_b[:, :], -1.0, math.pi / 2, ALU.mult, ALU.add) \
                  .then_inc(qk_ready, 1)

            @block.scalar
            def _(act):
                st = Steps(act, act_step)
                act.wait_ge(qk_ready, 1)
                st(nc.scalar.activation(sin[:, :], rope_a[:, :], ACT.Sin))
                st(nc.scalar.activation(cos[:, :], rope_b[:, :], ACT.Sin))
        end_of_stage()

        def t_index(a, qb, m, paired_from):
            return 4 * a + qb if a < paired_from else 4 * paired_from + 8 * (a - paired_from) + 2 * qb + m

        def before1(n):
            return (n - 4) // 2

        LAST = N_ATT - 1

        def head_unit(tile, f):
            if f == 0 and tile != "z":
                return B1_HEADS + "qkv".index(tile)
            if tile == "z":
                return B1_HEADS + (4 * f + 5 if f < LAST else 4 * f + 3)
            return B1_HEADS + 4 * f - 1 + {"q": 0, "k": 1, "v": 3}[tile]

        def fill_of(a, qb):
            if a == LAST:
                return ("z", a) if qb == 0 else None
            return (("q", a + 1), ("k", a + 1), ("z", a), ("v", a + 1))[qb]

        LATE1 = {}
        for a in range(N_ATT):
            LATE1[a, 0] = ("v", a)
            if a < LAST:
                LATE1[a, 1], LATE1[a, 2] = ("q", a + 1), ("k", a + 1)
            if 1 <= a <= N_A:
                LATE1[a, 3] = ("sum", a - 1)
        R1 = {use: i for i, use in enumerate([("mix", g) for g in range(4)] + [("q", 0), ("k", 0)]
                                             + [LATE1[key] for key in sorted(LATE1)])}

        def banks1(a, qb):
            return PT if (a, qb) == (LAST, NB - 1) else S

        def steps_back(a, qb, n):
            i = NB * a + qb - n
            return divmod(i, NB) if i >= 0 else None

        TURN_UNITS = GATE_TURN * 3 * (KD + 4) // KD
        GATE_BANK, PROJ_BANK = (PT[0], S[0], T[0]), (PT[1], S[1], T[1])

        def gate_at(mm, i):
            return (3 * mm + i) * (KD + 4)

        def gate_units(at, kts):
            return (at + kts - 1) // KD + 1

        def ti1(a, qb, m):
            return t_index(a, qb, m, N_A)

        with nc.Fori(0, DEPTH) as layer:
            with nc.Block() as block:
                w_layer = w1_in[bass.ds(layer, 1), :, :, :].rearrange("l n p c -> (l n) p c")

                @block.sync
                def _(sp):
                    sp.dma_start(colp[:, 0:P1_COLS], col1_in[bass.ds(layer, 1), :, :].rearrange("l p c -> p (l c)")) \
                      .then_inc(params_loaded, 16)
                    sp.dma_start(rowp[:, :], row1_in[bass.ds(layer, 1), :, :].rearrange("l p c -> p (l c)")) \
                      .then_inc(rows_loaded, 16)
                    load_units(sp, w_layer, B1_UNITS)

                @block.gpsimd
                def _(pool):
                    split_units(pool, B1_UNITS)

                @block.tensor
                def _(pe):
                    pe.wait_ge(norm_in, NB)
                    transpose_in(pe, hn, 0)
                    pe.wait_ge(xt_lo, KD)
                    for j in range(4):
                        pe.wait_ge(split_done, B1_V + j + 1)
                        s = j % 2
                        wh = w_hi[s][:, :].rearrange("p (k c) -> p k c", c=SEQ)
                        wl = w_lo[s][:, :].rearrange("p (k c) -> p k c", c=SEQ)
                        for tb in range(NB):
                            for k in (2 * j, 2 * j + 1):
                                last = mm3(TOK[tb][:, :], h_hi[:, k, tb * P:(tb + 1) * P], h_lo[:, k, tb * P:(tb + 1) * P],
                                           wh[:, k - 2 * j, :], wl[:, k - 2 * j, :], k == 0, k == KD - 1)
                        last.then_inc(unit_done, 1)

                    def mix(g):
                        pe.wait_ge(vb_ready, 2 * NB)
                        if g:
                            pe.wait_ge(r_out, g)
                        for c in range(NB):
                            last = nc.tensor.matmul(R[:, c * P:(c + 1) * P], ext[c][:, g * P:(g + 1) * P],
                                                    rowp[:, 3 * SEQ + g * P:3 * SEQ + (g + 1) * P], start=True, stop=True)
                        last.then_inc(r_ready, 1)

                    for g in range(4):
                        for j in range(2):
                            n = B1_UZ + 2 * g + j
                            for half in range(2):
                                tile_part(pe, n, before1(n), half, n % 2)
                        if g:
                            mix(g - 1)
                    mix(3)

                    def raw_wait(tile, f):
                        n = head_unit(tile, f)
                        pe.wait_ge(tile_out[n % 2], before1(n) + 1)
                        pe.wait_ge(r_out, R1[tile, f])

                    def rope(tile, f):
                        raw_wait(tile, f)
                        nc.tensor.matmul(R[:, :], rope1, raw_t["qk".index(tile)][:, :], start=True, stop=True).then_inc(r_ready, 1)

                    def v_transpose(f):
                        raw_wait("v", f)
                        for b in range(NB):
                            last = nc.tensor.transpose(R[:, b * P:(b + 1) * P], raw_t[0][:, b * P:(b + 1) * P], ident)
                        last.then_inc(r_ready, 1)

                    def sum_squares(a):
                        pe.wait_ge(sq_ready, a + 1)
                        pe.wait_ge(r_out, R1["sum", a])
                        nc.tensor.matmul(R[:, :], ones, nrm[:, :], start=True, stop=True).then_inc(r_ready, 1)

                    def scores(a, qb):
                        u, nk = 8 * a + 2 * qb, (qb + 1) * P
                        q, k, bank = qs[a % 2], ks[a % 2], banks1(a, qb)
                        if qb == 0:
                            pe.wait_ge(qk_ready, 2 * a + 2)
                        if bank is PT:
                            for t in range(2):
                                pe.wait_ge(tile_out[t], before1(B1_GATE))
                        elif u:
                            pe.wait_ge(probs_ready, u)
                        for m in range(2):
                            rows = slice(HD * m, HD * m + HD)
                            nc.tensor.matmul(bank[m][:, 0:nk], q[rows, qb * P:(qb + 1) * P], k[rows, 0:nk], start=True, stop=False)
                        for m in range(2):
                            if a < N_A:
                                last = nc.tensor.matmul(bank[m][:, nk - P:nk], ident_r[:, :], causal_r[:, :], start=False, stop=True)
                            else:
                                nc.tensor.matmul(bank[m][:, 0:nk], ident_r[:, :], m2_hi[:, SEQ - nk:SEQ], start=False, stop=False)
                                last = nc.tensor.matmul(bank[m][:, 0:nk], ident_r[:, :], m2_lo[:, SEQ - nk:SEQ],
                                                        start=False, stop=True)
                            last.then_inc(scores_ready, 1)

                    def transposes(a, qb):
                        pe.wait_ge(probs_normed, 4 * a + qb + 1)
                        for m in range(1 if a < N_A else 2):
                            i = ti1(a, qb, m)
                            if i >= 2:
                                pe.wait_ge(t_out, i - 1)
                            for b in range(qb + 1):
                                last = nc.tensor.transpose(T[i % 2][:, b * P:(b + 1) * P], pn[m][:, b * P:(b + 1) * P], ident)
                            last.then_inc(t_ready, 1)

                    def pv(a, qb):
                        pe.wait_ge(t_out, ti1(a, qb, 0 if a < N_A else 1) + 1)
                        if qb == 0:
                            pe.wait_ge(r_out, R1["v", a] + 1)
                            if a:
                                pe.wait_ge(o_out, a)
                        cols = slice(qb * P, (qb + 1) * P)
                        for b in range(qb + 1):
                            for m in range(1 if a < N_A else 2):
                                rows = slice(0, P) if a < N_A else slice(HD * m, HD * m + HD)
                                last = nc.tensor.matmul(O[rows, cols], vs[a % 2][:, b, rows],
                                                        pT[ti1(a, qb, m) % 2][:, b * P:(b + 1) * P],
                                                        start=(b == 0), stop=(b == qb))
                        last.then_inc(pv_done, 1)

                    def fill(a, qb, half):
                        if fill_of(a, qb):
                            n = head_unit(*fill_of(a, qb))
                            tile_part(pe, n, before1(n), half, n % 2)

                    def gate_tile(pe, turn, at, bank, kts, m_hi, m_lo):
                        for k in range(kts):
                            j, c = (at + k) // KD, (at + k) % KD
                            if c == 0:
                                pe.wait_ge(split_done, turn * TURN_UNITS + (B1_GATE + j + 1))
                            slot = (B1_GATE + j) % 2
                            w = slice(c * P, (c + 1) * P)
                            last = mm3(bank[:, :], w_hi[slot][:, w], w_lo[slot][:, w], m_hi[:, k, :], m_lo[:, k, :],
                                       k == 0, k == kts - 1)
                            if c == KD - 1:
                                last.then_inc(unit_done, 1)

                    for tile in "qkv":
                        n = head_unit(tile, 0)
                        for half in range(2):
                            tile_part(pe, n, before1(n), half, n % 2)
                        if tile == "k":
                            rope("q", 0)
                    rope("k", 0)
                    for a in range(N_ATT):
                        for qb in range(NB):
                            if banks1(a, qb) is S:
                                scores(a, qb)
                            if (a, qb) == (LAST, NB - 2):
                                scores(a, qb + 1)
                            if steps_back(a, qb, 2):
                                pv(*steps_back(a, qb, 2))
                            fill(a, qb, 0)
                            if steps_back(a, qb, 1):
                                transposes(*steps_back(a, qb, 1))
                            fill(a, qb, 1)
                            use, f = LATE1.get((a, qb), (None, 0))
                            if use == "v":
                                v_transpose(f)
                            elif use == "sum":
                                sum_squares(f)
                            elif use:
                                rope(use, f)
                    pv(LAST, NB - 2)
                    transposes(LAST, NB - 1)
                    pv(LAST, NB - 1)
                    with pe.Fori(0, KD // GATE_TURN) as turn:
                        for mm in range(GATE_TURN):
                            for i in range(3):
                                used = turn * (3 * GATE_TURN) + (before1(B1_GATE) + 3 * mm + i - 2)
                                pe.wait_ge(tile_out[0], used)
                                gate_tile(pe, turn, gate_at(mm, i), GATE_BANK[i], KD, h_hi, h_lo)
                                pe.wait_ge(tile_out[1], used)
                                if mm == 0 and i == 0:
                                    pe.wait_ge(y_ready, 12)
                                gate_tile(pe, turn, gate_at(mm, i) + KD, PROJ_BANK[i], 4,
                                          act_hi[:, 4 * i:4 * i + 4, :], act_lo[:, 4 * i:4 * i + 4, :])
                    pe.wait_ge(merged, KD)
                    for c in range(2):
                        tok_group(pe, B1_OUT + 4 * c, 4, KD, mrg_hi, mrg_lo, NB * c)

                @block.scalar
                def _(act):
                    st = Steps(act, act_step)
                    rms_stats(act, st, x, small[:, 0:4])
                    act.wait_ge(params_loaded, 16)
                    xt_hi_copy(act, 0, colp[:, P1_NORM:P1_NORM + KD])
                    act.wait_ge(lam_exp, 1)
                    nc.scalar.activation(small[:, 6:8], small[:, 4:6], ACT.Exp).then_inc(lam_exp, 1)
                    act.wait_ge(unit_done, 4)
                    for tb in range(NB):
                        nc.scalar.activation(ext[tb][:, :], TOK[tb][:, :], ACT.Gelu_apprx_tanh,
                                             accum_out=small[:, 12 + tb:13 + tb]).then_inc(v_ready, 1)
                    for tb in range(NB):
                        act.wait_ge(vb_ready, tb + 1)
                        last = st(nc.scalar.activation((*qs, *ks)[tb][:, :], ext[tb][:, :], ACT.Square,
                                                       accum_out=small[:, 16 + tb:17 + tb]))
                    st.wait(last)
                    st.wait(st(nc.scalar.activation(small[:, 20:24], small[:, 16:20], ACT.Ln, scale=1.0 / SEQ, bias=EPS)))
                    nc.scalar.activation(small[:, 20:24], small[:, 20:24], ACT.Exp, scale=-0.5).then_inc(stat_ready, 1)
                    for g in range(4):
                        n = B1_UZ + 2 * g
                        act.wait_ge(unit_done, n + 1)
                        if g:
                            act.wait_ge(y_ready, g)
                        nc.scalar.activation(sz[0][:, :], PT[0][:, :], ACT.Gelu_apprx_tanh).then_inc(tile_out[0], 1)
                        act.wait_ge(unit_done, n + 2)
                        nc.scalar.activation(z_t[:, :], PT[1][:, :], ACT.Tanh, scale=0.5).then_inc(z_ready, 1)

                    def raw_copy(tile, f):
                        n = head_unit(tile, f)
                        act.wait_ge(unit_done, n + 1)
                        if tile == "q" and f:
                            act.wait_ge(r_ready, R1["v", f - 1] + 1)
                        elif tile == "k" and f:
                            act.wait_ge(qk_ready, 2 * f)
                        elif tile == "v":
                            act.wait_ge(qk_ready, 2 * f + 1)
                        nc.scalar.activation(raw_t[tile == "k"][:, :], PT[n % 2][:, :], ACT.Copy,
                                             scale=HD ** -0.5 if tile == "q" else 1.0).then_inc(tile_out[n % 2], 1)

                    def v_copy(f):
                        act.wait_ge(r_ready, R1["v", f] + 1)
                        if f >= 2:
                            act.wait_ge(pv_done, 4 * (f - 1))
                        nc.scalar.activation(vs[f % 2][:, :, :], R[:, :].rearrange("p (b c) -> p b c", c=P), ACT.Copy) \
                          .then_inc(r_out, 1)

                    def z_tanh(f):
                        n = head_unit("z", f)
                        act.wait_ge(unit_done, n + 1)
                        before = head_unit("z", f - 1) if f else B1_HEADS - 1
                        act.wait_ge(tile_out[before % 2], before1(before) + 1)
                        nc.scalar.activation(z_t[:, :], PT[n % 2][:, :], ACT.Tanh, scale=0.5).then_inc(z_ready, 1)

                    def output_squares(a):
                        act.wait_ge(pv_done, 4 * a + 4)
                        if a >= 1:
                            act.wait_ge(y_ready, 4 + a)
                        nc.scalar.activation(ext[a % 2][:, :], O[:, :], ACT.Copy).then_inc(o_out, 1)
                        act.wait_ge(o_out, a + 1)
                        nc.scalar.activation(nrm[:, :], ext[a % 2][:, :], ACT.Square).then_inc(sq_ready, 1)

                    def output_rstd(a):
                        act.wait_ge(r_ready, R1["sum", a] + 1)
                        nc.scalar.activation(nrm[:, :], R[:, :], ACT.Ln, scale=1.0 / P, bias=EPS).then_inc(r_out, 1)
                        act.wait_ge(r_out, R1["sum", a] + 1)
                        nc.scalar.activation(nrm[:, :], nrm[:, :], ACT.Exp, scale=-0.5).then_inc(rs_ready, 1)

                    def softmax_exp(a, qb, m):
                        u, nk = 8 * a + 2 * qb + m, (qb + 1) * P
                        act.wait_ge(max_ready, u + 1)
                        if u >= 2:
                            act.wait_ge(probs_normed, 4 * a + qb)
                        nc.scalar.activation(prob[m][:, 0:nk], banks1(a, qb)[m][:, 0:nk], ACT.Exp,
                                             bias=small[:, 24 + 2 * qb + m:25 + 2 * qb + m],
                                             accum_out=small[:, 32 + 2 * qb + m:33 + 2 * qb + m]).then_inc(probs_ready, 1)

                    def pT_copy(a, qb):
                        for m in range(1 if a < N_A else 2):
                            i = ti1(a, qb, m)
                            act.wait_ge(t_ready, i + 1)
                            w = 4 * a + qb - (1 if a < N_A else 0)
                            if a == N_A and qb == 0:
                                w = 4 * a
                            if w > 0:
                                act.wait_ge(pv_done, w)
                            nc.scalar.activation(pT[i % 2][:, 0:(qb + 1) * P], T[i % 2][:, 0:(qb + 1) * P], ACT.Copy) \
                              .then_inc(t_out, 1)

                    for tile in "qkv":
                        raw_copy(tile, 0)
                    for a in range(N_ATT):
                        for qb in range(NB):
                            softmax_exp(a, qb, 0)
                            softmax_exp(a, qb, 1)
                            before = steps_back(a, qb, 1)
                            if before:
                                if fill_of(*before):
                                    tile, f = fill_of(*before)
                                    if tile == "z":
                                        z_tanh(f)
                                    else:
                                        raw_copy(tile, f)
                                if LATE1.get(before, ("", 0))[0] == "v":
                                    v_copy(a)
                                pT_copy(*before)
                            if qb == 1 and 1 <= a <= N_A:
                                output_squares(a - 1)
                            elif qb == 3 and 1 <= a <= N_A:
                                output_rstd(a - 1)
                    pT_copy(LAST, NB - 1)
                    with act.Fori(0, KD // GATE_TURN) as turn:
                        for mm in range(GATE_TURN):
                            for i in range(3):
                                act.wait_ge(unit_done, turn * TURN_UNITS + (B1_GATE + gate_units(gate_at(mm, i), KD)))
                                act.wait_ge(tile_out[1], turn * (3 * GATE_TURN) + (before1(B1_GATE) + 3 * mm + i - 2))
                                nc.scalar.activation(ext[i][:, :], GATE_BANK[i][:, :], ACT.Sigmoid).then_inc(tile_out[0], 1)

                @block.vector
                def _(dve):
                    st = Steps(dve, dve_step)
                    dve.wait_ge(stat_ready, 1)
                    for tb in range(NB):
                        nc.vector.tensor_scalar(hn[:, tb, :], x[:, tb, :], small[:, tb:tb + 1], None, ALU.mult) \
                          .then_inc(norm_in, 1)
                    dve.wait_ge(params_loaded, 16)
                    xt_lo_sub(dve, 0, colp[:, P1_NORM:P1_NORM + KD])
                    lam = colp[:, P1_LAM:P1_LAM + 4 * HD].rearrange("p (a b d) -> p a b d", a=2, b=2)
                    st.wait(st(nc.vector.tensor_tensor(rope_a[:, 0:2 * HD].rearrange("p (a d) -> p a d", a=2),
                                                       lam[:, :, 0, :], lam[:, :, 1, :], ALU.mult)))
                    nc.vector.tensor_reduce(small[:, 4:6], rope_a[:, 0:2 * HD].rearrange("p (a d) -> p a d", a=2),
                                            AX.X, ALU.add).then_inc(lam_exp, 1)
                    dve.wait_ge(lam_exp, 2)
                    st.wait(st(nc.vector.tensor_tensor(small[:, 8:9], small[:, 6:7], small[:, 7:8], ALU.subtract)))
                    st(nc.vector.tensor_tensor(small[:, 8:9], small[:, 8:9], colp[:, P1_INIT:P1_INIT + 1], ALU.add))
                    st(nc.vector.scalar_tensor_tensor(out=small[:, 9:10], in0=colp[:, P1_SUBLN:P1_SUBLN + 1], scalar=0.5,
                                                      in1=colp[:, P1_KEEP:P1_KEEP + 1], op0=ALU.mult, op1=ALU.mult))
                    dve.wait_ge(rows_loaded, 16)
                    sgw = rowp[:, 3 * SEQ:4 * SEQ].rearrange("p (g t) -> p g t", g=4)
                    upper = const[:, C_UPPER:C_UPPER + P].unsqueeze(1).to_broadcast([P, 4, P])
                    st(nc.vector.tensor_tensor(sgw, sgw, upper, ALU.mult))
                    for tb in range(NB):
                        dve.wait_ge(v_ready, tb + 1)
                        st.wait(st(nc.vector.tensor_scalar(small[:, 12 + tb:13 + tb], small[:, 12 + tb:13 + tb],
                                                           -1.0 / SEQ, None, ALU.mult)))
                        nc.vector.tensor_scalar(ext[tb][:, :], ext[tb][:, :], small[:, 12 + tb:13 + tb], None, ALU.add) \
                          .then_inc(vb_ready, 1)
                    dve.wait_ge(stat_ready, 2)
                    for tb in range(NB):
                        st.wait(st(nc.vector.scalar_tensor_tensor(out=ext[tb][:, :], in0=ext[tb][:, :],
                                                                  scalar=small[:, 20 + tb:21 + tb], in1=rowp[:, 0:SEQ],
                                                                  op0=ALU.mult, op1=ALU.mult)))
                        nc.vector.tensor_tensor(ext[tb][:, :], ext[tb][:, :], rowp[:, SEQ:2 * SEQ], ALU.add) \
                          .then_inc(vb_ready, 1)

                    def split_y(i):
                        st.wait(st(nc.vector.tensor_copy(act_hi[:, i, :], ytmp[:, :])))
                        nc.vector.tensor_tensor(act_lo[:, i, :], ytmp[:, :], act_hi[:, i, :].bitcast(F32), ALU.subtract) \
                          .then_inc(y_ready, 1)

                    for g in range(4):
                        dve.wait_ge(z_ready, g + 1)
                        nc.vector.scalar_tensor_tensor(out=sz[1][:, :], in0=z_t[:, :], scalar=1.0, in1=PT[1][:, :],
                                                       op0=ALU.add, op1=ALU.mult).then_inc(tile_out[1], 1)
                        dve.wait_ge(r_ready, g + 1)
                        bias = rowp[:, 2 * SEQ + g * P:2 * SEQ + (g + 1) * P].unsqueeze(1).to_broadcast([P, NB, P])
                        nc.vector.tensor_tensor(rope_a[:, :].rearrange("p (c t) -> p c t", c=NB),
                                                R[:, :].rearrange("p (c t) -> p c t", c=NB), bias, ALU.add).then_inc(r_out, 1)
                        dve.wait_ge(r_out, g + 1)
                        dve.wait_ge(tile_out[0], g + 1)
                        st.wait(st(nc.vector.scalar_tensor_tensor(out=rope_a[:, :], in0=rope_a[:, :], scalar=0.5, in1=sz[0][:, :],
                                                                  op0=ALU.mult, op1=ALU.mult)))
                        dve.wait_ge(tile_out[1], g + 1)
                        st.wait(st(nc.vector.tensor_tensor(ytmp[:, :], rope_a[:, :], sz[1][:, :], ALU.mult)))
                        split_y(4 + g)

                    def rotate(tile, f):
                        which, idx = "qk".index(tile), R1[tile, f]
                        dst = (qs, ks)[which][f % 2]
                        dve.wait_ge(r_ready, idx + 1)
                        if which or f:
                            dve.wait_ge(qk_ready, 2 * f + which)
                        st(nc.vector.tensor_tensor(rope_a[:, :], raw_t[which][:, :], cos[:, :], ALU.mult))
                        nc.vector.tensor_tensor(rope_b[:, :], R[:, :], sin[:, :], ALU.mult).then_inc(r_out, 1)
                        st.wait()
                        dve.wait_ge(r_out, idx + 1)
                        nc.vector.tensor_tensor(dst[:, :], rope_a[:, :], rope_b[:, :], ALU.add).then_inc(qk_ready, 1)

                    def row_max(a, qb, m):
                        u = 8 * a + 2 * qb + m
                        dve.wait_ge(scores_ready, u + 1)
                        nc.vector.tensor_reduce(small[:, 24 + 2 * qb + m:25 + 2 * qb + m], banks1(a, qb)[m][:, 0:(qb + 1) * P], AX.X,
                                                ALU.max, negate=True).then_inc(max_ready, 1)

                    def silu_z(f):
                        dve.wait_ge(z_ready, 4 + f + 1)
                        b = head_unit("z", f) % 2
                        nc.vector.scalar_tensor_tensor(out=sz[f % 2][:, :], in0=z_t[:, :], scalar=1.0, in1=PT[b][:, :],
                                                       op0=ALU.add, op1=ALU.mult).then_inc(tile_out[b], 1)

                    def normalise(a, qb):
                        nk = (qb + 1) * P
                        l, r = small[:, 32 + 2 * qb:34 + 2 * qb], small[:, 40:42]
                        dve.wait_ge(probs_ready, 8 * a + 2 * qb + 2)
                        st.wait(st(nc.vector.reciprocal(r, l)))
                        if a or qb:
                            dve.wait_ge(t_ready, ti1(a, qb - 1, 1) + 1 if qb else ti1(a - 1, 3, 1) + 1)
                        if a < N_A:
                            st.wait(st(nc.vector.tensor_scalar(small[:, 41:42], small[:, 41:42], small[:, 8:9], None, ALU.mult)))
                            st.wait(st(nc.vector.tensor_scalar(prob[1][:, 0:nk], prob[1][:, 0:nk], small[:, 41:42], None, ALU.mult)))
                            nc.vector.scalar_tensor_tensor(out=pn[0][:, 0:nk], in0=prob[0][:, 0:nk], scalar=small[:, 40:41],
                                                           in1=prob[1][:, 0:nk], op0=ALU.mult, op1=ALU.subtract) \
                              .then_inc(probs_normed, 1)
                        else:
                            st.wait(st(nc.vector.tensor_scalar(pn[0][:, 0:nk], prob[0][:, 0:nk], small[:, 40:41], None, ALU.mult)))
                            nc.vector.tensor_scalar(pn[1][:, 0:nk], prob[1][:, 0:nk], small[:, 41:42], None, ALU.mult) \
                              .then_inc(probs_normed, 1)

                    def epilogue(a):
                        z = head_unit("z", a)
                        dve.wait_ge(tile_out[z % 2], before1(z) + 1)
                        if a < N_A:
                            dve.wait_ge(rs_ready, a + 1)
                            st.wait(st(nc.vector.tensor_tensor(rope_a[:, :], ext[a % 2][:, :], nrm[:, :], ALU.mult)))
                            st.wait(st(nc.vector.scalar_tensor_tensor(out=ytmp[:, :], in0=rope_a[:, :], scalar=small[:, 9:10],
                                                                      in1=sz[a % 2][:, :], op0=ALU.mult, op1=ALU.mult)))
                        else:
                            dve.wait_ge(pv_done, 4 * a + 4)
                            nc.vector.scalar_tensor_tensor(out=ytmp[:, :], in0=O[:, :], scalar=0.5, in1=sz[a % 2][:, :],
                                                           op0=ALU.mult, op1=ALU.mult).then_inc(o_out, 1)
                            dve.wait_ge(o_out, a + 1)
                        split_y(a if a < N_A else 8 + a - N_A)

                    rotate("q", 0)
                    rotate("k", 0)
                    for a in range(N_ATT):
                        for qb in range(NB):
                            row_max(a, qb, 0)
                            row_max(a, qb, 1)
                            before = steps_back(a, qb, 1)
                            if before and fill_of(*before) == ("z", before[0]):
                                silu_z(before[0])
                            if LATE1.get(before, ("", 0))[0] in ("q", "k"):
                                rotate(*LATE1[before])
                            normalise(a, qb)
                            if qb == 0 and 2 <= a < N_A + 2:
                                epilogue(a - 2)
                            elif qb == 1 and a > N_A:
                                epilogue(a - 1)
                    epilogue(LAST)
                    base_step, per_tile = st.n, 3
                    total, term = ytmp[:, :], rope_a[:, :]
                    with dve.Fori(0, KD // GATE_TURN) as turn:
                        for mm in range(GATE_TURN):
                            m = turn * GATE_TURN + mm
                            for i in range(3):
                                done = turn * (3 * GATE_TURN) + (before1(B1_GATE) + 3 * mm + i + 1)
                                dve.wait_ge(tile_out[0], done)
                                dve.wait_ge(unit_done, turn * TURN_UNITS + (B1_GATE + gate_units(gate_at(mm, i) + KD, 4)))
                                nc.vector.tensor_tensor(term if i else total, ext[i][:, :], PROJ_BANK[i][:, :], ALU.mult) \
                                  .then_inc(tile_out[1], 1)
                                dve.wait_ge(tile_out[1], done)
                                if i:
                                    nc.vector.tensor_tensor(total, total, term, ALU.add).then_inc(dve_step, 1)
                                    dve.wait_ge(dve_step, turn * (per_tile * GATE_TURN) + (base_step + per_tile * mm + i))
                            hi = mrg_hi[:, bass.ds(m, 1), :].rearrange("p a t -> p (a t)")
                            lo = mrg_lo[:, bass.ds(m, 1), :].rearrange("p a t -> p (a t)")
                            nc.vector.tensor_copy(hi, total).then_inc(dve_step, 1)
                            dve.wait_ge(dve_step, turn * (per_tile * GATE_TURN) + (base_step + per_tile * mm + 3))
                            nc.vector.tensor_tensor(lo, total, hi.bitcast(F32), ALU.subtract).then_inc(merged, 1)
                            dve.wait_ge(merged, m + 1)
                    st.n += per_tile * KD
                    for c in range(2):
                        dve.wait_ge(unit_done, B1_OUT + 4 * c + 4)
                        for tb in range(NB):
                            cols = slice(c * SEQ, (c + 1) * SEQ)
                            nc.vector.tensor_tensor(x[:, tb, cols], x[:, tb, cols], TOK[tb][:, :], ALU.add).then_inc(tok_out, 1)
            end_of_stage()

        with nc.Block() as block:
            @block.sync
            def _(sp):
                sp.dma_start(rowp[:, 0:D], final_in.to_broadcast([P, D])).then_inc(rows_loaded, 16)
                sp.dma_start(cos[:, :], rope2_in[0, :, :]).then_inc(params_loaded, 16)
                sp.dma_start(sin[:, :], rope2_in[1, :, :]).then_inc(params_loaded, 16)
                sp.wait_ge(params_loaded, 32)

            @block.scalar
            def _(act):
                rms_stats(act, Steps(act, act_step), x, small[:, 0:4])

            @block.vector
            def _(dve):
                dve.wait_ge(stat_ready, 1)
                dve.wait_ge(rows_loaded, 16)
                for tb in range(NB):
                    nc.vector.scalar_tensor_tensor(out=x[:, tb, :], in0=x[:, tb, :], scalar=small[:, tb:tb + 1],
                                                   in1=rowp[:, 0:D], op0=ALU.mult, op1=ALU.mult)
        end_of_stage()

        SWA, MLA, SB, FOX = range(4)
        KIND = (SWA, SWA, MLA, MLA, SB, SB, FOX, FOX)
        N_STEPS = N_ATT * NB
        SOFTMAX = {0: 0, 1: 1, 2: 2, 3: 3, 6: 4, 7: 5}
        SB0 = KIND.index(SB)
        FIRST = ("wq0", "wk", "wv", "ckv", "cq0", "cq1")
        FILL = {(0, 0): ("wq1",), (0, 1): ("kr",), (0, 2): ("gates",), (0, 3): ("uq0",),
                (1, 0): ("uqr",), (1, 1): ("uk0", "uv0"), (1, 2): ("sq1",), (1, 3): ("sk1",),
                (2, 0): ("uq1",), (2, 1): ("uk1", "uv1"), (2, 2): ("sq0",), (2, 3): ("sk0",),
                (3, 0): ("sv0",), (3, 1): ("fq0",), (3, 2): ("fk0",), (4, 0): ("sv1",), (4, 1): ("fq1",), (4, 2): ("fk1",),
                (5, 0): ("fv0",), (6, 0): ("fv1",)}
        assert FIRST + tuple(t for key in sorted(FILL) for t in FILL[key]) == B2_TILES
        TILE = {name: t for t, name in enumerate(B2_TILES)}
        WHERE = {}
        DONE = {}
        for n, unit in enumerate(B2_PACKED):
            at = 0
            for name in unit:
                WHERE[name] = (n, at)
                at += B2_KT.get(name, KD)
                before = sum(signal is small_done for signal, _ in DONE.values())
                DONE[name] = (unit_done, n + 1) if name == unit[-1] else (small_done, before + 1)
        PREFIX = {SWA: "w", MLA: "u", SB: "s", FOX: "f"}
        FIRST_R = ("wv", "ckv")
        LATE = {(0, 0): "cq", (0, 2): "kr", (1, 1): "qr", (1, 2): "uv0", (2, 2): "e1", (2, 3): "uv1", (3, 1): "sv0",
                (4, 1): "e3", (4, 2): "sv1", (5, 1): "fv0", (6, 1): "e5", (6, 2): "fv1"}
        R2 = {name: i for i, name in enumerate(FIRST_R + tuple(LATE[key] for key in sorted(LATE)) + ("e7",))}
        SQUARES = {"ckv": 1, "cq": 2, "e1": 3, "e3": 4, "e5": 5, "e7": 6}
        V_TILES = ("wv", "uv0", "uv1", "sv0", "sv1", "fv0", "fv1")
        vw_t = ext[3][:, :].rearrange("p (b c) -> p b c", c=P)
        DEST = {"wq0": wq_t[0], "wq1": wq_t[1], "wk": wk_t, "ckv": ckv_t, "cq0": cq_t[0], "cq1": cq_t[1],
                "kr": raw_t[0], "uqr": raw_t[1], "uq0": qs[0], "uq1": qs[1], "uk0": ks[0], "uk1": ks[1],
                "sq0": wq_t[0], "sq1": cq_t[0], "sk0": wk_t, "sk1": ckv_t,
                "fq0": qs[0], "fq1": qs[1], "fk0": ks[0], "fk1": ks[1],
                "wv": raw_t[1], "uv0": raw_t[0], "uv1": raw_t[1], "sv0": raw_t[0], "sv1": raw_t[1],
                "fv0": raw_t[0], "fv1": raw_t[1]}

        def q_name(a):
            return f"{PREFIX[KIND[a]]}q{a % 2}"

        def k_name(a):
            return "wk" if KIND[a] == SWA else f"{PREFIX[KIND[a]]}k{a % 2}"

        def v_name(a):
            return "wv" if KIND[a] == SWA else f"{PREFIX[KIND[a]]}v{a % 2}"

        def v_of(a):
            return vw_t if KIND[a] == SWA else vs[a % 2]

        def head_of(a, m):
            i = a % 2
            return i + 2 * m if KIND[a] == SWA else 2 * i + m

        def first_key(a, qb):
            return max(0, qb - 1) * P if KIND[a] == SWA else 0

        def u_of(a, qb, m):
            return 8 * SOFTMAX[a] + 2 * qb + m

        def w_of(a, j):
            return 8 * (a - SB0) + 2 * j

        def banks(a, qb):
            if KIND[a] == SB:
                return (S, T)[qb % 2]
            return PT if a == N_ATT - 1 and qb % 2 else S

        def sb_weights_at(j):
            return pT if j % 2 else (z_t, qr_t)

        OUTPUT_AT = {(1, 1): 0, (2, 1): 1, (3, 1): 2, (4, 0): 3, (5, 0): 4, (6, 0): 5, (7, 1): 6}

        def step_before(a, qb):
            return divmod(NB * a + qb - 1, NB) if a or qb else None

        def is_sb(step):
            return step is not None and KIND[step[0]] == SB

        mla_scale = (HD + HD // 2) ** -0.5

        with nc.Fori(0, DEPTH) as layer:
            with nc.Block() as block:
                w_layer2 = w2_in[bass.ds(layer, 1), :, :, :].rearrange("l n p c -> (l n) p c")
                rows2 = row2_in[bass.ds(layer, 1), :, :, :].rearrange("l r p c -> (l r) p c")

                @block.sync
                def _(sp):
                    sp.dma_start(colp[:, 0:P2_COLS], col2_in[bass.ds(layer, 1), :, :].rearrange("l p c -> p (l c)")) \
                      .then_inc(params_loaded, 16)
                    load_units(sp, w_layer2, B2_UNITS)

                @block.gpsimd
                def _(pool):
                    split_units(pool, B2_UNITS)

                @block.tensor
                def _(pe):
                    transpose_in(pe, x, 0)
                    pe.wait_ge(xt_lo, KD)

                    def part(name, half):
                        t, (n, at), kt, mov = TILE[name], WHERE[name], B2_KT.get(name, KD), None
                        if kt < KD:
                            pe.wait_ge(latent_ready, 1 if kt == 1 else 3)
                            i = 10 if kt == 1 else 8
                            mov = (act_hi[:, i:i + 2, :], act_lo[:, i:i + 2, :])
                        if half == 0 or kt > 1:
                            tile_part(pe, n, t // 2, half, n % 2, kt=kt, mov=mov, bank=t % 2, at=at, done=DONE[name][0])

                    def tile_wait(name):
                        t = TILE[name]
                        pe.wait_ge(tile_out[t % 2], t // 2 + 1)

                    def r_free(name):
                        if R2[name]:
                            pe.wait_ge(r_out, R2[name])

                    def v_transpose(name):
                        tile_wait(name)
                        r_free(name)
                        for b in range(NB):
                            last = nc.tensor.transpose(R[:, b * P:(b + 1) * P], DEST[name][:, b * P:(b + 1) * P], ident)
                        last.then_inc(r_ready, 1)

                    def rope(name, tile):
                        tile_wait(tile)
                        r_free(name)
                        nc.tensor.matmul(R[:, :], rope2, DEST[tile][:, :], start=True, stop=True).then_inc(r_ready, 1)

                    def sum_squares(name, tiles):
                        pe.wait_ge(sq_ready, SQUARES[name])
                        r_free(name)
                        for i, t in enumerate(tiles):
                            last = nc.tensor.matmul(R[:, :], ones, t[:, :], start=(i == 0), stop=(i == len(tiles) - 1))
                        last.then_inc(r_ready, 1)

                    def operands_wait(a):
                        tile_wait(q_name(a))
                        tile_wait(k_name(a))
                        if KIND[a] == FOX:
                            pe.wait_ge(gate_ready, 1)
                        elif KIND[a] == MLA:
                            pe.wait_ge(qk_ready, 2)

                    def bank_wait(a, qb):
                        if KIND[a] == SB:
                            w = w_of(a, qb)
                            if w == 0:
                                pe.wait_ge(probs_ready, u_of(SB0 - 1, NB - 1, 1) + 1)
                            elif w == 2:
                                pe.wait_ge(t_out, u_of(SB0 - 1, NB - 1, 1) + 1)
                            else:
                                pe.wait_ge(sb_prob, w - 2)
                        elif a == SB0 + 2 and qb == 0:
                            pe.wait_ge(sb_prob, w_of(a - 1, NB - 1))
                        elif a == N_ATT - 1 and qb:
                            if qb >= 2:
                                pe.wait_ge(probs_ready, u_of(a, qb - 2, 1) + 1)
                        elif a or qb:
                            pe.wait_ge(probs_ready, u_of(a, qb, 0))

                    def scores(a, qb):
                        kind, k0, k1 = KIND[a], first_key(a, qb), (qb + 1) * P
                        nk, block_q = k1 - k0, slice(qb * P, (qb + 1) * P)
                        if qb == 0:
                            operands_wait(a)
                        bank_wait(a, qb)
                        q, k = DEST[q_name(a)], DEST[k_name(a)]
                        S = banks(a, qb)
                        for m in range(2):
                            rows = slice(HD * m, HD * m + HD)
                            nc.tensor.matmul(S[m][:, 0:nk], q[rows, block_q], k[rows, k0:k1], start=True, stop=False)
                        for m in range(2):
                            h = head_of(a, m)
                            if kind == FOX:
                                nc.tensor.matmul(S[m][:, 0:nk], const[0:4, C_SEL + h * P:C_SEL + (h + 1) * P], ext[2][0:4, 0:nk],
                                                 start=False, stop=False)
                            elif kind == MLA:
                                r = slice(32 * h, 32 * h + 32)
                                nc.tensor.matmul(S[m][:, 0:nk], qr_t[r, block_q], z_t[r, 0:nk], start=False, stop=False,
                                                 tile_position=(32 * h, 0))
                        for m in range(2):
                            if kind == SWA:
                                last = nc.tensor.matmul(S[m][:, 0:nk], ident_r[:, :], swa_r[:, head_of(a, m), 2 * P - nk:2 * P],
                                                        start=False, stop=True)
                            else:
                                last = nc.tensor.matmul(S[m][:, nk - P:nk], ident_r[:, :], causal_r[:, :], start=False, stop=True)
                            last.then_inc(scores_ready, 1)

                    def probs_transpose(a, qb, m):
                        u, nk = u_of(a, qb, m), (qb + 1) * P - first_key(a, qb)
                        pe.wait_ge(probs_normed, u // 2 + 1)
                        if u >= 2:
                            pe.wait_ge(t_out, u - 1)
                        for b in range(nk // P):
                            last = nc.tensor.transpose(T[m][:, b * P:(b + 1) * P], pn[m][:, b * P:(b + 1) * P], ident)
                        last.then_inc(t_ready, 1)

                    def v_wait(a):
                        pe.wait_ge(r_out, R2[v_name(a)] + 1)
                        if a:
                            pe.wait_ge(o_out, a)

                    def pv(a, qb):
                        pe.wait_ge(t_out, u_of(a, qb, 1) + 1)
                        if qb == 0:
                            v_wait(a)
                        b0 = first_key(a, qb) // P
                        for b in range(b0, qb + 1):
                            for m in range(2):
                                rows = slice(HD * m, HD * m + HD)
                                last = nc.tensor.matmul(O[rows, qb * P:(qb + 1) * P], v_of(a)[:, b, rows],
                                                        pT[m][:, (b - b0) * P:(b - b0 + 1) * P], start=(b == b0), stop=(b == qb))
                        last.then_inc(pv_done, 1)

                    def sb_scores_of(a, j):
                        lo = (NB - 1 - j) * P
                        if j == 0:
                            operands_wait(a)
                        bank_wait(a, j)
                        q, k, S = DEST[q_name(a)], DEST[k_name(a)], banks(a, j)
                        for m in range(2):
                            rows = slice(HD * m, HD * m + HD)
                            nc.tensor.matmul(S[m][:, lo:SEQ], k[rows, lo:lo + P], q[rows, lo:SEQ], start=True, stop=False)
                        for m in range(2):
                            nc.tensor.matmul(S[m][:, lo:lo + P], ident_r[:, :], sbmask_r[:, :], start=False, stop=True) \
                              .then_inc(sb_scores, 1)

                    def sb_between(a, j):
                        lo, w, S = (NB - 1 - j) * P, w_of(a, j), banks(a, j)
                        for m in range(2):
                            pe.wait_ge(sb_sp, w + m + 1)
                            last = nc.tensor.matmul(S[m][:, lo:SEQ], neg_tri, pn[m][:, lo:SEQ], start=False, stop=True,
                                                    skip_group_check=True)
                            if j:
                                pe.wait_ge(sb_sum, w + m - 1)
                                last = nc.tensor.matmul(S[m][:, lo + P:SEQ], neg_ones, sz[m][:, lo + P:SEQ],
                                                        start=False, stop=True, skip_group_check=True)
                            last.then_inc(sb_cum, 1)

                    def sb_pv(a, j):
                        kb, lo = NB - 1 - j, (NB - 1 - j) * P
                        if j == 0:
                            v_wait(a)
                        pe.wait_ge(sb_prob, w_of(a, j) + 2)
                        for m in range(2):
                            rows = slice(HD * m, HD * m + HD)
                            last = nc.tensor.matmul(O[rows, lo:SEQ], vs[a % 2][:, kb, rows], sb_weights_at(j)[m][:, lo:SEQ],
                                                    start=(j == 0), stop=(j == NB - 1), skip_group_check=True)
                        last.then_inc(pv_done, 1)

                    def transposes(step):
                        if step and not is_sb(step):
                            probs_transpose(*step, 0)
                            probs_transpose(*step, 1)

                    def weighted_v(step):
                        if step:
                            (sb_pv if is_sb(step) else pv)(*step)

                    def fill(a, qb, which):
                        halves = [(name, half) for name in FILL.get((a, qb), ()) for half in range(2)]
                        cut = (len(halves) + 1) // 2
                        for name, half in (halves[:cut] if which == 0 else halves[cut:]):
                            part(name, half)

                    def late_work(name):
                        if name == "cq":
                            sum_squares(name, sz)
                        elif name == "kr":
                            rope(name, "kr")
                        elif name == "qr":
                            rope(name, "uqr")
                        elif name[0] == "e":
                            sum_squares(name, (nrm, rope_b))
                        else:
                            v_transpose(name)

                    for name in FIRST:
                        part(name, 0)
                        part(name, 1)
                        if name == "cq0":
                            v_transpose("wv")
                    sum_squares("ckv", (z_t,))
                    for a in range(N_ATT):
                        for qb in range(NB):
                            before, after = step_before(a, qb), divmod(NB * a + qb + 1, NB)
                            two_before = before and step_before(*before)
                            if KIND[a] != SB:
                                if a < N_ATT - 1 or qb == 0:
                                    scores(a, qb)
                                if a == N_ATT - 1 and qb + 1 < NB:
                                    scores(*after)
                                if not is_sb(two_before):
                                    weighted_v(two_before)
                                if is_sb(before):
                                    weighted_v(before)
                                fill(a, qb, 0)
                                transposes(before)
                                fill(a, qb, 1)
                            elif w_of(a, qb) == 0:
                                sb_scores_of(a, qb)
                                weighted_v(two_before)
                                transposes(before)
                                fill(a, qb, 0)
                                weighted_v(before)
                                sb_between(a, qb)
                                sb_scores_of(a, qb + 1)
                                fill(a, qb, 1)
                            else:
                                sb_between(a, qb)
                                if is_sb(after):
                                    sb_scores_of(*after)
                                fill(a, qb, 0)
                                weighted_v(before)
                                fill(a, qb, 1)
                            if (a, qb) in LATE:
                                late_work(LATE[a, qb])
                    last_step = (N_ATT - 1, NB - 1)
                    weighted_v(step_before(*last_step))
                    transposes(last_step)
                    weighted_v(last_step)
                    for j in range(4):
                        if j == 1:
                            sum_squares("e7", (nrm, rope_b))
                        elif j == 3:
                            pe.wait_ge(y_ready, 8)
                        else:
                            pe.wait_ge(y_ready, 6)
                        tok_unit(pe, B2_WO, j, KD, act_hi, act_lo, 0)
                    tok_group(pe, B2_WO + 4, 4, KD, act_hi, act_lo, NB)
                    pe.wait_ge(ln_done, NB)
                    transpose_in(pe, x, KD)
                    pe.wait_ge(xt_lo, 2 * KD)
                    for hf in range(2):
                        n0 = B2_FFN + hf * B2_FFN_HALF
                        done = len(B2_TILES) // 2 + FF_HALF * hf
                        with pe.Fori(0, FF_HALF) as j:
                            for t in range(2):
                                for half in range(2):
                                    tile_part(pe, j * 2 + (n0 + t), j + done, half, t)
                        pe.wait_ge(gu_ready, FF_HALF * (hf + 1))
                        for c in range(2):
                            tok_group(pe, n0 + 2 * FF_HALF + DOWN_UNITS * c, DOWN_UNITS, FF_HALF, act_hi, act_lo,
                                      NB * (2 + 2 * hf + c))

                @block.scalar
                def _(act):
                    st = Steps(act, act_step)
                    nc.scalar.preload_act_table_set("natural_log_exp_and_others")
                    xt_hi_copy(act, 0)

                    def tile_copy(name):
                        t = TILE[name]
                        act.wait_ge(*DONE[name])
                        if name == "uv0":
                            act.wait_ge(qk_ready, 1)
                        elif name == "uv1":
                            act.wait_ge(qk_ready, 2)
                        scale = 1.0
                        if name[1] == "q" and name[0] != "c":
                            scale = mla_scale if name[0] == "u" else HD ** -0.5
                        nc.scalar.activation(DEST[name][:, :], PT[t % 2][:, :], ACT.Copy, scale=scale) \
                          .then_inc(tile_out[t % 2], 1)

                    def v_copy(name):
                        act.wait_ge(r_ready, R2[name] + 1)
                        if name[0] in "sf":
                            a = KIND.index(SB if name[0] == "s" else FOX) + int(name[2])
                            act.wait_ge(pv_done, NB * (a - 1))
                        dst = vw_t if name == "wv" else vs[int(name[2])][:, :, :]
                        nc.scalar.activation(dst, R[:, :].rearrange("p (b c) -> p b c", c=P), ACT.Copy).then_inc(r_out, 1)

                    def rstd(name, dst, width):
                        act.wait_ge(r_ready, R2[name] + 1)
                        nc.scalar.activation(dst[:, :], R[:, :], ACT.Ln, scale=1.0 / width, bias=EPS).then_inc(r_out, 1)
                        act.wait_ge(r_out, R2[name] + 1)
                        nc.scalar.activation(dst[:, :], dst[:, :], ACT.Exp, scale=-0.5).then_inc(rs_ready, 1)

                    def output_copy(a):
                        act.wait_ge(pv_done, 4 * a + 4)
                        if a >= 2:
                            act.wait_ge(y_ready, 2 * (a // 2))
                        nc.scalar.activation(ext[a % 2][:, :], O[:, :], ACT.Copy).then_inc(o_out, 1)
                        if a % 2:
                            act.wait_ge(o_out, a + 1)
                            st(nc.scalar.activation(nrm[:, :], ext[0][:, :], ACT.Square))
                            st.wait()
                            nc.scalar.activation(rope_b[:, :], ext[1][:, :], ACT.Square).then_inc(sq_ready, 1)

                    def softmax_exp(a, qb, m):
                        u, nk, c = u_of(a, qb, m), (qb + 1) * P - first_key(a, qb), 2 * qb + m
                        act.wait_ge(max_ready, u + 1)
                        if u >= 2:
                            act.wait_ge(probs_normed, u // 2)
                        if KIND[a] == SWA:
                            sink = colp[:, P2_SINK + head_of(a, m):P2_SINK + head_of(a, m) + 1]
                            st(nc.scalar.activation(small[:, 44 + m:45 + m], sink, ACT.Exp, bias=small[:, 24 + c:25 + c]))
                        nc.scalar.activation(prob[m][:, 0:nk], banks(a, qb)[m][:, 0:nk], ACT.Exp, bias=small[:, 24 + c:25 + c],
                                             accum_out=small[:, 32 + c:33 + c]).then_inc(probs_ready, 1)

                    def pT_copy(a, qb):
                        nk = (qb + 1) * P - first_key(a, qb)
                        for m in range(2):
                            act.wait_ge(t_ready, u_of(a, qb, m) + 1)
                            if 4 * a + qb:
                                act.wait_ge(pv_done, 4 * a + qb)
                            nc.scalar.activation(pT[m][:, 0:nk], T[m][:, 0:nk], ACT.Copy).then_inc(t_out, 1)

                    def sb_softplus(a, j):
                        lo, w = (NB - 1 - j) * P, w_of(a, j)
                        for m in range(2):
                            e = prob[m][:, lo:SEQ]
                            act.wait_ge(sb_scores, w + m + 1)
                            if w == 0:
                                act.wait_ge(probs_normed, NB * SB0)
                            else:
                                act.wait_ge(sb_sp, w + m - 1)
                            st.wait(st(nc.scalar.activation(e, banks(a, j)[m][:, lo:SEQ], ACT.Abs)))
                            st.wait(st(nc.scalar.activation(e, e, ACT.Exp, scale=-1.0)))
                            nc.scalar.activation(e, e, ACT.Ln, bias=1.0).then_inc(sb_ln, 1)

                    def sb_weights(a, j):
                        lo, w = (NB - 1 - j) * P, w_of(a, j)
                        for m in range(2):
                            act.wait_ge(sb_cum, w + m + 1)
                            act.wait_ge(pv_done, NB * a + j - 1)
                            nc.scalar.activation(sb_weights_at(j)[m][:, lo:SEQ], banks(a, j)[m][:, lo:SEQ], ACT.Exp) \
                              .then_inc(sb_prob, 1)

                    def latent_squares(names, squares):
                        for name, square in zip(names, squares):
                            t = TILE[name]
                            act.wait_ge(tile_out[t % 2], t // 2 + 1)
                            last = nc.scalar.activation(square[:, :], DEST[name][:, :], ACT.Square)
                            if name == names[-1]:
                                last.then_inc(sq_ready, 1)
                            else:
                                st.wait(st(last))

                    def gate_log():
                        t = TILE["gates"]
                        act.wait_ge(tile_out[t % 2], t // 2 + 1)
                        y, e = sz[0][0:4, :], sz[1][0:4, :]
                        st.wait(st(nc.scalar.activation(e, y, ACT.Abs)))
                        st.wait(st(nc.scalar.activation(e, e, ACT.Exp, scale=-1.0)))
                        nc.scalar.activation(e, e, ACT.Ln, bias=1.0).then_inc(gate_ln, 1)

                    act.wait_ge(params_loaded, 16)
                    for name in FIRST:
                        tile_copy(name)
                        if name == "ckv":
                            latent_squares(("ckv",), (z_t,))
                    v_copy("wv")
                    latent_squares(("cq0", "cq1"), sz)
                    rstd("ckv", z_t, P)
                    for a in range(N_ATT):
                        for qb in range(NB):
                            before, after = step_before(a, qb), divmod(NB * a + qb + 1, NB)
                            if KIND[a] != SB:
                                softmax_exp(a, qb, 0)
                                softmax_exp(a, qb, 1)
                            elif w_of(a, qb) == 0:
                                sb_softplus(a, qb)
                            for name in FILL.get(before, ()):
                                if name != "gates":
                                    tile_copy(name)
                            if LATE.get(before) in V_TILES:
                                v_copy(LATE[before])
                            if KIND[a] == SB and w_of(a, qb):
                                sb_weights(a, qb)
                                if is_sb(after):
                                    sb_softplus(*after)
                            if before and not is_sb(before):
                                pT_copy(*before)
                            if (a, qb) in OUTPUT_AT:
                                output_copy(OUTPUT_AT[a, qb])
                            if KIND[a] == SB and w_of(a, qb) == 0:
                                sb_weights(a, qb)
                                sb_softplus(*after)
                            late = LATE.get((a, qb), "")
                            if late == "cq":
                                rstd("cq", sz[0], 2 * P)
                            elif late[:1] == "e":
                                rstd(late, nrm, 4 * HD)
                            if (a, qb) == (1, 0):
                                gate_log()
                            elif (a, qb) == (6, 2):
                                act.dma_start(rowp[:, :], rows2[0, :, :]).then_inc(rows_loaded, 16)
                    pT_copy(N_ATT - 1, NB - 1)
                    output_copy(N_ATT - 1)
                    rstd("e7", nrm, 4 * HD)

                    def ln_stats(count):
                        for tb in range(NB):
                            act.wait_ge(ln_centre, count + tb + 1)
                            last = st(nc.scalar.activation(hn[:, tb, :], x[:, tb, :], ACT.Square,
                                                           accum_out=small[:, 16 + tb:17 + tb]))
                        st.wait(last)
                        st.wait(st(nc.scalar.activation(small[:, 20:24], small[:, 16:20], ACT.Ln, scale=1.0 / D, bias=LN_EPS)))
                        nc.scalar.activation(small[:, 20:24], small[:, 20:24], ACT.Exp, scale=-0.5).then_inc(stat_ready, 1)

                    ln_stats(0)
                    xt_hi_copy(act, KD)
                    act.wait_ge(ln_done, NB)
                    act.dma_start(rowp[:, :], rows2[1, :, :]).then_inc(rows_loaded, 16)
                    for hf in range(2):
                        n0 = B2_FFN + hf * B2_FFN_HALF
                        done = len(B2_TILES) // 2 + FF_HALF * hf
                        with act.Fori(0, FF_HALF) as j:
                            act.wait_ge(unit_done, j * 2 + (n0 + 1))
                            act.wait_ge(tile_out[1], j + done)
                            nc.scalar.activation(nrm[:, :], PT[0][:, :], ACT.Silu).then_inc(tile_out[0], 1)
                    ln_stats(NB)

                @block.vector
                def _(dve):
                    st = Steps(dve, dve_step)
                    xt_lo_sub(dve, 0)
                    dve.wait_ge(params_loaded, 16)
                    for h in range(4):
                        st(nc.vector.tensor_scalar(small[:, 48 + h:49 + h], colp[:, P2_SINK + h:P2_SINK + h + 1], -1.0, None, ALU.mult))
                    st.wait()

                    def row_max(a, qb, m):
                        u, c = u_of(a, qb, m), 2 * qb + m
                        nm = small[:, 24 + c:25 + c]
                        dve.wait_ge(scores_ready, u + 1)
                        top_ = nc.vector.tensor_reduce(nm, banks(a, qb)[m][:, 0:(qb + 1) * P - first_key(a, qb)], AX.X, ALU.max, negate=True)
                        if KIND[a] != SWA:
                            top_.then_inc(max_ready, 1)
                            return
                        st.wait(st(top_))
                        h = head_of(a, m)
                        nc.vector.tensor_tensor(nm, nm, small[:, 48 + h:49 + h], ALU.min).then_inc(max_ready, 1)

                    def normalise(a, qb):
                        u, nk = u_of(a, qb, 0), (qb + 1) * P - first_key(a, qb)
                        l, r = small[:, 32 + 2 * qb:34 + 2 * qb], small[:, 40:42]
                        dve.wait_ge(probs_ready, u + 2)
                        if KIND[a] == SWA:
                            st.wait(st(nc.vector.tensor_tensor(l, l, small[:, 44:46], ALU.add)))
                        st.wait(st(nc.vector.reciprocal(r, l)))
                        if u:
                            dve.wait_ge(t_ready, u)
                        st.wait(st(nc.vector.tensor_scalar(pn[0][:, 0:nk], prob[0][:, 0:nk], small[:, 40:41], None, ALU.mult)))
                        nc.vector.tensor_scalar(pn[1][:, 0:nk], prob[1][:, 0:nk], small[:, 41:42], None, ALU.mult) \
                          .then_inc(probs_normed, 1)

                    def rotate(name, buf, dst, count):
                        dve.wait_ge(r_ready, R2[name] + 1)
                        st(nc.vector.tensor_tensor(rope_a[:, :], raw_t[buf][:, :], cos[:, :], ALU.mult))
                        nc.vector.tensor_tensor(rope_b[:, :], R[:, :], sin[:, :], ALU.mult).then_inc(r_out, 1)
                        st.wait()
                        dve.wait_ge(r_out, R2[name] + 1)
                        nc.vector.tensor_tensor(dst[:, :], rope_a[:, :], rope_b[:, :], ALU.add).then_inc(qk_ready, 1)

                    def scaled_split(src, gain, rs, i, ready, count):
                        st.wait(st(nc.vector.scalar_tensor_tensor(out=ytmp[:, :], in0=src[:, :], scalar=gain, in1=rs[:, :],
                                                                  op0=ALU.mult, op1=ALU.mult)))
                        st.wait(st(nc.vector.tensor_copy(act_hi[:, i, :], ytmp[:, :])))
                        nc.vector.tensor_tensor(act_lo[:, i, :], ytmp[:, :], act_hi[:, i, :].bitcast(F32), ALU.subtract) \
                          .then_inc(ready, 1)
                        dve.wait_ge(ready, count)

                    def group_norm(a):
                        dve.wait_ge(rs_ready, SQUARES[f"e{a}"])
                        for i in range(2):
                            t = a - 1 + i
                            scaled_split(ext[i], colp[:, P2_MIX + t:P2_MIX + t + 1], nrm, t, y_ready, t + 1)

                    def gate_logits():
                        t = TILE["gates"]
                        dve.wait_ge(*DONE["gates"])
                        nc.vector.tensor_scalar(sz[0][0:4, :], PT[t % 2][0:4, :], colp[0:4, P2_BF:P2_BF + 1], -1.0,
                                                ALU.add, ALU.mult).then_inc(tile_out[t % 2], 1)

                    def gate_sums():
                        dve.wait_ge(gate_ln, 1)
                        y = sz[0][0:4, :]
                        st.wait(st(nc.vector.scalar_tensor_tensor(out=y, in0=y, scalar=0.0, in1=sz[1][0:4, :],
                                                                  op0=ALU.max, op1=ALU.add)))
                        nc.vector.tensor_tensor_scan(ext[2][0:4, :], y, y, 0.0, ALU.add, ALU.bypass).then_inc(gate_ready, 1)

                    def sb_step(a, j):
                        lo, w = (NB - 1 - j) * P, w_of(a, j)
                        if j == 0:
                            if w:
                                dve.wait_ge(sb_sum, w)
                                dve.wait_ge(sb_cum, w)
                            else:
                                dve.wait_ge(t_ready, u_of(SB0 - 1, NB - 1, 1) + 1)
                            for m in range(2):
                                st(nc.vector.memset(sz[m][:, :], 0.0))
                            st.wait()
                        for m in range(2):
                            dve.wait_ge(sb_ln, w + m + 1)
                            if w + m >= 2:
                                dve.wait_ge(sb_sum, w + m - 1)
                            nc.vector.scalar_tensor_tensor(out=pn[m][:, lo:SEQ], in0=banks(a, j)[m][:, lo:SEQ], scalar=0.0,
                                                           in1=prob[m][:, lo:SEQ], op0=ALU.max, op1=ALU.add).then_inc(sb_sp, 1)
                        for m in range(2):
                            dve.wait_ge(sb_cum, w + m + 1)
                            nc.vector.tensor_tensor(sz[m][:, lo:SEQ], sz[m][:, lo:SEQ], pn[m][:, lo:SEQ], ALU.add) \
                              .then_inc(sb_sum, 1)

                    dve.wait_ge(rs_ready, SQUARES["ckv"])
                    scaled_split(ckv_t, colp[:, P2_GKV:P2_GKV + 1], z_t, 10, latent_ready, 1)
                    for a in range(N_ATT):
                        for qb in range(NB):
                            if KIND[a] == SB:
                                sb_step(a, qb)
                            else:
                                row_max(a, qb, 0)
                                row_max(a, qb, 1)
                                normalise(a, qb)
                            if (a, qb) == (0, 0):
                                dve.wait_ge(rs_ready, SQUARES["cq"])
                                for i in range(2):
                                    scaled_split(cq_t[i], colp[:, P2_GQ + i:P2_GQ + i + 1], sz[0], 8 + i, latent_ready, 2 + i)
                            elif (a, qb) == (0, 3):
                                rotate("kr", 0, z_t, 1)
                            elif (a, qb) == (1, 2):
                                rotate("qr", 1, qr_t, 2)
                            if (a, qb) == (0, 3):
                                gate_logits()
                            elif (a, qb) == (1, 1):
                                gate_sums()
                            late = LATE.get(step_before(a, qb), "")
                            if late[:1] == "e":
                                group_norm(int(late[1]))
                    group_norm(7)

                    def to_residual(g, n_end, scale, sums):
                        c = g % 2
                        cols = slice(c * SEQ, (c + 1) * SEQ)
                        dve.wait_ge(unit_done, n_end)
                        for tb in range(NB):
                            acc = dict(accum_out=small[:, 2 * tb + c:2 * tb + c + 1]) if sums else {}
                            nc.vector.scalar_tensor_tensor(out=x[:, tb, cols], in0=x[:, tb, cols], scalar=scale,
                                                           in1=TOK[tb][:, :], op0=ALU.mult, op1=ALU.add, **acc) \
                              .then_inc(tok_out, 1)
                        dve.wait_ge(tok_out, NB * (g + 1))

                    def layernorm(count):
                        sums = small[:, 0:2 * NB].rearrange("p (b c) -> p b c", c=2)
                        st.wait(st(nc.vector.tensor_reduce(small[:, 52:56], sums, AX.X, ALU.add)))
                        st.wait(st(nc.vector.tensor_scalar(small[:, 52:56], small[:, 52:56], -1.0 / D, None, ALU.mult)))
                        for tb in range(NB):
                            nc.vector.tensor_scalar(x[:, tb, :], x[:, tb, :], small[:, 52 + tb:53 + tb], None, ALU.add) \
                              .then_inc(ln_centre, 1)
                        dve.wait_ge(stat_ready, count)
                        dve.wait_ge(rows_loaded, 16 * count)
                        for tb in range(NB):
                            st.wait(st(nc.vector.scalar_tensor_tensor(out=x[:, tb, :], in0=x[:, tb, :],
                                                                      scalar=small[:, 20 + tb:21 + tb], in1=rowp[:, 0:D],
                                                                      op0=ALU.mult, op1=ALU.mult)))
                            nc.vector.tensor_tensor(x[:, tb, :], x[:, tb, :], rowp[:, D:2 * D], ALU.add).then_inc(ln_done, 1)

                    for c in range(2):
                        to_residual(c, B2_WO + 4 * c + 4, ALPHA, True)
                    layernorm(1)
                    dve.wait_ge(ln_done, NB)
                    xt_lo_sub(dve, KD)
                    for hf in range(2):
                        n0 = B2_FFN + hf * B2_FFN_HALF
                        done = len(B2_TILES) // 2 + FF_HALF * hf
                        dve.wait_ge(unit_done, n0)
                        first = st.n + 1
                        with dve.Fori(0, FF_HALF) as j:
                            dve.wait_ge(tile_out[0], j + (done + 1))
                            dve.wait_ge(unit_done, j * 2 + (n0 + 2))
                            nc.vector.tensor_tensor(ytmp[:, :], nrm[:, :], PT[1][:, :], ALU.mult).then_inc(tile_out[1], 1)
                            dve.wait_ge(tile_out[1], j + (done + 1))
                            hi = act_hi[:, bass.ds(j, 1), :].rearrange("p a t -> p (a t)")
                            lo = act_lo[:, bass.ds(j, 1), :].rearrange("p a t -> p (a t)")
                            nc.vector.tensor_copy(hi, ytmp[:, :]).then_inc(dve_step, 1)
                            dve.wait_ge(dve_step, j + first)
                            nc.vector.tensor_tensor(lo, ytmp[:, :], hi.bitcast(F32), ALU.subtract).then_inc(gu_ready, 1)
                            dve.wait_ge(gu_ready, j + (FF_HALF * hf + 1))
                        st.n += FF_HALF
                        for c in range(2):
                            to_residual(2 + 2 * hf + c, n0 + 2 * FF_HALF + DOWN_UNITS * (c + 1), 1.0 if hf else ALPHA, hf == 1)
                    layernorm(2)
            end_of_stage()

        with nc.Block() as block:
            @block.sync
            def _(sp):
                sp.dma_start(out.rearrange("(b p) d -> p b d", p=P), x[:, :, :]).then_inc(stored, 16)
                sp.wait_ge(stored, 16)


def _t_unit(np, w):
    k = w.shape[0] // P
    u = np.zeros((P, UNIT), w.dtype)
    u[:, :k * P] = w.reshape(k, P, P).transpose(1, 0, 2).reshape(P, k * P)
    return u


def _tok_units(np, w):
    k = w.shape[0] // P
    out = []
    for j in range(0, k, 2):
        u = np.zeros((P, UNIT), w.dtype)
        for i in range(j, min(j + 2, k)):
            u[:, (i - j) * SEQ:(i - j + 1) * SEQ] = w[i * P:(i + 1) * P]
        out.append(u)
    return out


def _block1_units(np, w_in, w_branch, w_out):
    cols = lambda c, n=P: w_in[:, c:c + n]
    units = _tok_units(np, cols(2560, SEQ))
    for g in range(4):
        units += [_t_unit(np, cols(2048 + P * g)), _t_unit(np, cols(3072 + P * g))]
    head = lambda tile, f: _t_unit(np, cols((0, 3584)[f // 4] + SEQ * "qkvz".index(tile) + P * (f % 4)))
    units += [head(tile, 0) for tile in "qkv"]
    for a in range(N_ATT - 1):
        units += [head("q", a + 1), head("k", a + 1), head("z", a), head("v", a + 1)]
    units.append(head("z", N_ATT - 1))
    stream = [part for m in range(KD) for i in range(3)
              for part in (_t_unit(np, cols(5632 + D * i + P * m)), _t_unit(np, w_branch[i][:, P * m:P * m + P])[:, :UNIT // 2])]
    stream = np.concatenate(stream, axis=1)
    units += [stream[:, c:c + UNIT] for c in range(0, stream.shape[1], UNIT)]
    for c in range(2):
        units += _tok_units(np, w_out[:, SEQ * c:SEQ * (c + 1)])
    return np.stack(units)


def _block2_units(np, w_in, w_uq, w_ukv, w_o, w_gate, w_up, w_down):
    cols = lambda c, n=P: w_in[:, c:c + n]
    cat = lambda *a: np.concatenate(a, axis=1)
    q3, kv = w_uq.reshape(2 * P, 4, HD + 32), w_ukv.reshape(P, 4, 2 * HD)
    tiles = {"gates": cat(cols(768, 4), np.zeros((D, P - 4), w_in.dtype)),
             "wk": cols(2212), "wv": cols(2340), "ckv": cols(1028), "cq0": cols(772), "cq1": cols(900),
             "kr": cat(*[cols(1156, 32)] * 4), "uqr": q3[:, :, HD:].reshape(2 * P, P)}
    for i in range(2):
        pair = slice(2 * i, 2 * i + 2)
        tiles |= {f"wq{i}": cat(cols(1956 + HD * i, HD), cols(1956 + HD * (i + 2), HD)),
                  f"uq{i}": q3[:, pair, :HD].reshape(2 * P, P), f"uk{i}": kv[:, pair, :HD].reshape(P, P),
                  f"uv{i}": kv[:, pair, HD:].reshape(P, P)}
        for j, t in enumerate("qkv"):
            tiles |= {f"f{t}{i}": cols(256 * j + P * i), f"s{t}{i}": cols(1188 + 256 * j + P * i)}
    units = []
    for names in B2_PACKED:
        parts = [_t_unit(np, tiles[name])[:, :B2_KT.get(name, KD) * P] for name in names]
        parts.append(np.zeros((P, UNIT - sum(part.shape[1] for part in parts)), w_in.dtype))
        units.append(np.concatenate(parts, axis=1))
    w_o = _mix_order(np, w_o)
    for c in range(2):
        units += _tok_units(np, w_o[:, SEQ * c:SEQ * (c + 1)])
    for hf in range(2):
        for j in range(FF_HALF * hf, FF_HALF * (hf + 1)):
            units += [_t_unit(np, w_gate[:, P * j:P * j + P]), _t_unit(np, w_up[:, P * j:P * j + P])]
        rows = w_down[hf * FF_HALF * P:(hf + 1) * FF_HALF * P]
        for c in range(2):
            units += _tok_units(np, rows[:, SEQ * c:SEQ * (c + 1)])
    return np.stack(units)


def _mix_order(np, a):
    heads = a.reshape(16, HD, *a.shape[1:])
    return heads[[12, 14, 13, 15, 4, 5, 6, 7, 8, 9, 10, 11, 0, 1, 2, 3]].reshape(a.shape)


def _constants(np):
    f = np.float32
    c = np.zeros((P, C_KEEP), f)
    r = np.arange(P)
    c[:, C_IDENT:C_IDENT + P] = np.eye(P)
    c[:, C_ONES:C_ONES + P] = 1
    c[:, C_NTRI:C_NTRI + P] = -(r[:, None] >= r[None, :]).astype(f)
    c[:, C_NONES:C_NONES + P] = -1
    for at, width, half in ((C_ROPE1, HD, HD // 8), (C_ROPE2, 32, 16)):
        for p in range(P):
            d = p % width
            if d < half:
                c[p + half, at + p] = -1
            elif d < 2 * half:
                c[p - half, at + p] = 1
    c[:, C_UPPER:C_UPPER + P] = r[:, None] <= r[None, :]
    for h in range(4):
        c[h, C_SEL + P * h:C_SEL + P * (h + 1)] = 1
    inv = np.power(f(500000.0), -np.arange(8, dtype=f) * f(2.0) / f(16)).astype(f)
    for p in range(P):
        if p % HD < 16:
            c[p, C_INV] = inv[p % 8]
    m = np.zeros((P, M_WIDTH), f)
    m[:, M_CAUSAL:M_CAUSAL + P] = np.where(r[None, :] <= r[:, None], 0, NEG)
    m[:, M_STRICT:M_STRICT + P] = np.where(r[:, None] < r[None, :], 0, NEG)
    rel = r[:, None] - (np.arange(SEQ)[None, :] - (SEQ - P))
    count = (rel <= 128).astype(int) + (rel % 4 == 0) + (rel % 16 == 0)
    m[:, M_MULT:M_MULT + SEQ] = np.where((rel >= 0) & (count > 0), np.log(np.maximum(count, 1)), NEG)
    dist = r[:, None] + P - np.arange(2 * P)[None, :]
    for h in range(4):
        slope = 2.0 ** (-8.0 * (h + 1) / 4)
        m[:, M_SWA + 2 * P * h:M_SWA + 2 * P * (h + 1)] = np.where((dist >= 0) & (dist < 128), -slope * dist, NEG)
    inv2 = f(10000.0) ** (-np.arange(0, 32, 2, dtype=f) / f(32))
    ang = np.arange(SEQ, dtype=f)[None, :] * inv2[r % 16][:, None]
    rope2 = np.stack([np.cos(ang), np.sin(ang)]).astype(f)
    return c, m, rope2


def kernel(**inputs):
    import numpy as np
    import concourse.bacc as bacc
    from concourse.bass_utils import run_bass_kernel_spmd

    a = {k: np.asarray(v) for k, v in inputs.items()}
    f = a["x"].dtype
    c, m, rope2 = _constants(np)
    w1 = np.stack([_block1_units(np, a["w_in"][l], a["w_branch"][l], a["w_out"][l]) for l in range(DEPTH)])
    w2 = np.stack([_block2_units(np, a["w_in_2"][l], a["mla_w_uq_2"][l], a["mla_w_ukv_2"][l], a["w_o_2"][l],
                                 a["w_gate_2"][l], a["w_up_2"][l], a["w_down_2"][l]) for l in range(DEPTH)])
    rows = lambda v: np.broadcast_to(v.reshape(1, -1), (P, v.size))
    col1, row1, col2, row2 = [], [], [], []
    for l in range(DEPTH):
        lam_init = 0.8 - 0.6 * math.exp(-0.3 * l)
        col1.append(np.concatenate([
            a["norm_g"][l].reshape(KD, P).T, a["subln_g"][l].reshape(P, 1),
            rows(a["lam_q1"][l]), rows(a["lam_k1"][l]), rows(a["lam_q2"][l]), rows(a["lam_k2"][l]),
            np.full((P, 1), lam_init, f), np.full((P, 1), 1.0 - lam_init, f)], axis=1))
        row1.append(np.concatenate([
            rows(a["sgu_ln_g"][l]), rows(a["sgu_ln_b"][l]), rows(a["sgu_b"][l]),
            a["sgu_w"][l].transpose(2, 0, 1).reshape(P, SEQ)], axis=1))
        fox_b = np.zeros((P, 1), f)
        fox_b[:4, 0] = a["fox_b_f_2"][l]
        mix_g = _mix_order(np, a["mix_g_2"][l])
        col2.append(np.concatenate([
            a["mla_g_q_2"][l].reshape(2, P).T, a["mla_g_kv_2"][l].reshape(P, 1), mix_g.reshape(KD, P).T,
            fox_b, rows(a["swa_sinks_2"][l])], axis=1))
        row2.append(np.stack([np.concatenate([rows(a[g][l]), rows(a[b][l])], axis=1)
                              for g, b in (("ln1_g_2", "ln1_b_2"), ("ln2_g_2", "ln2_b_2"))]))
    arrays = {
        "x_dram": a["x"].reshape(SEQ, D), "pos_dram": a["positions"].reshape(1, SEQ), "const_dram": c, "mask_dram": m,
        "rope2_dram": rope2, "w1_dram": w1, "col1_dram": np.stack(col1), "row1_dram": np.stack(row1),
        "final_dram": a["final_g"].reshape(1, D), "w2_dram": w2, "col2_dram": np.stack(col2), "row2_dram": np.stack(row2),
    }
    arrays = {k: np.ascontiguousarray(v) for k, v in arrays.items()}
    nc = bacc.Bacc("TRN2", target_bir_lowering=False, num_devices=1)
    aps = [nc.dram_tensor(k, v.shape, mybir.dt.from_np(v.dtype), kind="ExternalInput").ap() for k, v in arrays.items()]
    out = nc.dram_tensor("out_dram", (SEQ, D), F32, kind="ExternalOutput").ap()
    program(nc, *aps, out)
    r = run_bass_kernel_spmd(nc, [arrays], core_ids=[0])
    return r.results[0]["out_dram"].reshape(1, SEQ, D)
```

```python
import math
from contextlib import ExitStack

import concourse.bass as bass
from concourse import mybir

F32 = mybir.dt.float32
F32R = mybir.dt.float32r
I32 = mybir.dt.int32
ALU = mybir.AluOpType
ACT = mybir.ActivationFunctionType
AX = mybir.AxisListType

DEPTH = 2
SEQ = 512
D = 1024
P = 128
NB = SEQ // P
KD = D // P
UNIT = 1024
RAW = 4
AHEAD = 2
EPS = 1e-6
LN_EPS = 1e-5
ALPHA = (2.0 * DEPTH) ** 0.25
NEG = -(2.0 ** 100)
HD = 64

B1_V = 0
B1_UZ = 4
B1_HEADS = 12
B1_GATE = 44
GATE_TURN = 4
B1_OUT = 80
B1_UNITS = 88
N_ATT = 8
N_A = 4

B2_PACKED = (("wq0",), ("wk",), ("wv",), ("ckv",), ("cq0",), ("cq1",), ("wq1",), ("kr",), ("gates",),
             ("uq0", "uqr", "uk0", "uv0"), ("sq1",), ("sk1",), ("uq1", "uk1", "uv1"), ("sq0",), ("sk0",), ("sv0",), ("fq0",), ("fk0",),
             ("sv1",), ("fq1",), ("fk1",), ("fv0",), ("fv1",))
B2_TILES = tuple(name for unit in B2_PACKED for name in unit)
B2_KT = {"uq0": 2, "uq1": 2, "uqr": 2, "uk0": 1, "uk1": 1, "uv0": 1, "uv1": 1}
B2_WO = len(B2_PACKED)
FF_PARTS = (12, 10)
FF_FIRST = (0, FF_PARTS[0])
B2_FFN = B2_WO + 8
B2_PART = (B2_FFN, B2_FFN + 3 * FF_PARTS[0])
B2_UNITS = B2_FFN + 3 * sum(FF_PARTS)

C_IDENT, C_ONES, C_NTRI, C_NONES, C_ROPE1, C_ROPE2, C_UPPER = (P * i for i in range(7))
C_SEL = 7 * P
C_INV = C_SEL + 4 * P
C_KEEP = C_INV + 8
M_CAUSAL, M_STRICT = 0, P
M_MULT = 2 * P
M_WIDTH = M_MULT + SEQ

P1_NORM, P1_SUBLN, P1_LAM, P1_INIT, P1_KEEP = 0, 8, 9, 9 + 4 * HD, 10 + 4 * HD
P1_COLS = 11 + 4 * HD
P2_GQ, P2_GKV, P2_MIX, P2_BF, P2_SINK = 0, 2, 3, 11, 12
P2_GIN, P2_BIN, P2_G1, P2_B1 = 16, 24, 32, 40
P2_COLS = 48
COLS = max(P1_COLS, P2_COLS)
ROWP = 2048


class Steps:

    def __init__(self, eng, sem):
        self.eng, self.sem, self.n = eng, sem, 0

    def __call__(self, ins):
        ins.then_inc(self.sem, 1)
        self.n += 1
        return self.n

    def wait(self, value=None):
        self.eng.wait_ge(self.sem, self.n if value is None else value)


def program(nc, x_in, pos_in, const_in, mask_in, swa_in, rope2_in, col_in, w_in, row1_in,
            row2_in, out):
    ctx = ExitStack()
    with ctx:
        base = nc.sbuf_base
        top = [(base + 31) // 32 * 32]
        addr = {}

        def sb(name, shape, dt=F32, at=None):
            size = 4
            for s in shape[1:]:
                size *= s
            offset = top[0] if at is None else at
            addr[name] = offset
            if at is None:
                top[0] += (size + 31) // 32 * 32
            return nc.alloc_sbuf_tensor_at(name, shape, dt, offset=offset)

        def sem(name):
            return ctx.enter_context(nc.semaphore(name))

        x = sb("x", [P, NB, D])
        h_hi = sb("h_hi", [P, KD, SEQ], F32R)
        h_lo = sb("h_lo", [P, KD, SEQ], F32R)
        raw_w = [sb(f"raw_w{s}", [P, UNIT]) for s in range(RAW)]
        w_hi = [sb(f"w_hi{s}", [P, UNIT], F32R) for s in range(2)]
        w_lo = [sb(f"w_lo{s}", [P, UNIT], F32R) for s in range(2)]
        act_hi = sb("act_hi", [P, 12, SEQ], F32R)
        act_lo = sb("act_lo", [P, 12, SEQ], F32R)
        const = sb("const", [P, C_KEEP])
        ident_r = sb("ident_r", [P, P], F32R)
        causal_r = sb("causal_r", [P, P], F32R)
        sbmask_r = sb("sbmask_r", [P, P], F32R)
        m2_hi = sb("m2_hi", [P, SEQ], F32R)
        m2_lo = sb("m2_lo", [P, SEQ], F32R)
        swa_r = sb("swa_r", [P, 4, 2 * P], F32R)
        swa_raw = sb("swa_raw", [P, 8 * P], at=addr["swa_r"])
        cos = sb("cos", [P, SEQ])
        sin = sb("sin", [P, SEQ])
        rowp = sb("rowp", [P, ROWP])
        colp = sb("colp", [P, COLS])
        small = sb("small", [P, 64])
        ext = [sb(f"ext{i}", [P, SEQ]) for i in range(4)]
        junk = sb("junk", [P, D], at=addr["ext0"])
        shared = top[0]
        qs = [sb(f"qs{i}", [P, SEQ]) for i in range(2)]
        ks = [sb(f"ks{i}", [P, SEQ]) for i in range(2)]
        vs = [sb(f"vs{i}", [P, NB, P]) for i in range(2)]
        raw_t = [sb(f"raw_t{i}", [P, SEQ]) for i in range(2)]
        prob = [sb(f"prob{i}", [P, SEQ]) for i in range(2)]
        pn = [sb(f"pn{i}", [P, SEQ]) for i in range(2)]
        pT = [sb(f"pT{i}", [P, SEQ]) for i in range(2)]
        sz = [sb(f"sz{i}", [P, SEQ]) for i in range(2)]
        z_t = sb("z_t", [P, SEQ])
        nrm = sb("nrm", [P, SEQ])
        rope_a = sb("rope_a", [P, SEQ])
        rope_b = sb("rope_b", [P, SEQ])
        ytmp = sb("ytmp", [P, SEQ])
        masks = sb("masks", [P, M_WIDTH], at=addr["prob0"])
        hn = sb("hn", [P, NB, D], at=shared)
        mrg_hi = sb("mrg_hi", [P, KD, SEQ], F32R, at=shared)
        mrg_lo = sb("mrg_lo", [P, KD, SEQ], F32R, at=shared + KD * SEQ * 4)
        rowp_at, m2_at = addr["rowp"], addr["m2_hi"]
        wq_t = [sb(f"wq_t{i}", [P, SEQ], at=rowp_at + 4 * SEQ * i) for i in range(2)]
        wk_t = sb("wk_t", [P, SEQ], at=rowp_at + 8 * SEQ)
        ckv_t = sb("ckv_t", [P, SEQ], at=rowp_at + 12 * SEQ)
        cq_t = [sb(f"cq_t{i}", [P, SEQ], at=m2_at + 4 * SEQ * i) for i in range(2)]
        qr_t = sb("qr_t", [P, SEQ], at=addr["act_hi"] + 11 * 4 * SEQ)

        ps = [ctx.enter_context(nc.psum_tensor(f"bank{i}", [P, SEQ], F32)) for i in range(8)]
        PT, S, T, R, O = ps[0:2], ps[2:4], ps[4:6], ps[6], ps[7]
        TOK = ps[2:6]
        OTHERS = (*PT, R, O)

        sel_r = sb("sel_r", [P, 4 * P], F32R, at=addr["m2_lo"])
        cum_r = sb("cum_r", [P, SEQ], F32R, at=addr["ext2"])
        ext_r = [sb(f"ext_r{i}", [P, SEQ], F32R, at=addr[f"ext{i}"]) for i in range(1, 4)]
        q_two = [[act_hi[:, 10 + m, :] for m in range(2)], [sb("q_two", [P, SEQ], F32R, at=addr["qs1"]), ext_r[0]]]
        k_two = [[act_lo[:, 10 + m, :] for m in range(2)], ext_r[1:3]]
        k_lo = [sb(f"k_lo{i}", [P, SEQ], F32R, at=addr[f"ks{i}"]) for i in range(2)]
        q_lo = sb("q_lo", [P, SEQ], F32R, at=addr["qs0"])
        qk_hi = sb("qk_hi", [P, SEQ], F32R, at=addr["rope_b"])
        hi_rest = (rope_a, rope_b)
        sq_tmp = rope_b
        row_in = sb("row_in", [P, 2 * D], at=addr["act_hi"] + 4 * 4 * SEQ)

        ident = const[:, C_IDENT:C_IDENT + P]
        ones = const[:, C_ONES:C_ONES + P]
        neg_tri = const[:, C_NTRI:C_NTRI + P]
        neg_ones = const[:, C_NONES:C_NONES + P]
        rope1 = const[:, C_ROPE1:C_ROPE1 + P]
        rope2 = const[:, C_ROPE2:C_ROPE2 + P]

        raw_loaded = [sem(f"raw_loaded{s}") for s in range(RAW)]
        params_loaded = sem("params_loaded")
        cols_loaded = sem("cols_loaded")
        ahead_loaded = [sem(f"ahead_loaded{s}") for s in range(AHEAD)]
        rows_loaded = sem("rows_loaded")
        hi_split = sem("hi_split")
        split_done = sem("split_done")
        small_done = sem("small_done")
        unit_done = sem("unit_done")
        tile_out = [sem(f"tile_out{b}") for b in range(2)]
        tok_ready = sem("tok_ready")
        tok_out = sem("tok_out")
        inv_loaded = sem("inv_loaded")
        masks_loaded = sem("masks_loaded")
        rms_ready = sem("rms_ready")
        norm_in = sem("norm_in")
        xt_ready = sem("xt_ready")
        xt_hi = sem("xt_hi")
        xt_rest = sem("xt_rest")
        xt_lo = sem("xt_lo")
        r_ready = sem("r_ready")
        r_out = sem("r_out")
        qk_ready = sem("qk_ready")
        qk_placed = sem("qk_placed")
        qk_copied = sem("qk_copied")
        scores_ready = sem("scores_ready")
        max_ready = sem("max_ready")
        probs_ready = sem("probs_ready")
        probs_normed = sem("probs_normed")
        t_ready = sem("t_ready")
        t_out = sem("t_out")
        pv_done = sem("pv_done")
        o_out = sem("o_out")
        sq_ready = sem("sq_ready")
        rs_ready = sem("rs_ready")
        z_ready = sem("z_ready")
        v_ready = sem("v_ready")
        vb_ready = sem("vb_ready")
        y_ready = sem("y_ready")
        merged = sem("merged")
        stat_ready = sem("stat_ready")
        lam_exp = sem("lam_exp")
        gate_ready = sem("gate_ready")
        latent_ready = sem("latent_ready")
        sb_scores = sem("sb_scores")
        sb_ln = sem("sb_ln")
        sb_sp = sem("sb_sp")
        sb_cum = sem("sb_cum")
        sb_sum = sem("sb_sum")
        sb_prob = sem("sb_prob")
        ln_done = sem("ln_done")
        ln_centre = sem("ln_centre")
        swa_loaded = sem("swa_loaded")
        swa_ready = sem("swa_ready")
        gain_done = sem("gain_done")
        sq_parts = sem("sq_parts")
        gate_ln = sem("gate_ln")
        gu_ready = sem("gu_ready")
        dve_step = sem("dve_step")
        act_step = sem("act_step")
        stored = sem("stored")
        sems = range(raw_loaded[0].num, stored.num + 1)
        engines = [e.engine for e in (nc.sync, nc.gpsimd, nc.scalar, nc.vector, nc.tensor)]

        def end_of_stage():
            nc.multi_engine_barrier(engines, sems_to_clear=sems)

        def load_units(sp, w_layer, units, after_first=None):
            def one(n, s, i):
                if not (isinstance(i, int) and i == 0):
                    unit_split(sp, n - RAW)
                sp.dma_start(raw_w[s][:, :], w_layer[bass.ds(n, 1), :, :].rearrange("a p c -> p (a c)")) \
                  .then_inc(raw_loaded[s], 16)
            for s in range(AHEAD, RAW):
                one(s, s, 0)
            if after_first:
                after_first()
            with sp.Fori(1, units // RAW) as i:
                for s in range(RAW):
                    one(i * RAW + s, s, i)
            for s in range(units % RAW):
                one(units // RAW * RAW + s, s, units // RAW)

        def next_layer(sp, n, n0, first=0):
            for s in range(first, AHEAD):
                sp.dma_start(raw_w[s][:, :], w_in[bass.ds(n0 + s, 1), :, :].rearrange("a p c -> p (a c)")) \
                  .then_inc(ahead_loaded[s], 16)
            sp.dma_start(colp[:, :], col_in[bass.ds(n, 1), :, :].rearrange("l p c -> p (l c)")).then_inc(cols_loaded, 16)
            for s in range(AHEAD):
                sp.wait_ge(ahead_loaded[s], 16)
            sp.wait_ge(cols_loaded, 16)

        def unit_split(eng, n):
            if not (isinstance(n, int) and n == 0):
                eng.wait_ge(split_done, n)

        def split(pool, s, hi_count):
            nc.gpsimd.tensor_tensor(w_hi[s % 2][:, :], raw_w[s][:, :], ones[:, 0:1].to_broadcast([P, UNIT]), ALU.mult) \
              .then_inc(hi_split, 1)
            pool.wait_ge(hi_split, hi_count)
            return nc.gpsimd.tensor_tensor(w_lo[s % 2][:, :], raw_w[s][:, :], w_hi[s % 2][:, :].bitcast(F32), ALU.subtract)

        def split_units(pool, units):
            def one(n, s, i):
                if s >= AHEAD:
                    pool.wait_ge(raw_loaded[s], (i + 1) * 16)
                elif not (isinstance(i, int) and i == 0):
                    pool.wait_ge(raw_loaded[s], i * 16)
                if not (isinstance(n, int) and n < 2):
                    pool.wait_ge(unit_done, n - 1)
                split(pool, s, n).then_inc(split_done, 1)
            for s in range(1, RAW):
                one(s, s, 0)
            with pool.Fori(1, units // RAW) as i:
                for s in range(RAW):
                    one(i * RAW + s, s, i)
            for s in range(units % RAW):
                one(units // RAW * RAW + s, s, units // RAW)
            pool.wait_ge(ahead_loaded[0], 16)
            pool.wait_ge(unit_done, units - 1 + units % 2)
            split(pool, 0, units)

        def mm3(dst, lh, ll, rh, rl, start, stop):
            nc.tensor.matmul(dst, lh, rh, start=start, stop=False)
            nc.tensor.matmul(dst, ll, rh, start=False, stop=False)
            return nc.tensor.matmul(dst, lh, rl, start=False, stop=stop)

        def tile_part(pe, n, before, half, slot, kt=KD, mov=None, bank=None, at=0, done=unit_done,
                      split_from=None):
            m_hi, m_lo = mov if mov else (h_hi, h_lo)
            b = slot if bank is None else bank
            if half == 0:
                unit_split(pe, n)
                if not (isinstance(before, int) and before == 0):
                    pe.wait_ge(tile_out[b], before)
            wh = w_hi[slot][:, :].rearrange("p (k c) -> p k c", c=P)
            wl = w_lo[slot][:, :].rearrange("p (k c) -> p k c", c=P)
            cut = (kt + 1) // 2
            for k in (range(cut) if half == 0 else range(cut, kt)):
                if split_from is not None:
                    pe.wait_ge(xt_lo, split_from + k + 1)
                last = mm3(PT[b][:, :], wh[:, at + k, :], wl[:, at + k, :], m_hi[:, k, :], m_lo[:, k, :],
                           k == 0, k == kt - 1)
            if half == 1 or kt == 1:
                last.then_inc(done, 1)

        def tok_unit(pe, n0, j, units, kts, st_hi, st_lo, before):
            unit_split(pe, n0 + j)
            s = (n0 + j) % 2
            wh = w_hi[s][:, :].rearrange("p (k c) -> p k c", c=SEQ)
            wl = w_lo[s][:, :].rearrange("p (k c) -> p k c", c=SEQ)
            for tb in range(NB):
                if j == 0 and before:
                    pe.wait_ge(tok_out, before - NB + tb + 1)
                cols = slice(tb * P, (tb + 1) * P)
                for k in range(2 * j, min(2 * j + 2, kts)):
                    last = mm3(TOK[tb][:, :], st_hi[:, k, cols], st_lo[:, k, cols],
                               wh[:, k - 2 * j, :], wl[:, k - 2 * j, :], k == 0, k == kts - 1)
                if j == units - 1 and tb < NB - 1:
                    last.then_inc(tok_ready, 1)
            last.then_inc(unit_done, 1)

        def tok_group(pe, n0, units, kts, st_hi, st_lo, before, operand=None):
            for j in range(units):
                if operand:
                    pe.wait_ge(operand[0], operand[1] + min(2 * j + 2, kts))
                tok_unit(pe, n0, j, units, kts, st_hi, st_lo, before)

        def tok_wait(dve, g, tb, n_end):
            if tb < NB - 1:
                dve.wait_ge(tok_ready, (NB - 1) * g + tb + 1)
            else:
                dve.wait_ge(unit_done, n_end)

        def transpose_block(src, tb, banks):
            for k in range(4):
                nc.tensor.transpose(banks[k][:, tb * P:(tb + 1) * P], src[:, tb, k * P:(k + 1) * P], ident)

        def transpose_in(pe, src, k0, banks, k_tiles=range(KD)):
            for k in k_tiles:
                if k >= 4:
                    pe.wait_ge(xt_lo, k0 + k - 3)
                for tb in range(0 if k >= 4 else NB - 1, NB):
                    last = nc.tensor.transpose(banks[k % 4][:, tb * P:(tb + 1) * P],
                                               src[:, tb, k * P:(k + 1) * P], ident)
                last.then_inc(xt_ready, 1)

        def xt_hi_copy(act, k0, banks, gain, bias=None):
            for k in range(KD):
                act.wait_ge(xt_ready, k0 + k + 1)
                hi, src, g = h_hi[:, k, :], banks[k % 4][:, :], gain[:, k:k + 1]
                if bias is None:
                    nc.scalar.activation(hi, src, ACT.Copy, scale=g).then_inc(xt_hi, 1)
                    continue
                nc.scalar.activation(hi, src, ACT.Identity, scale=g, bias=bias[:, k:k + 1]).then_inc(xt_hi, 1)
                if k % 2:
                    act.wait_ge(xt_hi, k0 + k + 1)
                    if k >= 2:
                        act.wait_ge(xt_lo, k0 + k - 1)
                    nc.scalar.activation(hi_rest[1][:, :], hi.bitcast(F32), ACT.Identity, scale=-1.0, bias=bias[:, k:k + 1]) \
                      .then_inc(xt_rest, 1)

        def xt_lo_sub(dve, st, k0, banks, gain, bias=None):
            for k in range(KD):
                dve.wait_ge(xt_hi, k0 + k + 1)
                rest, op = h_hi[:, k, :].bitcast(F32), ALU.subtract
                if bias is not None and k % 2:
                    dve.wait_ge(xt_rest, (k0 + k + 1) // 2)
                    rest, op = hi_rest[1][:, :], ALU.add
                elif bias is not None:
                    if k >= 2:
                        dve.wait_ge(xt_lo, k0 + k - 1)
                    st.wait(st(nc.vector.tensor_scalar(hi_rest[0][:, :], rest, bias[:, k:k + 1], None, ALU.subtract)))
                    rest = hi_rest[0][:, :]
                nc.vector.scalar_tensor_tensor(out=h_lo[:, k, :], in0=banks[k % 4][:, :], scalar=gain[:, k:k + 1], in1=rest,
                                               op0=ALU.mult, op1=op).then_inc(xt_lo, 1)

        def rms(st, tb):
            st.wait(st(nc.scalar.activation(junk[:, :], x[:, tb, :], ACT.Square, accum_out=small[:, 56 + tb:57 + tb])))
            st.wait(st(nc.scalar.activation(small[:, 60 + tb:61 + tb], small[:, 56 + tb:57 + tb], ACT.Ln, scale=1.0 / D, bias=EPS)))
            nc.scalar.activation(small[:, tb:tb + 1], small[:, 60 + tb:61 + tb], ACT.Exp, scale=-0.5).then_inc(rms_ready, 1)

        def normalise_in(dve, tb):
            dve.wait_ge(rms_ready, tb + 1)
            nc.vector.tensor_scalar(hn[:, tb, :], x[:, tb, :], small[:, tb:tb + 1], None, ALU.mult).then_inc(norm_in, 1)

        with nc.Block() as block:
            @block.sync
            def _(sp):
                sp.dma_start(z_t[:, :].bitcast(I32), pos_in.partition_broadcast(P)).then_inc(rows_loaded, 16)
                sp.dma_start(const[:, C_INV:C_KEEP], const_in[:, C_INV:C_KEEP]).then_inc(inv_loaded, 16)
                sp.dma_start(const[:, 0:C_INV], const_in[:, 0:C_INV]).then_inc(params_loaded, 16)
                for tb in range(NB):
                    if tb == NB // 2:
                        sp.dma_start(raw_w[0][:, :], w_in[0, :, :]).then_inc(ahead_loaded[0], 16)
                    sp.dma_start(x[:, tb, :], x_in[tb * P:(tb + 1) * P, :]).then_inc(raw_loaded[tb], 16)
                sp.dma_start(masks[:, :], mask_in).then_inc(masks_loaded, 16)
                next_layer(sp, 0, 0, 1)

            @block.gpsimd
            def _(pool):
                pool.wait_ge(params_loaded, 16)
                pool.wait_ge(ahead_loaded[0], 16)
                split(pool, 0, 1)

            @block.tensor
            def _(pe):
                pe.wait_ge(params_loaded, 16)
                for tb in range(NB - 1):
                    pe.wait_ge(norm_in, tb + 1)
                    transpose_block(hn, tb, OTHERS)

            @block.vector
            def _(dve):
                st = Steps(dve, dve_step)
                dve.wait_ge(rows_loaded, 16)
                dve.wait_ge(inv_loaded, 16)
                st.wait(st(nc.vector.tensor_copy(nrm[:, :], z_t[:, :].bitcast(I32))))
                st.wait(st(nc.vector.tensor_scalar(rope_a[:, :], nrm[:, :], const[:, C_INV:C_INV + 1], None, ALU.mult)))
                big = 1.5 * 2.0 ** 23
                st.wait(st(nc.vector.tensor_scalar(nrm[:, :], rope_a[:, :], 1.0 / (2 * math.pi), big,
                                                   ALU.mult, ALU.add)))
                st.wait(st(nc.vector.tensor_scalar(nrm[:, :], nrm[:, :], big, None, ALU.subtract)))
                two_pi = 2 * math.pi
                p1 = 6.28125
                p2 = math.floor((two_pi - p1) * 2.0 ** 21) / 2.0 ** 21
                p3 = two_pi - p1 - p2
                for part in (p1, p2, p3):
                    st.wait(st(nc.vector.scalar_tensor_tensor(out=rope_a[:, :], in0=nrm[:, :], scalar=-part,
                                                              in1=rope_a[:, :], op0=ALU.mult, op1=ALU.add)))
                st.wait(st(nc.vector.tensor_scalar(rope_a[:, :], rope_a[:, :], math.pi, -math.pi, ALU.min, ALU.max)))
                st.wait(st(nc.vector.tensor_scalar(rope_b[:, :], rope_a[:, :], -1.0, None, ALU.mult)))
                st.wait(st(nc.vector.tensor_tensor(rope_b[:, :], rope_a[:, :], rope_b[:, :], ALU.max)))
                nc.vector.tensor_scalar(rope_b[:, :], rope_b[:, :], -1.0, math.pi / 2, ALU.mult, ALU.add) \
                  .then_inc(qk_ready, 1)
                dve.wait_ge(params_loaded, 16)
                st(nc.vector.tensor_copy(ident_r[:, :], ident))
                for tb in range(NB):
                    normalise_in(dve, tb)
                dve.wait_ge(masks_loaded, 16)
                st(nc.vector.tensor_copy(causal_r[:, :], masks[:, M_CAUSAL:M_CAUSAL + P]))
                st(nc.vector.tensor_copy(sbmask_r[:, :], masks[:, M_STRICT:M_STRICT + P]))
                m2 = masks[:, M_MULT:M_MULT + SEQ]
                st.wait(st(nc.vector.tensor_copy(m2_hi[:, :], m2)))
                nc.vector.tensor_tensor(m2_lo[:, :], m2, m2_hi[:, :].bitcast(F32), ALU.subtract)

            @block.scalar
            def _(act):
                st = Steps(act, act_step)
                nc.scalar.preload_act_table_set("natural_log_exp_and_others")
                for tb in range(NB):
                    act.wait_ge(raw_loaded[tb], 16)
                    rms(st, tb)
                act.wait_ge(qk_ready, 1)
                nc.scalar.activation(sin[:, :], rope_a[:, :], ACT.Sin)
                nc.scalar.activation(cos[:, :], rope_b[:, :], ACT.Sin)
                nc.scalar.preload_act_table_set("natural_log_exp_and_others")
        end_of_stage()

        def head_block_order(heads, blocks, by_head):
            if by_head:
                return [(m, b) for m in range(heads) for b in blocks]
            return [(m, b) for b in blocks for m in range(heads)]

        def t_index(a, qb, m, paired_from):
            return 4 * a + qb if a < paired_from else 4 * paired_from + 8 * (a - paired_from) + 2 * qb + m

        def before1(n):
            return (n - 4) // 2

        LAST = N_ATT - 1
        PLACED = 2 * 16
        gelu_u = (sz[0], pn[0])

        def head_unit(tile, f):
            if (tile, f) == ("q", 1) or f == 0 and tile != "z":
                return B1_HEADS + (3 if f else "qkv".index(tile))
            if tile == "z":
                return B1_HEADS + (4 * f + 6 if f < LAST else 4 * f + 3)
            return B1_HEADS + {"q": 4 * f - 1, "k": 4 * f, "v": 4 * f + 1}[tile]

        def fill_of(a, qb):
            if a == LAST:
                return ("z", a) if qb == 0 else None
            tile, f = (("k", a + 1), ("v", a + 1), ("z", a), ("q", a + 2))[qb]
            return (tile, f) if f <= LAST else None

        LATE1 = {}
        for a in range(N_ATT):
            if a < LAST:
                LATE1[a, 0], LATE1[a, 1], LATE1[a, 2] = ("q", a + 1), ("k", a + 1), ("v", a + 1)
            if 1 <= a <= N_A:
                LATE1[a, 3] = ("sum", a - 1)
        R1 = {use: i for i, use in enumerate([("mix", g) for g in range(4)] + [("q", 0), ("k", 0), ("v", 0)]
                                             + [LATE1[key] for key in sorted(LATE1)])}

        def banks1(a, qb):
            return PT if (a, qb) == (LAST, NB - 1) else S

        def steps_back(a, qb, n):
            i = NB * a + qb - n
            return divmod(i, NB) if i >= 0 else None

        TURN_UNITS = GATE_TURN * 3 * (KD + 4) // KD
        GATE_BANK, PROJ_BANK = (PT[0], S[0], R), (PT[1], S[1], O)

        def gate_at(mm, i):
            return (3 * mm + i) * (KD + 4)

        def gate_units(at, kts):
            return (at + kts - 1) // KD + 1

        def ti1(a, qb, m):
            return t_index(a, qb, m, N_A)

        with nc.Fori(0, DEPTH) as layer:
            with nc.Block() as block:
                w_layer = w_in[bass.ds(layer * B1_UNITS, B1_UNITS), :, :]

                @block.sync
                def _(sp):
                    def load_rows():
                        sp.dma_start(rowp[:, :], row1_in[bass.ds(layer, 1), :, :].rearrange("l p c -> p (l c)")) \
                          .then_inc(rows_loaded, 16)

                    load_units(sp, w_layer, B1_UNITS, load_rows)
                    sp.wait_ge(xt_hi, KD)
                    sp.wait_ge(merged, KD)
                    sp.wait_ge(split_done, B1_UNITS - 1)
                    next_layer(sp, layer + 1, layer * B1_UNITS + B1_UNITS)

                @block.gpsimd
                def _(pool):
                    split_units(pool, B1_UNITS)

                @block.tensor
                def _(pe):
                    transpose_in(pe, hn, 0, OTHERS, range(4))
                    for j in range(4):
                        unit_split(pe, B1_V + j)
                        pe.wait_ge(xt_lo, 2 * j + 2)
                        s = j % 2
                        wh = w_hi[s][:, :].rearrange("p (k c) -> p k c", c=SEQ)
                        wl = w_lo[s][:, :].rearrange("p (k c) -> p k c", c=SEQ)
                        for tb in range(NB):
                            for k in (2 * j, 2 * j + 1):
                                last = mm3(TOK[tb][:, :], h_hi[:, k, tb * P:(tb + 1) * P], h_lo[:, k, tb * P:(tb + 1) * P],
                                           wh[:, k - 2 * j, :], wl[:, k - 2 * j, :], k == 0, k == KD - 1)
                            if j < 2 and tb % 2:
                                transpose_in(pe, hn, 0, OTHERS, (4 + 2 * j + tb // 2,))
                        last.then_inc(unit_done, 1)

                    def mix(g):
                        pe.wait_ge(vb_ready, 2 * NB)
                        if g:
                            pe.wait_ge(r_out, g)
                        for c in range(NB):
                            last = nc.tensor.matmul(R[:, c * P:(c + 1) * P], ext[c][:, g * P:(g + 1) * P],
                                                    rowp[:, 3 * SEQ + g * P:3 * SEQ + (g + 1) * P], start=True, stop=True)
                        last.then_inc(r_ready, 1)

                    for g in range(4):
                        for j in range(2):
                            n = B1_UZ + 2 * g + j
                            for half in range(2):
                                tile_part(pe, n, before1(n), half, n % 2)
                        if g:
                            mix(g - 1)
                    mix(3)

                    def raw_wait(tile, f):
                        n = head_unit(tile, f)
                        pe.wait_ge(tile_out[n % 2], before1(n) + 1)
                        pe.wait_ge(r_out, R1[tile, f])

                    def rope(tile, f):
                        raw_wait(tile, f)
                        nc.tensor.matmul(R[:, :], rope1, raw_t["qk".index(tile)][:, :], start=True, stop=True).then_inc(r_ready, 1)

                    def v_transpose(f):
                        raw_wait("v", f)
                        for b in range(NB):
                            last = nc.tensor.transpose(R[:, b * P:(b + 1) * P], raw_t[0][:, b * P:(b + 1) * P], ident)
                        last.then_inc(r_ready, 1)

                    def sum_squares(a):
                        pe.wait_ge(sq_ready, a + 1)
                        pe.wait_ge(r_out, R1["sum", a])
                        nc.tensor.matmul(R[:, :], ones, nrm[:, :], start=True, stop=True).then_inc(r_ready, 1)

                    def scores(a, qb):
                        u, nk = 8 * a + 2 * qb, (qb + 1) * P
                        i, bank, block_q = a % 2, banks1(a, qb), slice(qb * P, (qb + 1) * P)
                        if qb == 0:
                            pe.wait_ge(qk_placed, PLACED * (2 * a + 2))
                            pe.wait_ge(qk_copied, 2 * (2 * a + 2))
                        if bank is PT:
                            for t in range(2):
                                pe.wait_ge(tile_out[t], before1(B1_GATE))
                        for m in range(2):
                            if u and bank is S:
                                pe.wait_ge(probs_ready, u - 1 + m)
                            nc.tensor.matmul(bank[m][:, 0:nk], q_two[i][m][:, block_q], k_two[i][m][:, 0:nk], start=True, stop=False)
                        for m in range(2):
                            rows = slice(HD * m, HD * m + HD)
                            nc.tensor.matmul(bank[m][:, 0:nk], q_two[i][m][rows, block_q], k_lo[i][rows, 0:nk], start=False, stop=False)
                        for m in range(2):
                            if a < N_A:
                                last = nc.tensor.matmul(bank[m][:, nk - P:nk], ident_r[:, :], causal_r[:, :], start=False, stop=True)
                            else:
                                nc.tensor.matmul(bank[m][:, 0:nk], ident_r[:, :], m2_hi[:, SEQ - nk:SEQ], start=False, stop=False)
                                last = nc.tensor.matmul(bank[m][:, 0:nk], ident_r[:, :], m2_lo[:, SEQ - nk:SEQ],
                                                        start=False, stop=True)
                            last.then_inc(scores_ready, 1)

                    def transposes(a, qb):
                        pe.wait_ge(probs_normed, 4 * a + qb + 1)
                        for m in range(1 if a < N_A else 2):
                            i = ti1(a, qb, m)
                            if i >= 2:
                                pe.wait_ge(t_out, i - 1)
                            for b in range(qb + 1):
                                last = nc.tensor.transpose(T[i % 2][:, b * P:(b + 1) * P], pn[m][:, b * P:(b + 1) * P], ident)
                            last.then_inc(t_ready, 1)

                    def pv(a, qb):
                        if qb == 0:
                            pe.wait_ge(r_out, R1["v", a] + 1)
                            if a:
                                pe.wait_ge(o_out, a)
                        cols = slice(qb * P, (qb + 1) * P)
                        for m, b in head_block_order(1 if a < N_A else 2, range(qb + 1), a == LAST):
                            if b == 0:
                                pe.wait_ge(t_out, ti1(a, qb, m) + 1)
                            rows = slice(0, P) if a < N_A else slice(HD * m, HD * m + HD)
                            last = nc.tensor.matmul(O[rows, cols], vs[a % 2][:, b, rows],
                                                    pT[ti1(a, qb, m) % 2][:, b * P:(b + 1) * P],
                                                    start=(b == 0), stop=(b == qb))
                        last.then_inc(pv_done, 1)

                    def fill(a, qb, half):
                        if fill_of(a, qb):
                            n = head_unit(*fill_of(a, qb))
                            tile_part(pe, n, before1(n), half, n % 2)

                    def gate_tile(pe, turn, at, bank, kts, m_hi, m_lo):
                        for k in range(kts):
                            j, c = (at + k) // KD, (at + k) % KD
                            if c == 0:
                                unit_split(pe, turn * TURN_UNITS + (B1_GATE + j))
                            slot = (B1_GATE + j) % 2
                            w = slice(c * P, (c + 1) * P)
                            last = mm3(bank[:, :], w_hi[slot][:, w], w_lo[slot][:, w], m_hi[:, k, :], m_lo[:, k, :],
                                       k == 0, k == kts - 1)
                            if c == KD - 1:
                                last.then_inc(unit_done, 1)

                    for tile, f in (("q", 0), ("k", 0), ("v", 0), ("q", 1)):
                        n = head_unit(tile, f)
                        tile_part(pe, n, before1(n), 0, n % 2)
                        if tile == "k":
                            rope("q", 0)
                        elif tile == "v":
                            rope("k", 0)
                        elif f:
                            v_transpose(0)
                        tile_part(pe, n, before1(n), 1, n % 2)
                    for a in range(N_ATT):
                        for qb in range(NB):
                            if banks1(a, qb) is S:
                                scores(a, qb)
                            if (a, qb) == (LAST, NB - 2):
                                scores(a, qb + 1)
                            if steps_back(a, qb, 2):
                                pv(*steps_back(a, qb, 2))
                            fill(a, qb, 0)
                            if steps_back(a, qb, 1):
                                transposes(*steps_back(a, qb, 1))
                            fill(a, qb, 1)
                            use, f = LATE1.get((a, qb), (None, 0))
                            if use == "v":
                                v_transpose(f)
                            elif use == "sum":
                                sum_squares(f)
                            elif use:
                                rope(use, f)
                    pv(LAST, NB - 2)
                    transposes(LAST, NB - 1)
                    pv(LAST, NB - 1)
                    with pe.Fori(0, KD // GATE_TURN) as turn:
                        for mm in range(GATE_TURN):
                            for i in range(3):
                                used = turn * (3 * GATE_TURN) + (before1(B1_GATE) + 3 * mm + i - 2)
                                pe.wait_ge(tile_out[0], used)
                                gate_tile(pe, turn, gate_at(mm, i), GATE_BANK[i], KD, h_hi, h_lo)
                                pe.wait_ge(tile_out[1], used)
                                if mm == 0 and i == 0:
                                    pe.wait_ge(y_ready, 12)
                                gate_tile(pe, turn, gate_at(mm, i) + KD, PROJ_BANK[i], 4,
                                          act_hi[:, 4 * i:4 * i + 4, :], act_lo[:, 4 * i:4 * i + 4, :])
                    for t in range(2):
                        pe.wait_ge(tile_out[t], before1(B1_GATE) + 3 * KD - 1)
                    for c in range(2):
                        tok_group(pe, B1_OUT + 4 * c, 4, KD, mrg_hi, mrg_lo, NB * c, (merged, 0))
                    for tb in range(NB - 1):
                        pe.wait_ge(norm_in, tb + 1)
                        transpose_block(hn, tb, OTHERS)

                @block.scalar
                def _(act):
                    st = Steps(act, act_step)
                    xt_hi_copy(act, 0, OTHERS, colp[:, P1_NORM:P1_NORM + KD])
                    act.wait_ge(lam_exp, 1)
                    nc.scalar.activation(small[:, 6:8], small[:, 4:6], ACT.Exp).then_inc(lam_exp, 1)
                    act.wait_ge(unit_done, 4)
                    for tb in range(NB):
                        nc.scalar.activation(ext[tb][:, :], TOK[tb][:, :], ACT.Gelu_apprx_tanh,
                                             accum_out=small[:, 12 + tb:13 + tb]).then_inc(v_ready, 1)
                    for tb in range(NB):
                        act.wait_ge(vb_ready, tb + 1)
                        last = st(nc.scalar.activation((*qs, *ks)[tb][:, :], ext[tb][:, :], ACT.Square,
                                                       accum_out=small[:, 16 + tb:17 + tb]))
                    st.wait(last)
                    st.wait(st(nc.scalar.activation(small[:, 20:24], small[:, 16:20], ACT.Ln, scale=1.0 / SEQ, bias=EPS)))
                    nc.scalar.activation(small[:, 20:24], small[:, 20:24], ACT.Exp, scale=-0.5).then_inc(stat_ready, 1)
                    for g in range(4):
                        n = B1_UZ + 2 * g
                        act.wait_ge(unit_done, n + 1)
                        if g >= 2:
                            act.wait_ge(y_ready, g - 1)
                        nc.scalar.activation(gelu_u[g % 2][:, :], PT[0][:, :], ACT.Gelu_apprx_tanh).then_inc(tile_out[0], 1)
                        act.wait_ge(unit_done, n + 2)
                        nc.scalar.activation(z_t[:, :], PT[1][:, :], ACT.Tanh, scale=0.5).then_inc(z_ready, 1)

                    def raw_copy(tile, f):
                        n = head_unit(tile, f)
                        act.wait_ge(unit_done, n + 1)
                        if tile == "q" and f:
                            act.wait_ge(r_ready, R1["v", f - 1] + 1)
                        elif tile == "k" and f:
                            act.wait_ge(qk_ready, 2 * f)
                        elif tile == "v":
                            act.wait_ge(qk_ready, 2 * f + 1)
                        nc.scalar.activation(raw_t[tile == "k"][:, :], PT[n % 2][:, :], ACT.Copy,
                                             scale=HD ** -0.5 if tile == "q" else 1.0).then_inc(tile_out[n % 2], 1)

                    def v_copy(f):
                        act.wait_ge(r_ready, R1["v", f] + 1)
                        if f >= 2:
                            act.wait_ge(pv_done, 4 * (f - 1))
                        nc.scalar.activation(vs[f % 2][:, :, :], R[:, :].rearrange("p (b c) -> p b c", c=P), ACT.Copy) \
                          .then_inc(r_out, 1)

                    def z_tanh(f):
                        n = head_unit("z", f)
                        act.wait_ge(unit_done, n + 1)
                        before = head_unit("z", f - 1) if f else B1_HEADS - 1
                        act.wait_ge(tile_out[before % 2], before1(before) + 1)
                        nc.scalar.activation(z_t[:, :], PT[n % 2][:, :], ACT.Tanh, scale=0.5).then_inc(z_ready, 1)

                    def output_squares(a):
                        act.wait_ge(pv_done, 4 * a + 4)
                        if a >= 1:
                            act.wait_ge(y_ready, 4 + a)
                        nc.scalar.activation(ext[0][:, :], O[:, :], ACT.Copy).then_inc(o_out, 1)
                        act.wait_ge(o_out, a + 1)
                        nc.scalar.activation(nrm[:, :], ext[0][:, :], ACT.Square).then_inc(sq_ready, 1)

                    def output_rstd(a):
                        act.wait_ge(r_ready, R1["sum", a] + 1)
                        nc.scalar.activation(nrm[:, :], R[:, :], ACT.Ln, scale=1.0 / P, bias=EPS).then_inc(r_out, 1)
                        act.wait_ge(r_out, R1["sum", a] + 1)
                        nc.scalar.activation(nrm[:, :], nrm[:, :], ACT.Exp, scale=-0.5).then_inc(rs_ready, 1)

                    def softmax_exp(a, qb, m):
                        u, nk = 8 * a + 2 * qb + m, (qb + 1) * P
                        act.wait_ge(max_ready, u + 1)
                        if u >= 2:
                            act.wait_ge(probs_normed, 4 * a + qb)
                        nc.scalar.activation(prob[m][:, 0:nk], banks1(a, qb)[m][:, 0:nk], ACT.Exp,
                                             bias=small[:, 24 + 2 * qb + m:25 + 2 * qb + m],
                                             accum_out=small[:, 32 + 2 * qb + m:33 + 2 * qb + m]).then_inc(probs_ready, 1)

                    def pT_copy(a, qb):
                        for m in range(1 if a < N_A else 2):
                            i = ti1(a, qb, m)
                            act.wait_ge(t_ready, i + 1)
                            w = 4 * a + qb - (1 if a < N_A else 0)
                            if a == N_A and qb == 0:
                                w = 4 * a
                            if w > 0:
                                act.wait_ge(pv_done, w)
                            nc.scalar.activation(pT[i % 2][:, 0:(qb + 1) * P], T[i % 2][:, 0:(qb + 1) * P], ACT.Copy) \
                              .then_inc(t_out, 1)

                    def place(tile, f):
                        which, i = "qk".index(tile), f % 2
                        act.wait_ge(qk_ready, 2 * f + which + 1)
                        for m in range(2):
                            own, other = slice(HD * m, HD * m + HD), slice(HD * (1 - m), HD * (2 - m))
                            dst, second = (k_two[i][m], qk_hi) if which else (q_two[i][m], q_lo)
                            act.dma_start(dst[other, :].bitcast(F32), second[own, :].bitcast(F32)).then_inc(qk_placed, 16)
                        for m in range(2):
                            own, dst = slice(HD * m, HD * m + HD), (k_two if which else q_two)[i][m]
                            nc.scalar.activation(dst[own, :], qk_hi[own, :].bitcast(F32), ACT.Copy).then_inc(qk_copied, 1)

                    raw_copy("q", 0)
                    raw_copy("k", 0)
                    place("q", 0)
                    raw_copy("v", 0)
                    place("k", 0)
                    v_copy(0)
                    raw_copy("q", 1)
                    for a in range(N_ATT):
                        for qb in range(NB):
                            softmax_exp(a, qb, 0)
                            softmax_exp(a, qb, 1)
                            before = steps_back(a, qb, 1)
                            if before:
                                if fill_of(*before):
                                    tile, f = fill_of(*before)
                                    if tile == "z":
                                        z_tanh(f)
                                    else:
                                        raw_copy(tile, f)
                                if LATE1.get(before, ("", 0))[0] == "v":
                                    v_copy(LATE1[before][1])
                                pT_copy(*before)
                            if qb == 1 and 1 <= a <= N_A:
                                output_squares(a - 1)
                            elif qb == 3 and 1 <= a <= N_A:
                                output_rstd(a - 1)
                            if LATE1.get(before, ("", 0))[0] in ("q", "k"):
                                place(*LATE1[before])
                    pT_copy(LAST, NB - 1)
                    with act.Fori(0, KD // GATE_TURN) as turn:
                        for mm in range(GATE_TURN):
                            for i in range(3):
                                act.wait_ge(unit_done, turn * TURN_UNITS + (B1_GATE + gate_units(gate_at(mm, i), KD)))
                                act.wait_ge(tile_out[1], turn * (3 * GATE_TURN) + (before1(B1_GATE) + 3 * mm + i - 2))
                                nc.scalar.activation(ext[i][:, :], GATE_BANK[i][:, :], ACT.Sigmoid).then_inc(tile_out[0], 1)
                    nc.scalar.preload_act_table_set("natural_log_exp_and_others")
                    for tb in range(NB):
                        act.wait_ge(tok_out, NB + tb + 1)
                        rms(st, tb)

                @block.vector
                def _(dve):
                    st = Steps(dve, dve_step)
                    xt_lo_sub(dve, st, 0, OTHERS, colp[:, P1_NORM:P1_NORM + KD])
                    lam = colp[:, P1_LAM:P1_LAM + 4 * HD].rearrange("p (a b d) -> p a b d", a=2, b=2)
                    st.wait(st(nc.vector.tensor_tensor(rope_a[:, 0:2 * HD].rearrange("p (a d) -> p a d", a=2),
                                                       lam[:, :, 0, :], lam[:, :, 1, :], ALU.mult)))
                    nc.vector.tensor_reduce(small[:, 4:6], rope_a[:, 0:2 * HD].rearrange("p (a d) -> p a d", a=2),
                                            AX.X, ALU.add).then_inc(lam_exp, 1)
                    dve.wait_ge(lam_exp, 2)
                    st.wait(st(nc.vector.tensor_tensor(small[:, 8:9], small[:, 6:7], small[:, 7:8], ALU.subtract)))
                    st(nc.vector.tensor_tensor(small[:, 8:9], small[:, 8:9], colp[:, P1_INIT:P1_INIT + 1], ALU.add))
                    st(nc.vector.scalar_tensor_tensor(out=small[:, 9:10], in0=colp[:, P1_SUBLN:P1_SUBLN + 1], scalar=0.5,
                                                      in1=colp[:, P1_KEEP:P1_KEEP + 1], op0=ALU.mult, op1=ALU.mult))
                    dve.wait_ge(rows_loaded, 16)
                    sgw = rowp[:, 3 * SEQ:4 * SEQ].rearrange("p (g t) -> p g t", g=4)
                    upper = const[:, C_UPPER:C_UPPER + P].unsqueeze(1).to_broadcast([P, 4, P])
                    st(nc.vector.tensor_tensor(sgw, sgw, upper, ALU.mult))
                    for tb in range(NB):
                        dve.wait_ge(v_ready, tb + 1)
                        st.wait(st(nc.vector.tensor_scalar(small[:, 12 + tb:13 + tb], small[:, 12 + tb:13 + tb],
                                                           -1.0 / SEQ, None, ALU.mult)))
                        nc.vector.tensor_scalar(ext[tb][:, :], ext[tb][:, :], small[:, 12 + tb:13 + tb], None, ALU.add) \
                          .then_inc(vb_ready, 1)
                    dve.wait_ge(stat_ready, 1)
                    for tb in range(NB):
                        st.wait(st(nc.vector.scalar_tensor_tensor(out=ext[tb][:, :], in0=ext[tb][:, :],
                                                                  scalar=small[:, 20 + tb:21 + tb], in1=rowp[:, 0:SEQ],
                                                                  op0=ALU.mult, op1=ALU.mult)))
                        nc.vector.tensor_tensor(ext[tb][:, :], ext[tb][:, :], rowp[:, SEQ:2 * SEQ], ALU.add) \
                          .then_inc(vb_ready, 1)

                    def split_y(i):
                        st.wait(st(nc.vector.tensor_copy(act_hi[:, i, :], ytmp[:, :])))
                        nc.vector.tensor_tensor(act_lo[:, i, :], ytmp[:, :], act_hi[:, i, :].bitcast(F32), ALU.subtract) \
                          .then_inc(y_ready, 1)

                    for g in range(4):
                        dve.wait_ge(z_ready, g + 1)
                        nc.vector.scalar_tensor_tensor(out=sz[1][:, :], in0=z_t[:, :], scalar=1.0, in1=PT[1][:, :],
                                                       op0=ALU.add, op1=ALU.mult).then_inc(tile_out[1], 1)
                        dve.wait_ge(r_ready, g + 1)
                        bias = rowp[:, 2 * SEQ + g * P:2 * SEQ + (g + 1) * P].unsqueeze(1).to_broadcast([P, NB, P])
                        nc.vector.tensor_tensor(rope_a[:, :].rearrange("p (c t) -> p c t", c=NB),
                                                R[:, :].rearrange("p (c t) -> p c t", c=NB), bias, ALU.add).then_inc(r_out, 1)
                        dve.wait_ge(r_out, g + 1)
                        dve.wait_ge(tile_out[0], g + 1)
                        st.wait(st(nc.vector.scalar_tensor_tensor(out=rope_a[:, :], in0=rope_a[:, :], scalar=0.5, in1=gelu_u[g % 2][:, :],
                                                                  op0=ALU.mult, op1=ALU.mult)))
                        dve.wait_ge(tile_out[1], g + 1)
                        st.wait(st(nc.vector.tensor_tensor(ytmp[:, :], rope_a[:, :], sz[1][:, :], ALU.mult)))
                        split_y(4 + g)

                    def rotate(tile, f):
                        which, idx = "qk".index(tile), R1[tile, f]
                        dve.wait_ge(r_ready, idx + 1)
                        if which or f:
                            dve.wait_ge(qk_placed, PLACED * (2 * f + which))
                            dve.wait_ge(qk_copied, 2 * (2 * f + which))
                        st(nc.vector.tensor_tensor(rope_a[:, :], raw_t[which][:, :], cos[:, :], ALU.mult))
                        nc.vector.tensor_tensor(rope_b[:, :], R[:, :], sin[:, :], ALU.mult).then_inc(r_out, 1)
                        st.wait()
                        dve.wait_ge(r_out, idx + 1)
                        st.wait(st(nc.vector.tensor_tensor(rope_a[:, :], rope_a[:, :], rope_b[:, :], ALU.add)))
                        st.wait(st(nc.vector.tensor_copy(qk_hi[:, :], rope_a[:, :])))
                        lo = k_lo[f % 2] if which else q_lo
                        nc.vector.tensor_tensor(lo[:, :], rope_a[:, :], qk_hi[:, :].bitcast(F32), ALU.subtract).then_inc(qk_ready, 1)

                    def row_max(a, qb, m):
                        u = 8 * a + 2 * qb + m
                        dve.wait_ge(scores_ready, u + 1)
                        nc.vector.tensor_reduce(small[:, 24 + 2 * qb + m:25 + 2 * qb + m], banks1(a, qb)[m][:, 0:(qb + 1) * P], AX.X,
                                                ALU.max, negate=True).then_inc(max_ready, 1)

                    def silu_z(f):
                        dve.wait_ge(z_ready, 4 + f + 1)
                        b = head_unit("z", f) % 2
                        nc.vector.scalar_tensor_tensor(out=sz[f % 2][:, :], in0=z_t[:, :], scalar=1.0, in1=PT[b][:, :],
                                                       op0=ALU.add, op1=ALU.mult).then_inc(tile_out[b], 1)

                    def normalise(a, qb):
                        nk = (qb + 1) * P
                        l, r = small[:, 32 + 2 * qb:34 + 2 * qb], small[:, 40:42]
                        dve.wait_ge(probs_ready, 8 * a + 2 * qb + 2)
                        st.wait(st(nc.vector.reciprocal(r, l)))
                        if a or qb:
                            dve.wait_ge(t_ready, ti1(a, qb - 1, 1) + 1 if qb else ti1(a - 1, 3, 1) + 1)
                        if a < N_A:
                            st.wait(st(nc.vector.tensor_scalar(small[:, 41:42], small[:, 41:42], small[:, 8:9], None, ALU.mult)))
                            st.wait(st(nc.vector.tensor_scalar(prob[1][:, 0:nk], prob[1][:, 0:nk], small[:, 41:42], None, ALU.mult)))
                            nc.vector.scalar_tensor_tensor(out=pn[0][:, 0:nk], in0=prob[0][:, 0:nk], scalar=small[:, 40:41],
                                                           in1=prob[1][:, 0:nk], op0=ALU.mult, op1=ALU.subtract) \
                              .then_inc(probs_normed, 1)
                        else:
                            st.wait(st(nc.vector.tensor_scalar(pn[0][:, 0:nk], prob[0][:, 0:nk], small[:, 40:41], None, ALU.mult)))
                            nc.vector.tensor_scalar(pn[1][:, 0:nk], prob[1][:, 0:nk], small[:, 41:42], None, ALU.mult) \
                              .then_inc(probs_normed, 1)

                    def epilogue(a):
                        z = head_unit("z", a)
                        dve.wait_ge(tile_out[z % 2], before1(z) + 1)
                        if a < N_A:
                            dve.wait_ge(rs_ready, a + 1)
                            st.wait(st(nc.vector.tensor_tensor(rope_a[:, :], ext[0][:, :], nrm[:, :], ALU.mult)))
                            st.wait(st(nc.vector.scalar_tensor_tensor(out=ytmp[:, :], in0=rope_a[:, :], scalar=small[:, 9:10],
                                                                      in1=sz[a % 2][:, :], op0=ALU.mult, op1=ALU.mult)))
                        else:
                            dve.wait_ge(pv_done, 4 * a + 4)
                            nc.vector.scalar_tensor_tensor(out=ytmp[:, :], in0=O[:, :], scalar=0.5, in1=sz[a % 2][:, :],
                                                           op0=ALU.mult, op1=ALU.mult).then_inc(o_out, 1)
                            dve.wait_ge(o_out, a + 1)
                        split_y(a if a < N_A else 8 + a - N_A)

                    rotate("q", 0)
                    rotate("k", 0)
                    for a in range(N_ATT):
                        for qb in range(NB):
                            row_max(a, qb, 0)
                            row_max(a, qb, 1)
                            before = steps_back(a, qb, 1)
                            if before and fill_of(*before) == ("z", before[0]):
                                silu_z(before[0])
                            if LATE1.get(before, ("", 0))[0] in ("q", "k"):
                                rotate(*LATE1[before])
                            normalise(a, qb)
                            if qb == 0 and 2 <= a < N_A + 2:
                                epilogue(a - 2)
                            elif qb == 1 and a > N_A:
                                epilogue(a - 1)
                    epilogue(LAST)
                    base_step, per_tile = st.n, 3
                    total, term = ytmp[:, :], rope_a[:, :]
                    with dve.Fori(0, KD // GATE_TURN) as turn:
                        for mm in range(GATE_TURN):
                            m = turn * GATE_TURN + mm
                            for i in range(3):
                                done = turn * (3 * GATE_TURN) + (before1(B1_GATE) + 3 * mm + i + 1)
                                dve.wait_ge(tile_out[0], done)
                                dve.wait_ge(unit_done, turn * TURN_UNITS + (B1_GATE + gate_units(gate_at(mm, i) + KD, 4)))
                                nc.vector.tensor_tensor(term if i else total, ext[i][:, :], PROJ_BANK[i][:, :], ALU.mult) \
                                  .then_inc(tile_out[1], 1)
                                dve.wait_ge(tile_out[1], done)
                                if i:
                                    nc.vector.tensor_tensor(total, total, term, ALU.add).then_inc(dve_step, 1)
                                    dve.wait_ge(dve_step, turn * (per_tile * GATE_TURN) + (base_step + per_tile * mm + i))
                            hi = mrg_hi[:, bass.ds(m, 1), :].rearrange("p a t -> p (a t)")
                            lo = mrg_lo[:, bass.ds(m, 1), :].rearrange("p a t -> p (a t)")
                            nc.vector.tensor_copy(hi, total).then_inc(dve_step, 1)
                            dve.wait_ge(dve_step, turn * (per_tile * GATE_TURN) + (base_step + per_tile * mm + 3))
                            nc.vector.tensor_tensor(lo, total, hi.bitcast(F32), ALU.subtract).then_inc(merged, 1)
                            dve.wait_ge(merged, m + 1)
                    st.n += per_tile * KD
                    for c in range(2):
                        for tb in range(NB):
                            tok_wait(dve, c, tb, B1_OUT + 4 * c + 4)
                            cols = slice(c * SEQ, (c + 1) * SEQ)
                            nc.vector.tensor_tensor(x[:, tb, cols], x[:, tb, cols], TOK[tb][:, :], ALU.add).then_inc(tok_out, 1)
                            if c and tb:
                                normalise_in(dve, tb - 1)
                    normalise_in(dve, NB - 1)
            end_of_stage()

        with nc.Block() as block:
            @block.sync
            def _(sp):
                sp.dma_start(cos[:, :], rope2_in[0, :, :]).then_inc(params_loaded, 16)
                sp.dma_start(sin[:, :], rope2_in[1, :, :]).then_inc(params_loaded, 16)
                sp.wait_ge(params_loaded, 32)

            @block.vector
            def _(dve):
                for tb in range(NB):
                    nc.vector.tensor_scalar(x[:, tb, :], x[:, tb, :], small[:, tb:tb + 1], None, ALU.mult).then_inc(norm_in, 1)

            @block.tensor
            def _(pe):
                for tb in range(NB - 1):
                    pe.wait_ge(norm_in, tb + 1)
                    transpose_block(x, tb, TOK)
        end_of_stage()

        SWA, MLA, SB, FOX = range(4)
        KIND = (SWA, SWA, MLA, MLA, SB, SB, FOX, FOX)
        SOFTMAX = {0: 0, 1: 1, 2: 2, 3: 3, 6: 4, 7: 5}
        SB0 = KIND.index(SB)
        FIRST = ("wq0", "wk", "wv", "ckv", "cq0", "cq1")
        FILL = {(0, 0): ("wq1",), (0, 1): ("kr",), (0, 2): ("gates",), (0, 3): ("uq0",),
                (1, 0): ("uqr",), (1, 1): ("uk0", "uv0"), (1, 2): ("sq1",), (1, 3): ("sk1",),
                (2, 0): ("uq1",), (2, 1): ("uk1", "uv1"), (2, 2): ("sq0",), (2, 3): ("sk0",),
                (3, 0): ("sv0",), (3, 1): ("fq0",), (3, 2): ("fk0",), (4, 0): ("sv1",), (4, 1): ("fq1",), (4, 2): ("fk1",),
                (5, 0): ("fv0",), (5, 2): ("fv1",)}
        assert FIRST + tuple(t for key in sorted(FILL) for t in FILL[key]) == B2_TILES
        TILE = {name: t for t, name in enumerate(B2_TILES)}
        WHERE = {}
        DONE = {}
        for n, unit in enumerate(B2_PACKED):
            at = 0
            for name in unit:
                WHERE[name] = (n, at)
                at += B2_KT.get(name, KD)
                before = sum(signal is small_done for signal, _ in DONE.values())
                DONE[name] = (unit_done, n + 1) if name == unit[-1] else (small_done, before + 1)
        PREFIX = {SWA: "w", MLA: "u", SB: "s", FOX: "f"}
        FIRST_R = ("wv", "ckv")
        LATE = {(0, 0): "cq", (0, 2): "kr", (1, 1): "qr", (1, 2): "uv0", (2, 2): "e1", (2, 3): "uv1", (3, 1): "sv0",
                (4, 1): "e3", (4, 2): "sv1", (5, 1): "fv0", (6, 1): "e5", (6, 2): "fv1"}
        R2 = {name: i for i, name in enumerate(FIRST_R + tuple(LATE[key] for key in sorted(LATE)) + ("e7",))}
        SQUARES = {"ckv": 1, "cq": 2, "e1": 3, "e3": 4, "e5": 5, "e7": 6}
        V_TILES = ("wv", "uv0", "uv1", "sv0", "sv1", "fv0", "fv1")
        vw_t = ext[3][:, :].rearrange("p (b c) -> p b c", c=P)
        DEST = {"wq0": wq_t[0], "wq1": wq_t[1], "wk": wk_t, "ckv": ckv_t, "cq0": cq_t[0], "cq1": cq_t[1],
                "kr": raw_t[0], "uqr": raw_t[1], "uq0": qs[0], "uq1": qs[1], "uk0": ks[0], "uk1": ks[1],
                "sq0": wq_t[0], "sq1": cq_t[0], "sk0": wk_t, "sk1": ckv_t,
                "fq0": qs[0], "fq1": qs[1], "fk0": ks[0], "fk1": ks[1],
                "wv": raw_t[1], "uv0": raw_t[0], "uv1": raw_t[1], "sv0": raw_t[0], "sv1": raw_t[1],
                "fv0": raw_t[0], "fv1": raw_t[1]}

        def q_name(a):
            return f"{PREFIX[KIND[a]]}q{a % 2}"

        def k_name(a):
            return "wk" if KIND[a] == SWA else f"{PREFIX[KIND[a]]}k{a % 2}"

        def v_name(a):
            return "wv" if KIND[a] == SWA else f"{PREFIX[KIND[a]]}v{a % 2}"

        def v_of(a):
            return vw_t if KIND[a] == SWA else vs[a % 2]

        def head_of(a, m):
            i = a % 2
            return i + 2 * m if KIND[a] == SWA else 2 * i + m

        def first_key(a, qb):
            return max(0, qb - 1) * P if KIND[a] == SWA else 0

        def u_of(a, qb, m):
            return 8 * SOFTMAX[a] + 2 * qb + m

        def w_of(a, j):
            return 8 * (a - SB0) + 2 * j

        def banks(a, qb):
            if KIND[a] == SB:
                return (S, T)[qb % 2]
            return PT if KIND[a] == FOX and qb % 2 else S

        def probs_at(a, qb):
            return sz if KIND[a] == FOX and qb % 2 else prob

        def sb_weights_at(j):
            return pT if j % 2 else (z_t, qr_t)

        OUTPUT_AT = {(1, 1): 0, (2, 1): 1, (3, 1): 2, (4, 0): 3, (5, 0): 4, (6, 0): 5, (7, 1): 6}

        def step_before(a, qb, steps=1):
            return divmod(NB * a + qb - steps, NB) if NB * a + qb >= steps else None

        def is_sb(step):
            return step is not None and KIND[step[0]] == SB

        mla_scale = (HD + HD // 2) ** -0.5

        with nc.Fori(0, DEPTH) as layer:
            with nc.Block() as block:
                w_layer2 = w_in[bass.ds(layer * B2_UNITS + DEPTH * B1_UNITS, B2_UNITS), :, :]
                rows2 = row2_in[bass.ds(layer, 1), :, :, :].rearrange("l r p c -> (l r) p c")

                @block.sync
                def _(sp):
                    load_units(sp, w_layer2, B2_UNITS)
                    sp.wait_ge(xt_hi, 2 * KD)
                    sp.wait_ge(xt_lo, 2 * KD)
                    sp.wait_ge(split_done, B2_UNITS - 1)
                    next_layer(sp, layer + (DEPTH + 1), layer * B2_UNITS + (DEPTH * B1_UNITS + B2_UNITS))

                @block.gpsimd
                def _(pool):
                    split_units(pool, B2_UNITS)

                @block.tensor
                def _(pe):
                    def standardised(i):
                        pe.wait_ge(ln_done, NB * i + NB - 1)
                        for tb in range(NB - 1):
                            transpose_block(x, tb, TOK)

                    transpose_in(pe, x, 0, TOK)

                    def part(name, half):
                        t, (n, at), kt, mov = TILE[name], WHERE[name], B2_KT.get(name, KD), None
                        if kt < KD:
                            pe.wait_ge(latent_ready, 1 if kt == 1 else 3)
                            i = 10 if kt == 1 else 8
                            mov = (act_hi[:, i:i + 2, :], act_lo[:, i:i + 2, :])
                        if half == 0 or kt > 1:
                            tile_part(pe, n, t // 2, half, n % 2, kt=kt, mov=mov, bank=t % 2, at=at, done=DONE[name][0],
                                      split_from=0 if t == 0 else None)

                    def tile_wait(name):
                        t = TILE[name]
                        pe.wait_ge(tile_out[t % 2], t // 2 + 1)

                    def r_free(name):
                        if R2[name]:
                            pe.wait_ge(r_out, R2[name])

                    def v_transpose(name):
                        tile_wait(name)
                        r_free(name)
                        for b in range(NB):
                            last = nc.tensor.transpose(R[:, b * P:(b + 1) * P], DEST[name][:, b * P:(b + 1) * P], ident)
                        last.then_inc(r_ready, 1)

                    def rope(name, tile):
                        tile_wait(tile)
                        r_free(name)
                        nc.tensor.matmul(R[:, :], rope2, DEST[tile][:, :], start=True, stop=True).then_inc(r_ready, 1)

                    def sum_squares(name, squares):
                        pe.wait_ge(sq_ready, SQUARES[name])
                        r_free(name)
                        nc.tensor.matmul(R[:, :], ones, squares[:, :], start=True, stop=True).then_inc(r_ready, 1)

                    def operands_wait(a):
                        tile_wait(q_name(a))
                        tile_wait(k_name(a))
                        if KIND[a] == FOX:
                            pe.wait_ge(gate_ready, 1)
                        elif KIND[a] == SWA:
                            pe.wait_ge(swa_ready, 1)
                        elif KIND[a] == MLA:
                            pe.wait_ge(qk_ready, 2)

                    def bank_wait(a, qb, m):
                        if KIND[a] == SB:
                            w = w_of(a, qb)
                            if m:
                                return
                            if w == 0:
                                pe.wait_ge(probs_ready, u_of(SB0 - 1, NB - 1, 1) + 1)
                            elif w == 2:
                                pe.wait_ge(t_out, u_of(SB0 - 1, NB - 1, 1) + 1)
                            else:
                                pe.wait_ge(sb_prob, w - 2)
                        elif a == SB0 + 2 and qb < 2:
                            if qb == 0:
                                pe.wait_ge(sb_prob, w_of(a - 1, NB - 1))
                            else:
                                tile_wait(("fv0", "fv1")[m])
                        elif KIND[a] == FOX:
                            two = step_before(*step_before(a, qb))
                            pe.wait_ge(probs_ready, u_of(*two, m) + 1)
                        elif a or qb:
                            pe.wait_ge(probs_ready, u_of(*step_before(a, qb), m) + 1)

                    def scores(a, qb):
                        kind, k0, k1 = KIND[a], first_key(a, qb), (qb + 1) * P
                        nk, block_q = k1 - k0, slice(qb * P, (qb + 1) * P)
                        if qb == 0:
                            operands_wait(a)
                        q, k = DEST[q_name(a)], DEST[k_name(a)]
                        S = banks(a, qb)
                        for m in range(2):
                            bank_wait(a, qb, m)
                            rows = slice(HD * m, HD * m + HD)
                            nc.tensor.matmul(S[m][:, 0:nk], q[rows, block_q], k[rows, k0:k1], start=True, stop=False)
                        for m in range(2):
                            h = head_of(a, m)
                            if kind == FOX:
                                nc.tensor.matmul(S[m][:, 0:nk], sel_r[:, h * P:(h + 1) * P], cum_r[:, 0:nk],
                                                 start=False, stop=False)
                            elif kind == MLA:
                                r0 = HD * m + 32 * (a % 2)
                                r = slice(r0, r0 + 32)
                                nc.tensor.matmul(S[m][:, 0:nk], qr_t[r, block_q], z_t[r, 0:nk], start=False, stop=False,
                                                 tile_position=(r0, 0))
                        for m in range(2):
                            if kind == SWA:
                                last = nc.tensor.matmul(S[m][:, 0:nk], ident_r[:, :], swa_r[:, head_of(a, m), 2 * P - nk:2 * P],
                                                        start=False, stop=True)
                            else:
                                last = nc.tensor.matmul(S[m][:, nk - P:nk], ident_r[:, :], causal_r[:, :], start=False, stop=True)
                            last.then_inc(scores_ready, 1)

                    def probs_transpose(a, qb, m):
                        u, nk = u_of(a, qb, m), (qb + 1) * P - first_key(a, qb)
                        pe.wait_ge(probs_normed, u // 2 + 1)
                        if u >= 2:
                            pe.wait_ge(t_out, u - 1)
                        for b in range(nk // P):
                            last = nc.tensor.transpose(T[m][:, b * P:(b + 1) * P], pn[m][:, b * P:(b + 1) * P], ident)
                        last.then_inc(t_ready, 1)

                    def v_wait(a):
                        pe.wait_ge(r_out, R2[v_name(a)] + 1)
                        if a:
                            pe.wait_ge(o_out, a)

                    def pv(a, qb):
                        if qb == 0:
                            v_wait(a)
                        b0 = first_key(a, qb) // P
                        for m, b in head_block_order(2, range(b0, qb + 1), KIND[a] == FOX):
                            if b == b0:
                                pe.wait_ge(t_out, u_of(a, qb, m) + 1)
                            rows = slice(HD * m, HD * m + HD)
                            last = nc.tensor.matmul(O[rows, qb * P:(qb + 1) * P], v_of(a)[:, b, rows],
                                                    pT[m][:, (b - b0) * P:(b - b0 + 1) * P], start=(b == b0), stop=(b == qb))
                        last.then_inc(pv_done, 1)

                    def sb_scores_of(a, j):
                        lo = (NB - 1 - j) * P
                        if j == 0:
                            operands_wait(a)
                        bank_wait(a, j, 0)
                        q, k, S = DEST[q_name(a)], DEST[k_name(a)], banks(a, j)
                        for m in range(2):
                            rows = slice(HD * m, HD * m + HD)
                            nc.tensor.matmul(S[m][:, lo:SEQ], k[rows, lo:lo + P], q[rows, lo:SEQ], start=True, stop=False)
                        for m in range(2):
                            nc.tensor.matmul(S[m][:, lo:lo + P], ident_r[:, :], sbmask_r[:, :], start=False, stop=True) \
                              .then_inc(sb_scores, 1)

                    def sb_between(a, j):
                        lo, w, S = (NB - 1 - j) * P, w_of(a, j), banks(a, j)
                        for m in range(2):
                            pe.wait_ge(sb_sp, w + m + 1)
                            last = nc.tensor.matmul(S[m][:, lo:SEQ], neg_tri, pn[m][:, lo:SEQ], start=False, stop=True,
                                                    skip_group_check=True)
                            if j:
                                pe.wait_ge(sb_sum, w + m - 1)
                                last = nc.tensor.matmul(S[m][:, lo + P:SEQ], neg_ones, sz[m][:, lo + P:SEQ],
                                                        start=False, stop=True, skip_group_check=True)
                            last.then_inc(sb_cum, 1)

                    def sb_pv(a, j):
                        kb, lo = NB - 1 - j, (NB - 1 - j) * P
                        if j == 0:
                            v_wait(a)
                        pe.wait_ge(sb_prob, w_of(a, j) + 2)
                        for m in range(2):
                            rows = slice(HD * m, HD * m + HD)
                            last = nc.tensor.matmul(O[rows, lo:SEQ], vs[a % 2][:, kb, rows], sb_weights_at(j)[m][:, lo:SEQ],
                                                    start=(j == 0), stop=(j == NB - 1), skip_group_check=True)
                        last.then_inc(pv_done, 1)

                    def transposes(step):
                        if step and not is_sb(step):
                            probs_transpose(*step, 0)
                            probs_transpose(*step, 1)

                    def weighted_v(step):
                        if step:
                            (sb_pv if is_sb(step) else pv)(*step)

                    def fill(a, qb, which):
                        halves = [(name, half) for name in FILL.get((a, qb), ()) for half in range(2)]
                        cut = (len(halves) + 1) // 2
                        for name, half in (halves[:cut] if which == 0 else halves[cut:]):
                            part(name, half)

                    def late_work(name):
                        if name == "cq":
                            sum_squares(name, sz[0])
                        elif name == "kr":
                            rope(name, "kr")
                        elif name == "qr":
                            rope(name, "uqr")
                        elif name[0] == "e":
                            sum_squares(name, nrm)
                        else:
                            v_transpose(name)

                    for name in FIRST:
                        part(name, 0)
                        part(name, 1)
                        if name == "cq0":
                            v_transpose("wv")
                    sum_squares("ckv", z_t)
                    for a in range(N_ATT):
                        for qb in range(NB):
                            before, after = step_before(a, qb), divmod(NB * a + qb + 1, NB)
                            two_before = before and step_before(*before)
                            if KIND[a] != SB:
                                if KIND[a] != FOX or is_sb(before):
                                    scores(a, qb)
                                if KIND[a] == FOX and after[0] < N_ATT:
                                    scores(*after)
                                if not is_sb(two_before):
                                    weighted_v(two_before)
                                if is_sb(before):
                                    weighted_v(before)
                                fill(a, qb, 0)
                                transposes(before)
                                fill(a, qb, 1)
                            elif w_of(a, qb) == 0:
                                sb_scores_of(a, qb)
                                weighted_v(two_before)
                                transposes(before)
                                fill(a, qb, 0)
                                weighted_v(before)
                                sb_between(a, qb)
                                sb_scores_of(a, qb + 1)
                                fill(a, qb, 1)
                            else:
                                sb_between(a, qb)
                                if is_sb(after):
                                    sb_scores_of(*after)
                                fill(a, qb, 0)
                                weighted_v(before)
                                fill(a, qb, 1)
                            if (a, qb) in LATE:
                                late_work(LATE[a, qb])
                    last_step = (N_ATT - 1, NB - 1)
                    weighted_v(step_before(*last_step))
                    transposes(last_step)
                    weighted_v(last_step)
                    for j in range(4):
                        if j == 1:
                            sum_squares("e7", nrm)
                        elif j == 3:
                            pe.wait_ge(y_ready, 8)
                        else:
                            pe.wait_ge(y_ready, 6)
                        tok_unit(pe, B2_WO, j, 4, KD, act_hi, act_lo, 0)
                    tok_group(pe, B2_WO + 4, 4, KD, act_hi, act_lo, NB)
                    standardised(0)
                    pe.wait_ge(ln_done, NB)
                    transpose_in(pe, x, KD, TOK)
                    for hf in range(2):
                        n0, tiles = B2_PART[hf], FF_PARTS[hf]
                        done = len(B2_TILES) // 2 + FF_FIRST[hf]
                        with pe.Fori(0, tiles) as j:
                            for t in range(2):
                                for half in range(2):
                                    tile_part(pe, j * 2 + (n0 + t), j + done, half, (n0 + t) % 2, bank=t, split_from=KD if t == 0 and hf == 0 else None)
                        for c in range(2):
                            tok_group(pe, n0 + 2 * tiles + tiles // 2 * c, tiles // 2, tiles, act_hi, act_lo,
                                      NB * (2 + 2 * hf + c), (gu_ready, FF_FIRST[hf]))
                    standardised(1)

                @block.scalar
                def _(act):
                    st = Steps(act, act_step)
                    xt_hi_copy(act, 0, TOK, colp[:, P2_GIN:P2_GIN + KD], colp[:, P2_BIN:P2_BIN + KD])
                    act.dma_start(swa_raw[:, :], swa_in).then_inc(swa_loaded, 16)
                    act.dma_start(row_in[:, :], rows2[0, :, :]).then_inc(rows_loaded, 16)

                    def tile_copy(name):
                        t = TILE[name]
                        act.wait_ge(*DONE[name])
                        if name == "uv0":
                            act.wait_ge(qk_ready, 1)
                        elif name == "uv1":
                            act.wait_ge(qk_ready, 2)
                        scale = 1.0
                        if name[1] == "q" and name[0] != "c":
                            scale = mla_scale if name[0] == "u" else HD ** -0.5
                        nc.scalar.activation(DEST[name][:, :], PT[t % 2][:, :], ACT.Copy, scale=scale) \
                          .then_inc(tile_out[t % 2], 1)

                    def v_copy(name):
                        act.wait_ge(r_ready, R2[name] + 1)
                        if name[0] in "sf":
                            a = KIND.index(SB if name[0] == "s" else FOX) + int(name[2])
                            act.wait_ge(pv_done, NB * (a - 1))
                        dst = vw_t if name == "wv" else vs[int(name[2])][:, :, :]
                        nc.scalar.activation(dst, R[:, :].rearrange("p (b c) -> p b c", c=P), ACT.Copy).then_inc(r_out, 1)

                    def rstd(name, dst, width):
                        act.wait_ge(r_ready, R2[name] + 1)
                        nc.scalar.activation(dst[:, :], R[:, :], ACT.Ln, scale=1.0 / width, bias=EPS).then_inc(r_out, 1)
                        act.wait_ge(r_out, R2[name] + 1)
                        nc.scalar.activation(dst[:, :], dst[:, :], ACT.Exp, scale=-0.5).then_inc(rs_ready, 1)

                    def output_copy(a):
                        act.wait_ge(pv_done, 4 * a + 4)
                        if a >= 2:
                            act.wait_ge(y_ready, 2 * (a // 2))
                        nc.scalar.activation(ext[a % 2][:, :], O[:, :], ACT.Copy).then_inc(o_out, 1)
                        if a % 2:
                            act.wait_ge(o_out, a + 1)
                            st(nc.scalar.activation(nrm[:, :], ext[0][:, :], ACT.Square))
                            st.wait()
                            nc.scalar.activation(sq_tmp[:, :], ext[1][:, :], ACT.Square).then_inc(sq_parts, 1)

                    def softmax_exp(a, qb, m):
                        u, nk, c = u_of(a, qb, m), (qb + 1) * P - first_key(a, qb), 2 * qb + m
                        act.wait_ge(max_ready, u + 1)
                        if u >= 2:
                            act.wait_ge(probs_normed, u // 2 - (KIND[a] == FOX and not is_sb(step_before(a, qb))))
                        if KIND[a] == SWA:
                            sink = colp[:, P2_SINK + head_of(a, m):P2_SINK + head_of(a, m) + 1]
                            st(nc.scalar.activation(small[:, 44 + m:45 + m], sink, ACT.Exp, bias=small[:, 24 + c:25 + c]))
                        nc.scalar.activation(probs_at(a, qb)[m][:, 0:nk], banks(a, qb)[m][:, 0:nk], ACT.Exp, bias=small[:, 24 + c:25 + c],
                                             accum_out=small[:, 32 + c:33 + c]).then_inc(probs_ready, 1)

                    def pT_copy(a, qb):
                        nk = (qb + 1) * P - first_key(a, qb)
                        for m in range(2):
                            act.wait_ge(t_ready, u_of(a, qb, m) + 1)
                            if 4 * a + qb:
                                act.wait_ge(pv_done, 4 * a + qb)
                            nc.scalar.activation(pT[m][:, 0:nk], T[m][:, 0:nk], ACT.Copy).then_inc(t_out, 1)

                    def sb_softplus(a, j):
                        lo, w = (NB - 1 - j) * P, w_of(a, j)
                        for m in range(2):
                            e = prob[m][:, lo:SEQ]
                            act.wait_ge(sb_scores, w + m + 1)
                            if w == 0:
                                act.wait_ge(probs_normed, NB * SB0)
                            else:
                                act.wait_ge(sb_sp, w + m - 1)
                            st.wait(st(nc.scalar.activation(e, banks(a, j)[m][:, lo:SEQ], ACT.Abs)))
                            st.wait(st(nc.scalar.activation(e, e, ACT.Exp, scale=-1.0)))
                            nc.scalar.activation(e, e, ACT.Ln, bias=1.0).then_inc(sb_ln, 1)

                    def sb_weights(a, j):
                        lo, w = (NB - 1 - j) * P, w_of(a, j)
                        for m in range(2):
                            act.wait_ge(sb_cum, w + m + 1)
                            act.wait_ge(pv_done, NB * a + j - 1)
                            nc.scalar.activation(sb_weights_at(j)[m][:, lo:SEQ], banks(a, j)[m][:, lo:SEQ], ACT.Exp) \
                              .then_inc(sb_prob, 1)

                    def latent_squares(names, squares):
                        for name, square in zip(names, squares):
                            t = TILE[name]
                            act.wait_ge(tile_out[t % 2], t // 2 + 1)
                            last = nc.scalar.activation(square[:, :], DEST[name][:, :], ACT.Square)
                            if name == names[-1]:
                                last.then_inc(sq_ready if len(names) == 1 else sq_parts, 1)
                            else:
                                st.wait(st(last))

                    def gate_log():
                        t = TILE["gates"]
                        act.wait_ge(tile_out[t % 2], t // 2 + 1)
                        y, e = sz[0][0:4, :], sz[1][0:4, :]
                        st.wait(st(nc.scalar.activation(e, y, ACT.Abs)))
                        st.wait(st(nc.scalar.activation(e, e, ACT.Exp, scale=-1.0)))
                        nc.scalar.activation(e, e, ACT.Ln, bias=1.0).then_inc(gate_ln, 1)

                    for name in FIRST:
                        tile_copy(name)
                        if name == "ckv":
                            latent_squares(("ckv",), (z_t,))
                    v_copy("wv")
                    latent_squares(("cq0", "cq1"), sz)
                    rstd("ckv", z_t, P)
                    for a in range(N_ATT):
                        for qb in range(NB):
                            before, after = step_before(a, qb), divmod(NB * a + qb + 1, NB)
                            if KIND[a] != SB:
                                softmax_exp(a, qb, 0)
                                softmax_exp(a, qb, 1)
                            elif w_of(a, qb) == 0:
                                sb_softplus(a, qb)
                            for name in FILL.get(before, ())[-1:]:
                                if name != "gates":
                                    tile_copy(name)
                            if LATE.get(before) in V_TILES:
                                v_copy(LATE[before])
                            if KIND[a] == SB and w_of(a, qb):
                                sb_weights(a, qb)
                                if is_sb(after):
                                    sb_softplus(*after)
                            if before and not is_sb(before):
                                pT_copy(*before)
                            if (a, qb) in OUTPUT_AT:
                                output_copy(OUTPUT_AT[a, qb])
                            if KIND[a] == SB and w_of(a, qb) == 0:
                                sb_weights(a, qb)
                                sb_softplus(*after)
                            for name in FILL.get((a, qb), ())[:-1]:
                                tile_copy(name)
                            late = LATE.get((a, qb), "")
                            if late == "cq":
                                rstd("cq", sz[0], 2 * P)
                            elif late[:1] == "e":
                                rstd(late, nrm, 4 * HD)
                            if (a, qb) == (1, 0):
                                gate_log()
                            elif (a, qb) == (6, 2):
                                act.dma_start(rowp[:, :], rows2[1, :, :]).then_inc(rows_loaded, 16)
                    pT_copy(N_ATT - 1, NB - 1)
                    output_copy(N_ATT - 1)
                    rstd("e7", nrm, 4 * HD)

                    def ln_stats(i):
                        for tb in range(NB):
                            act.wait_ge(ln_centre, NB * i + tb + 1)
                            st.wait(st(nc.scalar.activation(hn[:, tb, :], x[:, tb, :], ACT.Square, bias=small[:, 52 + tb:53 + tb],
                                                            accum_out=small[:, 16 + tb:17 + tb])))
                            st.wait(st(nc.scalar.activation(small[:, 20 + tb:21 + tb], small[:, 16 + tb:17 + tb], ACT.Ln,
                                                            scale=1.0 / D, bias=LN_EPS)))
                            nc.scalar.activation(small[:, 20 + tb:21 + tb], small[:, 20 + tb:21 + tb], ACT.Exp, scale=-0.5) \
                              .then_inc(stat_ready, 1)

                    ln_stats(0)
                    xt_hi_copy(act, KD, TOK, colp[:, P2_G1:P2_G1 + KD], colp[:, P2_B1:P2_B1 + KD])
                    for hf in range(2):
                        n0, tiles = B2_PART[hf], FF_PARTS[hf]
                        done = len(B2_TILES) // 2 + FF_FIRST[hf]
                        with act.Fori(0, tiles) as j:
                            act.wait_ge(unit_done, j * 2 + (n0 + 1))
                            act.wait_ge(tile_out[1], j + done)
                            nc.scalar.activation(nrm[:, :], PT[0][:, :], ACT.Silu).then_inc(tile_out[0], 1)
                        if hf == 0:
                            act.wait_ge(gain_done, 2)
                            act.dma_start(rowp[:, :], rows2[2, :, :]).then_inc(rows_loaded, 16)
                    nc.scalar.preload_act_table_set("natural_log_exp_and_others")
                    ln_stats(1)
                    act.wait_ge(rows_loaded, 48)

                @block.vector
                def _(dve):
                    st = Steps(dve, dve_step)
                    xt_lo_sub(dve, st, 0, TOK, colp[:, P2_GIN:P2_GIN + KD], colp[:, P2_BIN:P2_BIN + KD])

                    dve.wait_ge(swa_loaded, 16)
                    nc.vector.tensor_copy(swa_r[:, :, :], swa_raw[:, :].rearrange("p (h c) -> p h c", h=4)).then_inc(swa_ready, 1)

                    def gain_x(tb, row):
                        st.wait(st(nc.vector.tensor_tensor(x[:, tb, :], x[:, tb, :], row[:, 0:D], ALU.mult)))
                        return nc.vector.tensor_tensor(x[:, tb, :], x[:, tb, :], row[:, D:2 * D], ALU.add)

                    for h in range(4):
                        st(nc.vector.tensor_scalar(small[:, 48 + h:49 + h], colp[:, P2_SINK + h:P2_SINK + h + 1], -1.0, None, ALU.mult))
                    st.wait()

                    def row_max(a, qb, m):
                        u, c = u_of(a, qb, m), 2 * qb + m
                        nm = small[:, 24 + c:25 + c]
                        dve.wait_ge(scores_ready, u + 1)
                        top_ = nc.vector.tensor_reduce(nm, banks(a, qb)[m][:, 0:(qb + 1) * P - first_key(a, qb)], AX.X, ALU.max, negate=True)
                        if KIND[a] != SWA:
                            top_.then_inc(max_ready, 1)
                            return
                        st.wait(st(top_))
                        h = head_of(a, m)
                        nc.vector.tensor_tensor(nm, nm, small[:, 48 + h:49 + h], ALU.min).then_inc(max_ready, 1)

                    def normalise(a, qb):
                        u, nk = u_of(a, qb, 0), (qb + 1) * P - first_key(a, qb)
                        l, r = small[:, 32 + 2 * qb:34 + 2 * qb], small[:, 40:42]
                        dve.wait_ge(probs_ready, u + 2)
                        if KIND[a] == SWA:
                            st.wait(st(nc.vector.tensor_tensor(l, l, small[:, 44:46], ALU.add)))
                        st.wait(st(nc.vector.reciprocal(r, l)))
                        if u:
                            dve.wait_ge(t_ready, u)
                        st.wait(st(nc.vector.tensor_scalar(pn[0][:, 0:nk], probs_at(a, qb)[0][:, 0:nk], small[:, 40:41], None, ALU.mult)))
                        nc.vector.tensor_scalar(pn[1][:, 0:nk], probs_at(a, qb)[1][:, 0:nk], small[:, 41:42], None, ALU.mult) \
                          .then_inc(probs_normed, 1)

                    def rotate(name, buf, dst):
                        dve.wait_ge(r_ready, R2[name] + 1)
                        st(nc.vector.tensor_tensor(rope_a[:, :], raw_t[buf][:, :], cos[:, :], ALU.mult))
                        nc.vector.tensor_tensor(rope_b[:, :], R[:, :], sin[:, :], ALU.mult).then_inc(r_out, 1)
                        st.wait()
                        dve.wait_ge(r_out, R2[name] + 1)
                        nc.vector.tensor_tensor(dst[:, :], rope_a[:, :], rope_b[:, :], ALU.add).then_inc(qk_ready, 1)

                    def scaled_split(src, gain, rs, i, ready, count):
                        st.wait(st(nc.vector.scalar_tensor_tensor(out=ytmp[:, :], in0=src[:, :], scalar=gain, in1=rs[:, :],
                                                                  op0=ALU.mult, op1=ALU.mult)))
                        st.wait(st(nc.vector.tensor_copy(act_hi[:, i, :], ytmp[:, :])))
                        nc.vector.tensor_tensor(act_lo[:, i, :], ytmp[:, :], act_hi[:, i, :].bitcast(F32), ALU.subtract) \
                          .then_inc(ready, 1)
                        dve.wait_ge(ready, count)

                    def group_norm(t):
                        if t % 2 == 0:
                            dve.wait_ge(rs_ready, SQUARES[f"e{t + 1}"])
                        scaled_split(ext[t % 2], colp[:, P2_MIX + t:P2_MIX + t + 1], nrm, t, y_ready, t + 1)

                    def gate_logits():
                        t = TILE["gates"]
                        dve.wait_ge(*DONE["gates"])
                        nc.vector.tensor_scalar(sz[0][0:4, :], PT[t % 2][0:4, :], colp[0:4, P2_BF:P2_BF + 1], -1.0,
                                                ALU.add, ALU.mult).then_inc(tile_out[t % 2], 1)

                    def gate_sums():
                        dve.wait_ge(gate_ln, 1)
                        y = sz[0][0:4, :]
                        st.wait(st(nc.vector.scalar_tensor_tensor(out=y, in0=y, scalar=0.0, in1=sz[1][0:4, :],
                                                                  op0=ALU.max, op1=ALU.add)))
                        cum = sz[1][0:4, :]
                        st.wait(st(nc.vector.tensor_tensor_scan(cum, y, y, 0.0, ALU.add, ALU.bypass)))
                        st(nc.vector.tensor_copy(sel_r[:, :], const[:, C_SEL:C_SEL + 4 * P]))
                        st.wait(st(nc.vector.tensor_scalar(cum_r[:, :], const[:, 0:SEQ], 0.0, None, ALU.mult)))
                        st.wait(st(nc.vector.tensor_copy(cum_r[0:4, :], cum)))
                        nc.vector.tensor_tensor(cum_r[32:36, :], cum, cum_r[0:4, :].bitcast(F32), ALU.subtract) \
                          .then_inc(gate_ready, 1)

                    def sb_step(a, j):
                        lo, w = (NB - 1 - j) * P, w_of(a, j)
                        if j == 0:
                            if w:
                                dve.wait_ge(sb_sum, w)
                                dve.wait_ge(sb_cum, w)
                            else:
                                dve.wait_ge(t_ready, u_of(SB0 - 1, NB - 1, 1) + 1)
                            for m in range(2):
                                st(nc.vector.memset(sz[m][:, :], 0.0))
                            st.wait()
                        for m in range(2):
                            dve.wait_ge(sb_ln, w + m + 1)
                            if w + m >= 2:
                                dve.wait_ge(sb_sum, w + m - 1)
                            nc.vector.scalar_tensor_tensor(out=pn[m][:, lo:SEQ], in0=banks(a, j)[m][:, lo:SEQ], scalar=0.0,
                                                           in1=prob[m][:, lo:SEQ], op0=ALU.max, op1=ALU.add).then_inc(sb_sp, 1)
                        for m in range(2):
                            dve.wait_ge(sb_cum, w + m + 1)
                            nc.vector.tensor_tensor(sz[m][:, lo:SEQ], sz[m][:, lo:SEQ], pn[m][:, lo:SEQ], ALU.add) \
                              .then_inc(sb_sum, 1)

                    def add_squares(name, a, b):
                        dve.wait_ge(sq_parts, SQUARES[name] - 1)
                        nc.vector.tensor_tensor(a[:, :], a[:, :], b[:, :], ALU.add).then_inc(sq_ready, 1)

                    dve.wait_ge(rs_ready, SQUARES["ckv"])
                    scaled_split(ckv_t, colp[:, P2_GKV:P2_GKV + 1], z_t, 10, latent_ready, 1)
                    add_squares("cq", *sz)
                    for a in range(N_ATT):
                        for qb in range(NB):
                            if (a, qb) == (0, 3):
                                gate_logits()
                            if LATE.get((a, qb), "")[:1] == "e":
                                add_squares(LATE[a, qb], nrm, sq_tmp)
                            if KIND[a] == SB:
                                sb_step(a, qb)
                            else:
                                row_max(a, qb, 0)
                                row_max(a, qb, 1)
                                normalise(a, qb)
                            if (a, qb) == (0, 0):
                                dve.wait_ge(rs_ready, SQUARES["cq"])
                                for i in range(2):
                                    scaled_split(cq_t[i], colp[:, P2_GQ + i:P2_GQ + i + 1], sz[0], 8 + i, latent_ready, 2 + i)
                            elif (a, qb) == (0, 3):
                                rotate("kr", 0, z_t)
                            elif (a, qb) == (1, 2):
                                rotate("qr", 1, qr_t)
                            if (a, qb) == (1, 1):
                                gate_sums()
                            if a == 3:
                                if qb == 0:
                                    dve.wait_ge(rows_loaded, 16)
                                gained = gain_x(qb, row_in)
                                if qb < NB - 1:
                                    st(gained)
                                else:
                                    st.wait()
                                    gained.then_inc(gain_done, 1)
                            for tile, steps in ((0, 1), (1, 1 if is_sb((a, qb)) else 2)):
                                squared = LATE.get(step_before(a, qb, steps), "")
                                if squared[:1] == "e":
                                    group_norm(int(squared[1]) - 1 + tile)
                    add_squares("e7", nrm, sq_tmp)
                    group_norm(6)
                    group_norm(7)

                    def to_residual(g, n_end, scale, tb, sums):
                        c = g % 2
                        cols = slice(c * SEQ, (c + 1) * SEQ)
                        tok_wait(dve, g, tb, n_end)
                        acc = dict(accum_out=small[:, 2 * tb + c:2 * tb + c + 1]) if sums else {}
                        nc.vector.scalar_tensor_tensor(out=x[:, tb, cols], in0=x[:, tb, cols], scalar=scale,
                                                       in1=TOK[tb][:, :], op0=ALU.mult, op1=ALU.add, **acc).then_inc(tok_out, 1)

                    def centre(g, i, tb):
                        dve.wait_ge(tok_out, NB * g + tb + 1)
                        nc.vector.tensor_scalar(small[:, 52 + tb:53 + tb], small[:, 2 * tb:2 * tb + 1],
                                                small[:, 2 * tb + 1:2 * tb + 2], -1.0 / D, ALU.add, ALU.mult).then_inc(ln_centre, 1)

                    def standardise(i, tb):
                        dve.wait_ge(stat_ready, NB * i + tb + 1)
                        nc.vector.tensor_scalar(x[:, tb, :], x[:, tb, :], small[:, 52 + tb:53 + tb], small[:, 20 + tb:21 + tb],
                                                ALU.add, ALU.mult).then_inc(ln_done, 1)

                    def last_residual(g, n_end, scale, i):
                        for tb in range(NB):
                            to_residual(g, n_end, scale, tb, True)
                            centre(g, i, tb)
                            if tb:
                                standardise(i, tb - 1)
                        standardise(i, NB - 1)

                    dve.wait_ge(gain_done, 1)
                    for tb in range(NB):
                        to_residual(0, B2_WO + 4, ALPHA, tb, True)
                    last_residual(1, B2_WO + 8, ALPHA, 0)
                    xt_lo_sub(dve, st, KD, TOK, colp[:, P2_G1:P2_G1 + KD], colp[:, P2_B1:P2_B1 + KD])
                    for hf in range(2):
                        n0, tiles = B2_PART[hf], FF_PARTS[hf]
                        done = len(B2_TILES) // 2 + FF_FIRST[hf]
                        dve.wait_ge(unit_done, n0)
                        first = st.n + 1
                        with dve.Fori(0, tiles) as j:
                            dve.wait_ge(tile_out[0], j + (done + 1))
                            dve.wait_ge(unit_done, j * 2 + (n0 + 2))
                            nc.vector.tensor_tensor(ytmp[:, :], nrm[:, :], PT[1][:, :], ALU.mult).then_inc(tile_out[1], 1)
                            dve.wait_ge(tile_out[1], j + (done + 1))
                            hi = act_hi[:, bass.ds(j, 1), :].rearrange("p a t -> p (a t)")
                            lo = act_lo[:, bass.ds(j, 1), :].rearrange("p a t -> p (a t)")
                            nc.vector.tensor_copy(hi, ytmp[:, :]).then_inc(dve_step, 1)
                            dve.wait_ge(dve_step, j + first)
                            nc.vector.tensor_tensor(lo, ytmp[:, :], hi.bitcast(F32), ALU.subtract).then_inc(gu_ready, 1)
                            dve.wait_ge(gu_ready, j + (FF_FIRST[hf] + 1))
                        st.n += tiles
                        if hf == 0:
                            dve.wait_ge(rows_loaded, 32)
                            for tb in range(NB):
                                last = gain_x(tb, rowp)
                                if tb < NB - 1:
                                    st(last)
                                else:
                                    st.wait()
                                    last.then_inc(gain_done, 1)
                            dve.wait_ge(gain_done, 2)
                        for c in range(2):
                            g, end = 2 + 2 * hf + c, n0 + 2 * tiles + tiles // 2 * (c + 1)
                            if hf and c:
                                last_residual(g, end, 1.0, 1)
                                continue
                            for tb in range(NB):
                                dve.wait_ge(tok_out, NB * g)
                                to_residual(g, end, 1.0 if hf else ALPHA, tb, hf == 1)
            end_of_stage()

        bias = rowp[:, D:2 * D]
        halves = [(tb, c) for tb in range(NB) for c in range(2)]
        halves = halves[:-2], halves[-2:]
        with nc.Block() as block:
            @block.vector
            def _(dve):
                st = Steps(dve, dve_step)
                for tb, c in halves[0]:
                    cols = slice(c * SEQ, (c + 1) * SEQ)
                    st.wait(st(nc.vector.tensor_tensor(x[:, tb, cols], x[:, tb, cols], rowp[:, cols], ALU.mult)))
                    nc.vector.tensor_tensor(x[:, tb, cols], x[:, tb, cols], bias[:, cols], ALU.add).then_inc(ln_done, 1)

            @block.gpsimd
            def _(pool):
                for i, (tb, c) in enumerate(halves[1]):
                    cols = slice(c * SEQ, (c + 1) * SEQ)
                    nc.gpsimd.tensor_tensor(x[:, tb, cols], x[:, tb, cols], rowp[:, cols], ALU.mult).then_inc(hi_split, 1)
                    pool.wait_ge(hi_split, i + 1)
                    nc.gpsimd.tensor_tensor(x[:, tb, cols], x[:, tb, cols], bias[:, cols], ALU.add).then_inc(split_done, 1)

            def store(eng, half):
                tb, c = half
                cols = slice(c * SEQ, (c + 1) * SEQ)
                eng.dma_start(out[tb * P:(tb + 1) * P, cols], x[:, tb, cols]).then_inc(stored, 16)

            @block.sync
            def _(sp):
                for i, half in enumerate(halves[0]):
                    sp.wait_ge(ln_done, i + 1)
                    store(sp, half)
                sp.wait_ge(stored, 16 * 2 * NB)

            @block.scalar
            def _(act):
                for i, half in enumerate(halves[1]):
                    act.wait_ge(split_done, i + 1)
                    store(act, half)


def _t_unit(np, w):
    k = w.shape[0] // P
    u = np.zeros((P, UNIT), w.dtype)
    u[:, :k * P] = w.reshape(k, P, P).transpose(1, 0, 2).reshape(P, k * P)
    return u


def _tok_units(np, w):
    k = w.shape[0] // P
    out = []
    for j in range(0, k, 2):
        u = np.zeros((P, UNIT), w.dtype)
        for i in range(j, min(j + 2, k)):
            u[:, (i - j) * SEQ:(i - j + 1) * SEQ] = w[i * P:(i + 1) * P]
        out.append(u)
    return out


def _block1_units(np, w_in, w_branch, w_out):
    cols = lambda c, n=P: w_in[:, c:c + n]
    units = _tok_units(np, cols(2560, SEQ))
    for g in range(4):
        units += [_t_unit(np, cols(2048 + P * g)), _t_unit(np, cols(3072 + P * g))]
    head = lambda tile, f: _t_unit(np, cols((0, 3584)[f // 4] + SEQ * "qkvz".index(tile) + P * (f % 4)))
    units += [head("q", 0), head("k", 0), head("v", 0), head("q", 1)]
    for a in range(N_ATT - 1):
        units += [head("k", a + 1), head("v", a + 1), head("z", a)] + [head("q", f) for f in (a + 2,) if f < N_ATT]
    units.append(head("z", N_ATT - 1))
    stream = [part for m in range(KD) for i in range(3)
              for part in (_t_unit(np, cols(5632 + D * i + P * m)), _t_unit(np, w_branch[i][:, P * m:P * m + P])[:, :UNIT // 2])]
    stream = np.concatenate(stream, axis=1)
    units += [stream[:, c:c + UNIT] for c in range(0, stream.shape[1], UNIT)]
    for c in range(2):
        units += _tok_units(np, w_out[:, SEQ * c:SEQ * (c + 1)])
    return np.stack(units)


def _block2_units(np, w_in, w_uq, w_ukv, w_o, w_gate, w_up, w_down):
    cols = lambda c, n=P: w_in[:, c:c + n]
    cat = lambda *a: np.concatenate(a, axis=1)
    q3, kv = w_uq.reshape(2 * P, 4, HD + 32), w_ukv.reshape(P, 4, 2 * HD)
    tiles = {"gates": cat(cols(768, 4), np.zeros((D, P - 4), w_in.dtype)),
             "wk": cols(2212), "wv": cols(2340), "ckv": cols(1028), "cq0": cols(772), "cq1": cols(900),
             "kr": cat(*[cols(1156, 32)] * 4), "uqr": q3[:, [0, 2, 1, 3], HD:].reshape(2 * P, P)}
    for i in range(2):
        pair = slice(2 * i, 2 * i + 2)
        tiles |= {f"wq{i}": cat(cols(1956 + HD * i, HD), cols(1956 + HD * (i + 2), HD)),
                  f"uq{i}": q3[:, pair, :HD].reshape(2 * P, P), f"uk{i}": kv[:, pair, :HD].reshape(P, P),
                  f"uv{i}": kv[:, pair, HD:].reshape(P, P)}
        for j, t in enumerate("qkv"):
            tiles |= {f"f{t}{i}": cols(256 * j + P * i), f"s{t}{i}": cols(1188 + 256 * j + P * i)}
    units = []
    for names in B2_PACKED:
        parts = [_t_unit(np, tiles[name])[:, :B2_KT.get(name, KD) * P] for name in names]
        parts.append(np.zeros((P, UNIT - sum(part.shape[1] for part in parts)), w_in.dtype))
        units.append(np.concatenate(parts, axis=1))
    w_o = _mix_order(np, w_o)
    for c in range(2):
        units += _tok_units(np, w_o[:, SEQ * c:SEQ * (c + 1)])
    for hf in range(2):
        for j in range(FF_FIRST[hf], FF_FIRST[hf] + FF_PARTS[hf]):
            units += [_t_unit(np, w_gate[:, P * j:P * j + P]), _t_unit(np, w_up[:, P * j:P * j + P])]
        rows = w_down[FF_FIRST[hf] * P:(FF_FIRST[hf] + FF_PARTS[hf]) * P]
        for c in range(2):
            units += _tok_units(np, rows[:, SEQ * c:SEQ * (c + 1)])
    return np.stack(units)


def _mix_order(np, a):
    heads = a.reshape(16, HD, *a.shape[1:])
    return heads[[12, 14, 13, 15, 4, 5, 6, 7, 8, 9, 10, 11, 0, 1, 2, 3]].reshape(a.shape)


def _constants(np):
    f = np.float32
    c = np.zeros((P, C_KEEP), f)
    r = np.arange(P)
    c[:, C_IDENT:C_IDENT + P] = np.eye(P)
    c[:, C_ONES:C_ONES + P] = 1
    c[:, C_NTRI:C_NTRI + P] = -(r[:, None] >= r[None, :]).astype(f)
    c[:, C_NONES:C_NONES + P] = -1
    for at, width, half in ((C_ROPE1, HD, HD // 8), (C_ROPE2, 32, 16)):
        for p in range(P):
            d = p % width
            if d < half:
                c[p + half, at + p] = -1
            elif d < 2 * half:
                c[p - half, at + p] = 1
    c[:, C_UPPER:C_UPPER + P] = r[:, None] <= r[None, :]
    for h in range(4):
        c[[h, 32 + h], C_SEL + P * h:C_SEL + P * (h + 1)] = 1
    inv = np.power(f(500000.0), -np.arange(8, dtype=f) * f(2.0) / f(16)).astype(f)
    for p in range(P):
        if p % HD < 16:
            c[p, C_INV] = inv[p % 8]
    m = np.zeros((P, M_WIDTH), f)
    m[:, M_CAUSAL:M_CAUSAL + P] = np.where(r[None, :] <= r[:, None], 0, NEG)
    m[:, M_STRICT:M_STRICT + P] = np.where(r[:, None] < r[None, :], 0, NEG)
    rel = r[:, None] - (np.arange(SEQ)[None, :] - (SEQ - P))
    count = (rel <= 128).astype(int) + (rel % 4 == 0) + (rel % 16 == 0)
    m[:, M_MULT:M_MULT + SEQ] = np.where((rel >= 0) & (count > 0), np.log(np.maximum(count, 1)), NEG)
    swa = np.zeros((P, 8 * P), f)
    dist = r[:, None] + P - np.arange(2 * P)[None, :]
    for h in range(4):
        slope = 2.0 ** (-8.0 * (h + 1) / 4)
        swa[:, 2 * P * h:2 * P * (h + 1)] = np.where((dist >= 0) & (dist < 128), -slope * dist, NEG)
    inv2 = f(10000.0) ** (-np.arange(0, 32, 2, dtype=f) / f(32))
    ang = np.arange(SEQ, dtype=f)[None, :] * inv2[r % 16][:, None]
    rope2 = np.stack([np.cos(ang), np.sin(ang)]).astype(f)
    return c, m, swa, rope2


def kernel(**inputs):
    import numpy as np
    import concourse.bacc as bacc
    from concourse.bass_utils import run_bass_kernel_spmd

    a = {k: np.asarray(v) for k, v in inputs.items()}
    f = a["x"].dtype
    c, m, swa, rope2 = _constants(np)
    w1 = np.concatenate([_block1_units(np, a["w_in"][l], a["w_branch"][l], a["w_out"][l]) for l in range(DEPTH)])
    w2 = np.concatenate([_block2_units(np, a["w_in_2"][l], a["mla_w_uq_2"][l], a["mla_w_ukv_2"][l], a["w_o_2"][l],
                                 a["w_gate_2"][l], a["w_up_2"][l], a["w_down_2"][l]) for l in range(DEPTH)])
    rows = lambda v: np.broadcast_to(v.reshape(1, -1), (P, v.size))
    col1, row1, col2, row2 = [], [], [], []
    padded = lambda v: np.concatenate([v, np.zeros((P, COLS - v.shape[1]), f)], axis=1)
    for l in range(DEPTH):
        lam_init = 0.8 - 0.6 * math.exp(-0.3 * l)
        col1.append(np.concatenate([
            a["norm_g"][l].reshape(KD, P).T, a["subln_g"][l].reshape(P, 1),
            rows(a["lam_q1"][l]), rows(a["lam_k1"][l]), rows(a["lam_q2"][l]), rows(a["lam_k2"][l]),
            np.full((P, 1), lam_init, f), np.full((P, 1), 1.0 - lam_init, f)], axis=1))
        row1.append(np.concatenate([
            rows(a["sgu_ln_g"][l]), rows(a["sgu_ln_b"][l]), rows(a["sgu_b"][l]),
            a["sgu_w"][l].transpose(2, 0, 1).reshape(P, SEQ)], axis=1))
        fox_b = np.zeros((P, 1), f)
        fox_b[:4, 0] = a["fox_b_f_2"][l]
        mix_g = _mix_order(np, a["mix_g_2"][l])
        start = (a["final_g"], np.zeros(D, f)) if l == 0 else (a["ln2_g_2"][l - 1], a["ln2_b_2"][l - 1])
        pairs = (start, (a["ln1_g_2"][l], a["ln1_b_2"][l]), (a["ln2_g_2"][l], a["ln2_b_2"][l]))
        col2.append(np.concatenate([
            a["mla_g_q_2"][l].reshape(2, P).T, a["mla_g_kv_2"][l].reshape(P, 1), mix_g.reshape(KD, P).T,
            fox_b, rows(a["swa_sinks_2"][l]), *[v.reshape(KD, P).T for pair in pairs[:2] for v in pair]], axis=1))
        row2.append(np.stack([np.concatenate([rows(v) for v in pair], axis=1) for pair in pairs]))
    arrays = {
        "x_dram": a["x"].reshape(SEQ, D), "pos_dram": a["positions"].reshape(1, SEQ), "const_dram": c, "mask_dram": m, "swa_dram": swa,
        "rope2_dram": rope2, 
        "col_dram": np.stack([padded(v) for v in (*col1, *col2, col2[-1])]), 
        "w_dram": np.concatenate([w1, w2, np.zeros((AHEAD, P, UNIT), f)]), "row1_dram": np.stack(row1),
        "row2_dram": np.stack(row2),
    }
    arrays = {k: np.ascontiguousarray(v) for k, v in arrays.items()}
    nc = bacc.Bacc("TRN2", target_bir_lowering=False, num_devices=1)
    aps = [nc.dram_tensor(k, v.shape, mybir.dt.from_np(v.dtype), kind="ExternalInput").ap() for k, v in arrays.items()]
    out = nc.dram_tensor("out_dram", (SEQ, D), F32, kind="ExternalOutput").ap()
    program(nc, *aps, out)
    r = run_bass_kernel_spmd(nc, [arrays], core_ids=[0])
    return r.results[0]["out_dram"].reshape(1, SEQ, D)
```
